# Optimizing a Trainium2 kernel written in Bass

```python
import math
import jax, jax.numpy as jnp
from jax import lax
import numpy as np

D_MODEL = 1024
BATCH = 1
SEQ = 512
DEPTH = 2

GRID_W = 64
CTX_LEN = 256
D_MIX = D_MODEL
GROUP_W = D_MIX // 4
HEAD_DIM = 64
NA_HEADS = GROUP_W // HEAD_DIM
NA_WIN_ROWS = 8
NA_WIN_COLS = 16
CONV_CH = GROUP_W
CONV_K = 31
GQA_Q_HEADS = GROUP_W // HEAD_DIM
GQA_KV_HEADS = GQA_Q_HEADS // 2
DIFF_HEADS = 4
DIFF_QK_DIM = GROUP_W // (2 * DIFF_HEADS)
DIFF_V_DIM = 2 * DIFF_QK_DIM
N_EXPERTS = 16
D_EXPERT = D_MODEL
EC_CAPACITY_FACTOR = 2

Q_BLOCK = 128
ROPE_BASE = 10000.0
EPS = 1e-6

IN_SPLITS = (
    NA_HEADS * HEAD_DIM, NA_HEADS * HEAD_DIM, NA_HEADS * HEAD_DIM,
    2 * CONV_CH,
    GQA_Q_HEADS * HEAD_DIM, GQA_KV_HEADS * HEAD_DIM, GQA_KV_HEADS * HEAD_DIM,
    2 * DIFF_HEADS * DIFF_QK_DIM, 2 * DIFF_HEADS * DIFF_QK_DIM, DIFF_HEADS * DIFF_V_DIM,
)
D_IN = sum(IN_SPLITS)
IN_OFFSETS = tuple(int(v) for v in np.cumsum(IN_SPLITS)[:-1])

kernel_name = "hybrid_parallel_group_diffusion_block"

def rms_norm(x, g):
    xf = x.astype(jnp.float32)
    y = xf * lax.rsqrt(jnp.mean(xf * xf, axis=-1, keepdims=True) + EPS)
    return (y * g.astype(jnp.float32)).astype(x.dtype)

def layer_norm(x, g, b):
    xf = x.astype(jnp.float32)
    mu = jnp.mean(xf, axis=-1, keepdims=True)
    xc = xf - mu
    y = xc * lax.rsqrt(jnp.mean(xc * xc, axis=-1, keepdims=True) + EPS)
    return (y * g.astype(jnp.float32) + b.astype(jnp.float32)).astype(x.dtype)

def softmax_f32(s):
    return jax.nn.softmax(s.astype(jnp.float32), axis=-1)

def axial_rope(x, rows, cols):
    d = x.shape[-1]
    half = d // 2
    nf = half // 2
    inv = 1.0 / (ROPE_BASE ** (jnp.arange(nf, dtype=jnp.float32) / nf))
    ang = jnp.concatenate([rows[:, None] * inv, cols[:, None] * inv], axis=-1)
    cos = jnp.cos(ang)[None, :, None, :]
    sin = jnp.sin(ang)[None, :, None, :]
    xf = x.astype(jnp.float32)
    x1, x2 = xf[..., :half], xf[..., half:]
    return jnp.concatenate([x1 * cos - x2 * sin, x2 * cos + x1 * sin], axis=-1).astype(x.dtype)

def block_sweep(fn, *qs):
    B, S = qs[0].shape[:2]
    nb = S // Q_BLOCK
    blocks = tuple(jnp.swapaxes(q.reshape(B, nb, Q_BLOCK, *q.shape[2:]), 0, 1) for q in qs)
    out = lax.map(lambda bs: fn(*bs), blocks)
    return jnp.swapaxes(out, 0, 1).reshape(B, S, *out.shape[3:])

def mha(q, k, v, scale):
    s = jnp.einsum('bqhd,bkhd->bhqk', q, k) * scale
    p = softmax_f32(s).astype(v.dtype)
    return jnp.einsum('bhqk,bkhd->bqhd', p, v)

def neighborhood_attention(q, k, v, qc, kc, vc, rpb, need_ctx):
    B, S, H, d = q.shape
    R = S // GRID_W
    KH = min(NA_WIN_ROWS, R)
    scale = d ** -0.5
    r = jnp.arange(R)
    row_idx = jnp.clip(r - KH // 2, 0, R - KH)[:, None] + jnp.arange(KH)[None, :]
    j = jnp.arange(GRID_W)
    col_start = jnp.clip(j - NA_WIN_COLS // 2, 0, GRID_W - NA_WIN_COLS)
    col_valid = (j[None, :] >= col_start[:, None]) & (j[None, :] < col_start[:, None] + NA_WIN_COLS)
    dr = row_idx - r[:, None] + NA_WIN_ROWS - 1
    dc = jnp.clip(j[None, :] - j[:, None], -(NA_WIN_COLS - 1), NA_WIN_COLS - 1) + NA_WIN_COLS - 1
    bias = rpb[:, dr[:, None, :, None], dc[None, :, None, :]].astype(jnp.float32)
    bias = jnp.where(col_valid[None, None, :, None, :], bias, -jnp.inf)
    qg = q.reshape(B, R, GRID_W, H, d)
    kg = k.reshape(B, R, GRID_W, H, d)[:, row_idx]
    vg = v.reshape(B, R, GRID_W, H, d)[:, row_idx]
    s_win = jnp.einsum('brqhd,brkwhd->bhrqkw', qg, kg).astype(jnp.float32) * scale + bias[None]
    s_ctx = jnp.einsum('brqhd,bchd->bhrqc', qg, kc).astype(jnp.float32) * scale
    nwin = KH * GRID_W
    s = jnp.concatenate([s_win.reshape(B, H, R, GRID_W, nwin), s_ctx], axis=-1)
    p = softmax_f32(s).astype(v.dtype)
    p_win = p[..., :nwin].reshape(B, H, R, GRID_W, KH, GRID_W)
    p_ctx = p[..., nwin:]
    o = jnp.einsum('bhrqkw,brkwhd->brqhd', p_win, vg) + jnp.einsum('bhrqc,bchd->brqhd', p_ctx, vc)
    o_lat = o.reshape(B, S, H * d)
    o_ctx = mha(qc, kc, vc, scale).reshape(B, qc.shape[1], H * d) if need_ctx else None
    return o_lat, o_ctx

def conformer_conv(u, dw_w, dw_b, ln_g, ln_b, pw_w, pw_b):
    a, g = jnp.split(u, 2, axis=-1)
    z = a * jax.nn.sigmoid(g)
    z = lax.conv_general_dilated(
        z, dw_w[:, None, :], window_strides=(1,), padding=((CONV_K // 2, CONV_K // 2),),
        dimension_numbers=('NWC', 'WIO', 'NWC'), feature_group_count=CONV_CH) + dw_b
    z = jax.nn.silu(layer_norm(z, ln_g, ln_b))
    return z @ pw_w + pw_b

def gqa_attention(q, k, v, qc, kc, vc, qn_g, kn_g, rows, cols, need_ctx):
    B, S, Hq, d = q.shape
    G = Hq // GQA_KV_HEADS
    scale = d ** -0.5
    q = axial_rope(rms_norm(q, qn_g), rows, cols)
    k = axial_rope(rms_norm(k, kn_g), rows, cols)
    qc = rms_norm(qc, qn_g)
    kc = rms_norm(kc, kn_g)
    k_all = jnp.concatenate([kc, k], axis=1)
    v_all = jnp.concatenate([vc, v], axis=1)

    def attend(qb, kk, vv):
        Bq, Lq = qb.shape[:2]
        qb = qb.reshape(Bq, Lq, GQA_KV_HEADS, G, d)
        s = jnp.einsum('bqkgd,bskd->bkgqs', qb, kk) * scale
        p = softmax_f32(s).astype(vv.dtype)
        return jnp.einsum('bkgqs,bskd->bqkgd', p, vv).reshape(Bq, Lq, Hq * d)

    o_lat = block_sweep(lambda qb: attend(qb, k_all, v_all), q)
    o_ctx = attend(qc, kc, vc) if need_ctx else None
    return o_lat, o_ctx

def diff_attention(q1, q2, k1, k2, v, q1c, q2c, k1c, k2c, vc, lam, lam_init, dn_g, rows, cols, need_ctx):
    B, S, H, dq = q1.shape
    scale = dq ** -0.5
    q1, q2 = axial_rope(q1, rows, cols), axial_rope(q2, rows, cols)
    k1a = jnp.concatenate([k1c, axial_rope(k1, rows, cols)], axis=1)
    k2a = jnp.concatenate([k2c, axial_rope(k2, rows, cols)], axis=1)
    va = jnp.concatenate([vc, v], axis=1)

    def attend(q1b, q2b, kk1, kk2, vv):
        Bq, Lq = q1b.shape[:2]
        p1 = softmax_f32(jnp.einsum('bqhd,bshd->bhqs', q1b, kk1) * scale)
        p2 = softmax_f32(jnp.einsum('bqhd,bshd->bhqs', q2b, kk2) * scale)
        p = (p1 - lam * p2).astype(vv.dtype)
        o = jnp.einsum('bhqs,bshd->bqhd', p, vv)
        o = rms_norm(o, dn_g) * (1.0 - lam_init)
        return o.reshape(Bq, Lq, H * vv.shape[-1])

    o_lat = block_sweep(lambda a, b: attend(a, b, k1a, k2a, va), q1, q2)
    o_ctx = attend(q1c, q2c, k1c, k2c, vc) if need_ctx else None
    return o_lat, o_ctx

def token_mixers(u, uc, w_in, rpb, dw_w, dw_b, ln_g, ln_b, pw_w, pw_b, qn_g, kn_g,
                 lq1, lk1, lq2, lk2, dn_g, lam_init, rows, cols, need_ctx):
    B, S, _ = u.shape
    Lc = uc.shape[1]
    p = jnp.split(u @ w_in, IN_OFFSETS, axis=-1)
    pc = jnp.split(uc @ w_in, IN_OFFSETS, axis=-1)
    oa, oca = neighborhood_attention(
        p[0].reshape(B, S, NA_HEADS, HEAD_DIM), p[1].reshape(B, S, NA_HEADS, HEAD_DIM),
        p[2].reshape(B, S, NA_HEADS, HEAD_DIM), pc[0].reshape(B, Lc, NA_HEADS, HEAD_DIM),
        pc[1].reshape(B, Lc, NA_HEADS, HEAD_DIM), pc[2].reshape(B, Lc, NA_HEADS, HEAD_DIM), rpb, need_ctx)
    ob = conformer_conv(p[3], dw_w, dw_b, ln_g, ln_b, pw_w, pw_b)
    ocb = conformer_conv(pc[3], dw_w, dw_b, ln_g, ln_b, pw_w, pw_b) if need_ctx else None
    oc_, occ = gqa_attention(
        p[4].reshape(B, S, GQA_Q_HEADS, HEAD_DIM), p[5].reshape(B, S, GQA_KV_HEADS, HEAD_DIM),
        p[6].reshape(B, S, GQA_KV_HEADS, HEAD_DIM), pc[4].reshape(B, Lc, GQA_Q_HEADS, HEAD_DIM),
        pc[5].reshape(B, Lc, GQA_KV_HEADS, HEAD_DIM), pc[6].reshape(B, Lc, GQA_KV_HEADS, HEAD_DIM),
        qn_g, kn_g, rows, cols, need_ctx)
    qd = p[7].reshape(B, S, DIFF_HEADS, 2, DIFF_QK_DIM)
    kd = p[8].reshape(B, S, DIFF_HEADS, 2, DIFF_QK_DIM)
    qdc = pc[7].reshape(B, Lc, DIFF_HEADS, 2, DIFF_QK_DIM)
    kdc = pc[8].reshape(B, Lc, DIFF_HEADS, 2, DIFF_QK_DIM)
    lam = (jnp.exp(jnp.sum(lq1.astype(jnp.float32) * lk1.astype(jnp.float32)))
           - jnp.exp(jnp.sum(lq2.astype(jnp.float32) * lk2.astype(jnp.float32))) + lam_init)
    od, ocd = diff_attention(
        qd[..., 0, :], qd[..., 1, :], kd[..., 0, :], kd[..., 1, :], p[9].reshape(B, S, DIFF_HEADS, DIFF_V_DIM),
        qdc[..., 0, :], qdc[..., 1, :], kdc[..., 0, :], kdc[..., 1, :], pc[9].reshape(B, Lc, DIFF_HEADS, DIFF_V_DIM),
        lam, lam_init, dn_g, rows, cols, need_ctx)
    y = jnp.concatenate([oa, ob, oc_, od], axis=-1)
    yc = jnp.concatenate([oca, ocb, occ, ocd], axis=-1) if need_ctx else None
    return y, yc

def expert_choice_ffn(h, w_router, w_gate, w_up, w_down):
    B, N, D = h.shape
    cap = EC_CAPACITY_FACTOR * N // N_EXPERTS
    aff = softmax_f32(jnp.einsum('bnd,de->bne', h, w_router))
    g, idx = lax.top_k(jnp.swapaxes(aff, 1, 2), cap)
    bi = jnp.arange(B)[:, None, None]
    xe = h[bi, idx]
    a = jnp.einsum('becd,edf->becf', xe, w_gate)
    up = jnp.einsum('becd,edf->becf', xe, w_up)
    y = jnp.einsum('becf,efd->becd', jax.nn.silu(a) * up, w_down)
    y = y * g[..., None].astype(y.dtype)
    return jnp.zeros_like(h).at[bi, idx].add(y)

def setup_inputs(seed: int = 0) -> dict:
    key = jax.random.key(seed)
    ks = jax.random.split(key, 32)
    f32 = jnp.float32
    L = DEPTH

    def nrm(k, shape, scale):
        return jax.random.normal(k, shape, f32) * scale

    return {
        "x": nrm(ks[0], (BATCH, SEQ, D_MODEL), 1.0),
        "c": nrm(ks[1], (BATCH, D_MODEL), 1.0),
        "ctx": nrm(ks[2], (BATCH, CTX_LEN, D_MODEL), 1.0),
        "c_ctx": nrm(ks[3], (D_MODEL,), 1.0),
        "norm1_g": 1.0 + nrm(ks[4], (L, D_MODEL), 0.05),
        "w_mod": nrm(ks[5], (L, D_MODEL, 6 * D_MODEL), 0.5 * D_MODEL ** -0.5),
        "b_mod": nrm(ks[6], (L, 6 * D_MODEL), 0.02),
        "w_in": nrm(ks[7], (L, D_MODEL, D_IN), D_MODEL ** -0.5),
        "na_rpb": nrm(ks[8], (L, NA_HEADS, 2 * NA_WIN_ROWS - 1, 2 * NA_WIN_COLS - 1), 0.1),
        "conv_dw_w": nrm(ks[9], (L, CONV_K, CONV_CH), CONV_K ** -0.5),
        "conv_dw_b": nrm(ks[10], (L, CONV_CH), 0.02),
        "conv_ln_g": 1.0 + nrm(ks[11], (L, CONV_CH), 0.05),
        "conv_ln_b": nrm(ks[12], (L, CONV_CH), 0.02),
        "conv_pw_w": nrm(ks[13], (L, CONV_CH, CONV_CH), CONV_CH ** -0.5),
        "conv_pw_b": nrm(ks[14], (L, CONV_CH), 0.02),
        "gqa_qn_g": 1.0 + nrm(ks[15], (L, HEAD_DIM), 0.05),
        "gqa_kn_g": 1.0 + nrm(ks[16], (L, HEAD_DIM), 0.05),
        "diff_lq1": nrm(ks[17], (L, DIFF_QK_DIM), 0.1),
        "diff_lk1": nrm(ks[18], (L, DIFF_QK_DIM), 0.1),
        "diff_lq2": nrm(ks[19], (L, DIFF_QK_DIM), 0.1),
        "diff_lk2": nrm(ks[20], (L, DIFF_QK_DIM), 0.1),
        "diff_norm_g": 1.0 + nrm(ks[21], (L, DIFF_V_DIM), 0.05),
        "w_out": nrm(ks[22], (L, D_MIX, D_MODEL), D_MIX ** -0.5),
        "norm2_g": 1.0 + nrm(ks[23], (L, D_MODEL), 0.05),
        "w_router": nrm(ks[24], (L, D_MODEL, N_EXPERTS), D_MODEL ** -0.5),
        "w_gate": nrm(ks[25], (L, N_EXPERTS, D_MODEL, D_EXPERT), D_MODEL ** -0.5),
        "w_up": nrm(ks[26], (L, N_EXPERTS, D_MODEL, D_EXPERT), D_MODEL ** -0.5),
        "w_down": nrm(ks[27], (L, N_EXPERTS, D_EXPERT, D_MODEL), D_EXPERT ** -0.5),
        "final_g": 1.0 + nrm(ks[28], (D_MODEL,), 0.05),
    }

def reference(x, c, ctx, c_ctx, norm1_g, w_mod, b_mod, w_in, na_rpb, conv_dw_w, conv_dw_b, conv_ln_g,
              conv_ln_b, conv_pw_w, conv_pw_b, gqa_qn_g, gqa_kn_g, diff_lq1, diff_lk1, diff_lq2, diff_lk2,
              diff_norm_g, w_out, norm2_g, w_router, w_gate, w_up, w_down, final_g):
    B, S, D = x.shape
    t = jnp.arange(S)
    rows = (t // GRID_W).astype(jnp.float32)
    cols = (t % GRID_W).astype(jnp.float32)
    cond = jax.nn.silu(c)
    cond_ctx = jax.nn.silu(c_ctx)
    h, hc = x, ctx
    for l in range(DEPTH):
        need_ctx = l < DEPTH - 1
        lam_init = 0.8 - 0.6 * math.exp(-0.3 * l)
        sh1, sc1, g1, sh2, sc2, g2 = jnp.split((cond @ w_mod[l] + b_mod[l])[:, None, :], 6, axis=-1)
        sh1c, sc1c, g1c, sh2c, sc2c, g2c = jnp.split(cond_ctx @ w_mod[l] + b_mod[l], 6, axis=-1)
        u = rms_norm(h, norm1_g[l]) * (1.0 + sc1) + sh1
        uc = rms_norm(hc, norm1_g[l]) * (1.0 + sc1c) + sh1c
        y, yc = token_mixers(u, uc, w_in[l], na_rpb[l], conv_dw_w[l], conv_dw_b[l], conv_ln_g[l], conv_ln_b[l],
                             conv_pw_w[l], conv_pw_b[l], gqa_qn_g[l], gqa_kn_g[l], diff_lq1[l], diff_lk1[l],
                             diff_lq2[l], diff_lk2[l], diff_norm_g[l], lam_init, rows, cols, need_ctx)
        h = h + g1 * (y @ w_out[l])
        u = rms_norm(h, norm2_g[l]) * (1.0 + sc2) + sh2
        h = h + g2 * expert_choice_ffn(u, w_router[l], w_gate[l], w_up[l], w_down[l])
        if need_ctx:
            hc = hc + g1c * (yc @ w_out[l])
            uc = rms_norm(hc, norm2_g[l]) * (1.0 + sc2c) + sh2c
            hc = hc + g2c * expert_choice_ffn(uc, w_router[l], w_gate[l], w_up[l], w_down[l])
    return rms_norm(h, final_g)


_drawn_inputs = setup_inputs


def setup_inputs(seed=0):
    import zlib

    import numpy as np

    out = dict(_drawn_inputs(seed))
    spreads = {}
    factors = {'norm1_g': 4.994,
     'na_rpb': 8.0,
     'conv_dw_b': 8.0,
     'conv_ln_g': 6.348,
     'conv_ln_b': 8.0,
     'conv_pw_b': 8.0,
     'gqa_qn_g': 8.0,
     'gqa_kn_g': 8.0,
     'diff_lq1': 8.0,
     'diff_lk1': 6.818,
     'diff_lq2': 8.0,
     'diff_lk2': 8.0,
     'diff_norm_g': 6.217,
     'norm2_g': 3.781}
    for name, (base, spread) in spreads.items():
        noise = np.random.default_rng([zlib.crc32(name.encode()), seed]).standard_normal(out[name].shape)
        drawn = base * np.exp(spread * noise) if base else spread * noise
        out[name] = __import__('jax').numpy.asarray(drawn.astype(out[name].dtype))
    for name, factor in factors.items():
        out[name] = (out[name] * factor).astype(out[name].dtype)
    return out
```

```python
from contextlib import ExitStack
import math

import numpy as np

import concourse.bass as bass
from concourse import mybir

F32 = mybir.dt.float32
ALU = mybir.AluOpType
ACT = mybir.ActivationFunctionType
AX = mybir.AxisListType

P = 128
D = 1024
KD = D // P
LAT, CTX = 512, 256
TOK = LAT + CTX
TL, TC = LAT // P, CTX // P
LAYERS = 2
GRID_W, ROWS = 64, LAT // 64
WIN_R, WIN_C = 8, 16
TAPS = 31
HALO = TAPS // 2
HD = 64
DQ = 32
E = 16
CAP_L, CAP_C = 2 * LAT // E, 2 * CTX // E
EPS = 1e-6
RING = 4
BLK = 512
MOD_BLOCKS = 6 * D // BLK
IN_BLOCKS = 5
OUT_BLOCKS = D // BLK
PAIRS = E // 2
LAM_INIT = [0.8 - 0.6 * math.exp(-0.3 * l) for l in range(LAYERS)]
NEG = -1.0e30

SMALL = {}
_at = 0
for _name, _n in (("b_mod", 96), ("norm1", 16), ("norm2", 16), ("taps", 2 * TAPS), ("dw_b", 2), ("ln_g", 2),
                  ("ln_b", 2), ("pw_b", 2), ("qn", 1), ("kn", 1), ("dn", 1), ("lam", 4 * DQ),
                  ("router", KD * E), ("final", KD)):
    SMALL[_name] = (_at, _at + _n)
    _at += _n
SMALL_N = _at

CONST = {}
_at = 0
for _name, _n in (("ident", P), ("ones_d", P), ("ones_c", P), ("ones_h", P), ("swap32", P), ("swap16", P),
                  ("mask", GRID_W), ("iota", 64), ("j_lat", 1), ("j_ctx", 1), ("eps", 1)):
    CONST[_name] = (_at, _at + _n)
    _at += _n
CONST_N = _at

QK_AT = 0
V_AT = QK_AT + 11 * TOK
WORK_AT = V_AT + 6 * 640
ZW = TOK + 4 * HALO
ACCW = ZW - 2 * HALO
ACC_AT = WORK_AT
TH_AT = ACC_AT + 2 * ACCW
Z_AT = TH_AT + 2 * TOK
TAB_AT = Z_AT + 2 * ZW
TA_AT = TAB_AT + 4 * LAT
TB_AT = TA_AT + TOK
PW_AT = TB_AT + TOK
BIAS_DR = 14
BT_AT = WORK_AT
EX_AT = BT_AT + 4 * BIAS_DR * GRID_W
PT_AT = EX_AT + 3 * TOK
QST_AT = PT_AT + TOK
OT_AT = QST_AT + 16 * P
UTOK_AT = 0
XE_AT = UTOK_AT + 6 * D
HE0_AT = XE_AT + 2 * KD * 192
HE1_AT = HE0_AT + KD * P
TH2_AT = HE1_AT + KD * P
YL_AT = 13056
YC_AT = YL_AT + D
SL_AT = YC_AT + D
SC_AT = SL_AT + LAT
GL_AT = SC_AT + CTX
GC_AT = GL_AT + TL * P
PBL_AT = GC_AT + TC * 64
PBC_AT = PBL_AT + 2 * LAT
PTOK_AT = PBC_AT + 2 * CTX
LG_AT = PTOK_AT + 6 * (E + 2)
AFFT_AT = LG_AT + 6 * E
WRK_AT = AFFT_AT + TOK
CUM_AT = WRK_AT + TOK
POS_AT = CUM_AT + TOK
ARENA = max(OT_AT + 6 * P, PW_AT + 2 * 256, POS_AT + TOK)
assert TH2_AT + 4 * P <= YL_AT


def program(nc, a, out):
    ctx = ExitStack()
    with ctx:
        def sb(name, shape):
            return ctx.enter_context(nc.sbuf_tensor(name, shape, F32))

        ring = sb("ring", [P, RING, KD, BLK])
        h = sb("h", [P, KD, TOK])
        u = sb("u", [P, KD, TOK])
        arena = sb("arena", [P, ARENA])
        small = sb("small", [P, LAYERS, SMALL_N])
        const = sb("const", [P, CONST_N])
        cond = sb("cond", [P, KD, 2])
        cond_t = sb("cond_t", [P, KD, 2])
        mod = sb("mod", [P, LAYERS, 48, 2])
        gain = sb("gain", [P, 2, KD, 2])
        lam = sb("lam", [P, 4])
        qn_s = sb("qn_s", [P, 2])
        negmax = sb("negmax", [P, 16])
        sums = sb("sums", [P, 16])
        rsum = sb("rsum", [P, 16])
        top8 = sb("top8", [E, 8])
        mx6 = sb("mx6", [P, 12])
        ps = ctx.enter_context(nc.psum_tensor("ps", [P, 8, 512], F32))
        route = nc.dram_tensor("route", [E, 2, TOK], F32, kind="Internal").ap()

        def view(at, *shape, parts=P):
            n = int(np.prod(shape))
            v = arena[0:parts, at:at + n]
            if len(shape) == 2:
                v = v.rearrange("p (a b) -> p a b", b=shape[1])
            if len(shape) == 3:
                v = v.rearrange("p (a b c) -> p a b c", b=shape[1], c=shape[2])
            return v

        def sm(l, name):
            lo, hi = SMALL[name]
            return small[:, l, lo:hi]

        def cst(name, parts=P):
            lo, hi = CONST[name]
            return const[0:parts, lo:hi]

        psf = ps[:, :, :].rearrange("p b n -> p (b n)")

        def bank2(b, n=TOK):
            return psf[:, 512 * b:512 * b + n]

        qk = view(QK_AT, 11, TOK)
        val = view(V_AT, 6, 640)
        acc, th, z = view(ACC_AT, 2, ACCW), view(TH_AT, 2, TOK), view(Z_AT, 2, ZW)
        a_raw = arena[:, ACC_AT:ACC_AT + 2 * TOK].rearrange("p (a b) -> p a b", b=TOK)
        tab = view(TAB_AT, 4, LAT)
        tmp = [view(TA_AT, TOK), view(TB_AT, TOK), view(TH_AT, TOK)]
        bt = view(BT_AT, 4, BIAS_DR * GRID_W)
        ex = view(EX_AT, 3, TOK)
        pt = view(PT_AT, TOK)
        qst = view(QST_AT, 16, P)
        pw = view(PW_AT, 2, 256)
        otok = view(OT_AT, TOK)
        utok = view(UTOK_AT, 6, D)
        gl, gc = view(GL_AT, TL, P), view(GC_AT, TC, 64)
        s_lat, s_ctx = view(SL_AT, LAT), view(SC_AT, CTX)
        yl, yc = view(YL_AT, D), view(YC_AT, D)
        pbl, pbc = view(PBL_AT, 2, LAT), view(PBC_AT, 2, CTX)
        ptok = view(PTOK_AT, 6, E + 2)
        lg = view(LG_AT, 6, E)
        afft, wrk = view(AFFT_AT, TOK, parts=E), view(WRK_AT, TOK, parts=E)
        cum, pos = view(CUM_AT, TOK, parts=E), view(POS_AT, TOK, parts=E)
        he = [view(HE0_AT, KD, P), view(HE1_AT, KD, P)]
        th2 = view(TH2_AT, 4 * P)

        filled = [ctx.enter_context(nc.semaphore(f"filled{s}")) for s in range(RING)]
        used = [ctx.enter_context(nc.semaphore(f"used{s}")) for s in range(RING)]
        names = ("loaded x_loaded stored cond_tanh cond_done mod_mm mod_ev self0 gain_done lam_dot lam_exp fin_mm fin_sq "
                 "fin_root fin_rinv fin_out").split()
        sig = {n: ctx.enter_context(nc.semaphore(n)) for n in names}
        SINCE = {}
        for names_, n_ in (("n1_sq n1_mm n1_pre n1_u n2_sq n2_mm n2_pre n2_u o_mm o_ev", 8), ("t_mm t_ev", 15),
                           ("v_mm v_ev", 18), ("z_done c_sq c_lin c_tanh c_pw c_out dn_sq dn_mm dn_root dn_done", 2),
                           ("n1_root n2_root z_zero c_mean c_cent c_var c_root c_act bias_done r_mm r_cp r_exp r_aff r_tr "
                            "r_afft r_pos r_ptr q_zero", 1), ("tables layer_in", 16), ("hn_sq hn_mm hn_root hn_done", 3),
                           ("rp_mm rp_done", 7), ("bias_ld", 16), ("r_store", 32), ("ut_mm ut_ev", 12)):
            for n in names_.split():
                SINCE[n] = n_
                sig[n, 0] = sig[n, 1] = ctx.enter_context(nc.semaphore(n))

        def since(n, l):
            return l * SINCE[n]

        per_layer = "tap e_clear e_bc e_s e_g e_xmm e_xev e_gu e_tanh e_h e_dn e_y e_sc e_acc self".split()
        ATTN = {"q_st": (10, 10), "s_mm": (16, 16), "s_max": (16, 16), "s_exp": (16, 16), "p_diff": (4, 4), "t_mm": (24, 12),
                "t_dve": (12, 12), "t_act": (12, 0), "o_mm": (12, 12), "o_ev": (12, 12), "y_mm": (2, 2), "y_ev": (3, 3),
                "self": (24, 20)}
        at_sem = {n: ctx.enter_context(nc.semaphore("at_" + n)) for n in ATTN}

        def attn_since(l, kind):
            done = (0, 0) if (l, kind) == (0, "lat") else (TL, 0) if kind == "ctx" else (TL, TC)
            return {n: done[0] * x + done[1] * y for n, (x, y) in ATTN.items()}

        for l in range(LAYERS):
            for n in per_layer:
                sig[n, l] = ctx.enter_context(nc.semaphore(f"{n}_{l}"))
        def parts_of(l, second=False):
            both = [(0, LAT, 0), (LAT, CTX, 1)]
            return both[:1] if (l and second) else both

        at = {"mod0a": 0}
        at["in0"] = at["mod0a"] + 4
        at["mod0b"] = at["in0"] + IN_BLOCKS
        at["out0"] = at["mod0b"] + MOD_BLOCKS - 4
        at["mod1"] = at["out0"] + OUT_BLOCKS
        at["exp0"] = at["mod1"] + MOD_BLOCKS
        at["in1"] = at["exp0"] + 6 * E
        at["out1"] = at["in1"] + IN_BLOCKS
        at["exp1"] = at["out1"] + OUT_BLOCKS

        T_TILES = [("nq", 0, 0, 0), ("nq", 0, 1, 1), ("k", 0, 2, 2), ("k", 0, 3, 3),
                   ("a", 1, 2, 0), ("a", 1, 3, 1), ("g", 2, 0, 0), ("g", 2, 1, 1),
                   ("q", 2, 2, 4), ("q", 2, 3, 5), ("k", 3, 0, 6),
                   ("dq", 3, 2, 7), ("dq", 3, 3, 8), ("k", 4, 0, 9), ("k", 4, 1, 10)]
        V_COLS = [(1, 0, 256, 0), (3, 128, 128, 256), (4, 256, 256, 384)]
        P_ORDER = [[("t", 0), ("t", 1), ("t", 2), ("t", 3)], [("v", 0), ("t", 4), ("t", 5)],
                   [("t", 6), ("t", 7), ("t", 8), ("t", 9)], [("t", 10), ("v", 1), ("t", 11), ("t", 12)],
                   [("t", 13), ("t", 14), ("v", 2)]]

        def t_width(l, kind):
            return TOK if (l == 0 or kind == "k") else LAT

        HN = [(4, "q"), (5, "q"), (6, "k")]
        ROPE = [(4, "swap32", 0), (5, "swap32", 0), (6, "swap32", 0),
                (7, "swap16", 2), (8, "swap16", 2), (9, "swap16", 2), (10, "swap16", 2)]
        T_INDEX = {t[3] + (100 if t[0] in "ag" else 0): i for i, t in enumerate(T_TILES)}

        def kinds(l):
            return ("lat", "ctx") if l == 0 else ("lat",)

        def score_units():
            return [2, 2, 3, 3] + [6] * 4 + [9] * 4 + [10] * 4

        STAGE = [[(64, 64 * r, 64 * r, slice(0, 2), slice(r, 4, 2)) for r in range(2)],
                 [(64, 64 * r, 64 * g, slice(4 + g, 5 + g), slice(4 + 2 * g + r, 5 + 2 * g + r))
                  for g in range(2) for r in range(2)],
                 [(32, 32 * r, 32 * r, slice(7, 9), slice(8 + r, 16, 4)) for r in range(4)]]
        SU = score_units()
        last_score = [i if i < 8 else 9 + 2 * (i - 8) for i in range(12)]
        v_col = [64 * i for i in range(4)] + [256 + 64 * (i // 2) for i in range(4)] + [384 + 64 * i for i in range(4)]

        block = ctx.enter_context(nc.Block())

        @block.sync
        def _(sp):
            sp.dma_start(cond[:], a["cond"]).then_inc(sig["loaded"], 16)
            sp.dma_start(const[:], a["const"]).then_inc(sig["loaded"], 16)
            sp.dma_start(small[:], a["small"]).then_inc(sig["loaded"], 16)

            def fill(n, src):
                s = n % RING
                if n >= RING:
                    sp.wait_ge(used[s], n // RING)
                sp.dma_start(ring[:, s, :, :], src).then_inc(filled[s], 16)

            for l in range(LAYERS):
                if l == 0:
                    for j in range(4):
                        fill(at["mod0a"] + j, a["w_mod"][0, j])
                    sp.dma_start(h[:], a["x"]).then_inc(sig["x_loaded"], 16)
                for j in range(IN_BLOCKS):
                    fill(at[f"in{l}"] + j, a["w_in"][l, j])
                if l == 0:
                    for j in range(MOD_BLOCKS - 4):
                        fill(at["mod0b"] + j, a["w_mod"][0, 4 + j])
                for j in range(OUT_BLOCKS):
                    fill(at[f"out{l}"] + j, a["w_out"][l, j])
                if l == 0:
                    for j in range(MOD_BLOCKS):
                        fill(at["mod1"] + j, a["w_mod"][1, j])
                with sp.Fori(0, PAIRS) as p:
                    for j in range(12):
                        n = at[f"exp{l}"] + j
                        s = n % RING
                        sp.wait_ge(used[s], p * 3 + n // RING)
                        sp.dma_start(ring[:, s, :, :], a["w_exp"][l, p, j]).then_inc(filled[s], 16)
            for k in range(KD):
                sp.wait_ge(sig["fin_out"], k + 1)
                sp.dma_start(out[:, k, :], u[:, k, 0:LAT]).then_inc(sig["stored"], 16)
            sp.wait_ge(sig["stored"], 16 * KD)

        @block.tensor
        def _(pe):
            def ready(n, p3=None):
                s = n % RING
                v = 16 * (n // RING + 1)
                pe.wait_ge(filled[s], v if p3 is None else p3 * 48 + v)
                return ring[:, s, :, :]

            def release(held, p3=0):
                if held:
                    n, sem, count = held
                    pe.wait_ge(sem, count)
                    pe.sem_inc(used[n % RING], 1)

            def modulation(l, j0, j1, n0):
                held = None
                for j in range(j0, j1):
                    w = ready(n0 + j - j0)
                    m = l * MOD_BLOCKS + j
                    if m >= 2:
                        pe.wait_ge(sig["mod_ev"], m - 1)
                    for b in range(4):
                        for k in range(KD):
                            mm = pe.matmul(ps[:, 6 + j % 2, P * b:P * b + P].rearrange("p (r c) -> p r c", c=2),
                                           w[:, k, P * b:P * b + P], cond[:, k, :].unsqueeze(1).to_broadcast([P, P // 2, 2]),
                                           start=k == 0, stop=k == KD - 1)
                        if b == 0:
                            release(held)
                    mm.then_inc(sig["mod_mm"], 1)
                    held = (n0 + j - j0, sig["mod_mm"], m + 1)
                release(held)

            def norm_sum(which, l, parts):
                for k in range(KD):
                    pe.wait_ge(sig[which + "_sq", l], since(which + "_sq", l) + k + 1)
                    for t0, n, c in parts:
                        mm = pe.matmul(ps[:, c, 0:n], cst("ones_d"), ex[:, k % 2, t0:t0 + n],
                                       start=k == 0, stop=k == KD - 1)
                    mm.then_inc(sig[which + "_mm", l], 1)

            pe.wait_ge(sig["cond_done"], 1)
            for l in range(LAYERS):
                if l == 0:
                    modulation(0, 0, 4, at["mod0a"])
                norm_sum("n1", l, parts_of(l))
                nt = nv = 0
                held = None
                for blk in range(IN_BLOCKS):
                    w = ready(at[f"in{l}"] + blk)
                    if blk == 0:
                        pe.wait_ge(sig["n1_u", l], since("n1_u", l) + KD)
                        pe.wait_ge(sig["n1_root", l], since("n1_root", l) + 1)
                    for what, i in P_ORDER[blk]:
                        if what == "t":
                            kind, _, ct, _ = T_TILES[i]
                            if nt >= 2:
                                pe.wait_ge(sig["t_ev", l], since("t_ev", l) + nt - 1)
                            b = 2 * (nt % 2)
                            halves = [(0, LAT, b)] + ([(LAT, CTX, b + 1)] if t_width(l, kind) > LAT else [])
                            for k in range(KD):
                                for t0, n, bb in halves:
                                    mm = pe.matmul(ps[:, bb, 0:n], w[:, k, P * ct:P * ct + P], u[:, k, t0:t0 + n],
                                                   start=k == 0, stop=k == KD - 1)
                            mm.then_inc(sig["t_mm", l], 1)
                            nt += 1
                            release(held)
                            held = None
                        else:
                            _, c0, cn, _ = V_COLS[i]
                            for t in range(TL + TC):
                                if nv >= 2:
                                    pe.wait_ge(sig["v_ev", l], since("v_ev", l) + nv - 1)
                                for k in range(KD):
                                    mm = pe.matmul(ps[:, 4 + nv % 2, 0:cn], u[:, k, P * t:P * t + P],
                                                   w[:, k, c0:c0 + cn], start=k == 0, stop=k == KD - 1)
                                mm.then_inc(sig["v_mm", l], 1)
                                nv += 1
                                release(held)
                                held = None
                    last = ("t_mm", nt) if P_ORDER[blk][-1][0] == "t" else ("v_mm", nv)
                    held = (at[f"in{l}"] + blk, sig[last[0], l], since(last[0], l) + last[1])
                release(held)
                pe.wait_ge(sig["t_ev", l], since("t_ev", l) + len(T_TILES))
                pe.wait_ge(sig["v_ev", l], since("v_ev", l) + nv)
                for i, (tile, g) in enumerate(HN):
                    pe.wait_ge(sig["hn_sq", l], since("hn_sq", l) + i + 1)
                    wd = t_width(l, g)
                    for t0, n, c in parts_of(0)[:1 if wd == LAT else 2]:
                        mm = pe.matmul(ps[:, 2 * i + c, 0:n], cst("ones_h"), tmp[i][:, t0:t0 + n], start=True, stop=True)
                    mm.then_inc(sig["hn_mm", l], 1)
                for i, (tile, perm, _) in enumerate(ROPE):
                    if i < 3:
                        pe.wait_ge(sig["hn_done", l], since("hn_done", l) + i + 1)
                    if i == 0:
                        pe.wait_ge(sig["hn_root", l], since("hn_root", l) + 3)
                    if i >= 2:
                        pe.wait_ge(sig["rp_done", l], since("rp_done", l) + i - 1)
                    pe.matmul(ps[:, 4 + i % 2, :], cst(perm), qk[:, tile, 0:LAT], start=True,
                              stop=True).then_inc(sig["rp_mm", l], 1)
                if l == 0:
                    modulation(0, 4, MOD_BLOCKS, at["mod0b"])
                pe.wait_ge(sig["tap", l], 2 * TAPS)
                pc = parts_of(0)[:2 - l]
                for j in range(2):
                    for t0, n, c in pc:
                        s0 = t0 + (2 * HALO if c else 0)
                        mm = pe.matmul(ps[:, c, 0:n], cst("ones_c"), acc[:, j, s0:s0 + n], start=j == 0, stop=j == 1)
                mm.then_inc(sig["c_mean", l], 1)
                pe.wait_ge(sig["c_sq", l], since("c_sq", l) + 2)
                for j in range(2):
                    for t0, n, c in pc:
                        mm = pe.matmul(ps[:, 2 + c, 0:n], cst("ones_c"), tmp[j][:, t0:t0 + n], start=j == 0, stop=j == 1)
                mm.then_inc(sig["c_var", l], 1)
                pe.wait_ge(sig["c_act", l], since("c_act", l) + 1)
                pe.wait_ge(sig["layer_in", l], since("layer_in", l) + 16)
                for co in range(2):
                    for t0, n, c in pc:
                        s0 = t0 + (2 * HALO if c else 0)
                        for ci in range(2):
                            mm = pe.matmul(ps[:, 4 * co + c, 0:n], pw[:, ci, P * co:P * co + P], acc[:, ci, s0:s0 + n],
                                           start=ci == 0, stop=ci == 1)
                    mm.then_inc(sig["c_pw", l], 1)
                pe.wait_ge(sig["c_out", l], since("c_out", l) + 2)
                for kind in kinds(l):
                    s, s0 = at_sem, attn_since(l, kind)
                    lat = kind == "lat"
                    k0, kn, trips = (0, TOK, TL) if lat else (LAT, CTX, TC)
                    ktiles = range(k0 // P, (k0 + kn) // P)
                    cuts = [(0, LAT, 0), (LAT, CTX, 1)] if lat else [(LAT, CTX, 0)]
                    nb = len(cuts)
                    with pe.Fori(0, trips) as it:
                        def scores(j):
                            if j in (0, 4, 8):
                                pe.wait_ge(s["q_st"], s0["q_st"] + it * 10 + (2, 6, 10)[j // 4])
                            for t0, n, c in cuts:
                                mm = pe.matmul(ps[:, 2 * (j % 2) + c, 0:n], qst[:, j, :], qk[:, SU[j], t0:t0 + n],
                                               start=True, stop=True)
                            mm.then_inc(s["s_mm"], 1)

                        scores(0)
                        scores(1)
                        nxt = 2
                        for i in range(12):
                            if i < 8:
                                pe.wait_ge(s["s_exp"], s0["s_exp"] + it * 16 + i + 1)
                                src = ex[:, i % 3, :]
                            else:
                                pe.wait_ge(s["p_diff"], s0["p_diff"] + it * 4 + i - 7)
                                src = ex[:, last_score[i] % 3, :]
                            if i:
                                pe.wait_ge(s["t_dve"], s0["t_dve"] + it * 12 + i)
                                if lat:
                                    pe.wait_ge(s["t_act"], s0["t_act"] + it * 12 + i)
                            else:
                                pe.wait_ge(s["y_ev"], s0["y_ev"] + it * 3)
                            for x, kt in enumerate(ktiles):
                                mm = pe.transpose(ps[:, 4 + x // 4, P * (x % 4):P * (x % 4) + P],
                                                  src[:, P * x:P * x + P], cst("ident"))
                                if x in (3, len(ktiles) - 1):
                                    mm.then_inc(s["t_mm"], 1)
                            while nxt < 16 and nxt <= last_score[i] + 2:
                                scores(nxt)
                                nxt += 1
                            pe.wait_ge(s["t_dve"], s0["t_dve"] + it * 12 + i + 1)
                            if lat:
                                pe.wait_ge(s["t_act"], s0["t_act"] + it * 12 + i + 1)
                            pe.wait_ge(s["o_ev"], s0["o_ev"] + it * 12 + (i - 1 if i >= 2 else 0))
                            for x, kt in enumerate(ktiles):
                                v0 = v_col[i] - (HD if i % 2 else 0)
                                mm = pe.matmul(ps[:, 6 + i % 2, 0:P], pt[:, P * x:P * x + P], val[:, kt, v0:v0 + P],
                                               start=x == 0, stop=x == len(ktiles) - 1)
                            mm.then_inc(s["o_mm"], 1)
                        pe.wait_ge(s["o_ev"], s0["o_ev"] + it * 12 + 12)
                        for x in range(6):
                            mm = pe.transpose(ps[:, 4 + x // 4, P * (x % 4):P * (x % 4) + P],
                                              otok[:, P * x:P * x + P], cst("ident"))
                            if x in (3, 5):
                                mm.then_inc(s["y_mm"], 1)
                    pe.wait_ge(s["y_ev"], s0["y_ev"] + 3 * trips)
                wp = parts_of(0)[:2 - l]
                for i in range(2):
                    pe.wait_ge(sig["dn_sq", l], since("dn_sq", l) + i + 1)
                    for t0, n, c in wp:
                        mm = pe.matmul(ps[:, 2 * i + c, 0:n], cst("ones_h"), ex[:, i, t0:t0 + n], start=True, stop=True)
                    mm.then_inc(sig["dn_mm", l], 1)
                pe.wait_ge(sig["dn_done", l], since("dn_done", l) + 2)
                held = None
                for blk in range(OUT_BLOCKS):
                    w = ready(at[f"out{l}"] + blk)
                    for ct in range(4):
                        i = 4 * blk + ct
                        if i >= 2:
                            pe.wait_ge(sig["o_ev", l], since("o_ev", l) + i - 1)
                        for k in range(KD):
                            for t0, n, c in wp:
                                mm = pe.matmul(ps[:, 4 + 2 * (i % 2) + c, 0:n], w[:, k, P * ct:P * ct + P],
                                               u[:, k, t0:t0 + n], start=k == 0, stop=k == KD - 1)
                        mm.then_inc(sig["o_mm", l], 1)
                        release(held)
                        held = None
                    held = (at[f"out{l}"] + blk, sig["o_mm", l], since("o_mm", l) + 4 * blk + 4)
                release(held)
                norm_sum("n2", l, wp)
                nt = TL + (TC if l == 0 else 0)
                pe.wait_ge(sig["n2_u", l], since("n2_u", l) + KD)
                wr = sm(l, "router").rearrange("p (k e) -> p k e", e=E)
                for t in range(nt):
                    for k in range(KD):
                        mm = pe.matmul(ps[:, 2, E * t:E * t + E], u[:, k, P * t:P * t + P], wr[:, k, :],
                                       start=k == 0, stop=k == KD - 1)
                mm.then_inc(sig["r_mm", l], 1)
                pe.wait_ge(sig["o_ev", l], since("o_ev", l) + 8)
                for x in range(2 * nt):
                    if x >= 2:
                        pe.wait_ge(sig["ut_ev", l], since("ut_ev", l) + x - 1)
                    for y in range(4):
                        mm = pe.transpose(ps[:, 4 + x % 2, P * y:P * y + P],
                                          u[:, 4 * (x % 2) + y, P * (x // 2):P * (x // 2) + P], cst("ident"))
                    mm.then_inc(sig["ut_mm", l], 1)
                pe.wait_ge(sig["r_aff", l], since("r_aff", l) + 1)
                for t in range(nt):
                    mm = pe.transpose(ps[0:E, t // 4, P * (t % 4):P * (t % 4) + P], lg[:, t, :], cst("ident"))
                mm.then_inc(sig["r_tr", l], 1)
                if l == 0:
                    modulation(1, 0, MOD_BLOCKS, at["mod1"])
                pe.wait_ge(sig["r_pos", l], since("r_pos", l) + 1)
                for t in range(nt):
                    mm = pe.transpose(ps[:, 3, E * t:E * t + E], pos[:, P * t:P * t + P], cst("ident", E)[:, 0:E])
                mm.then_inc(sig["r_ptr", l], 1)
                both = l == 0
                XW = 192 if both else P
                pe.wait_ge(sig["ut_ev", l], since("ut_ev", l) + 2 * nt)
                pe.wait_ge(sig["mod_ev"], 2 * MOD_BLOCKS)
                xe = [view(XE_AT + i * KD * 192, KD, XW) for i in range(2)]

                def gather(buf, cnt):
                    pe.wait_ge(sig["e_g", l], cnt * 1 + 1)
                    for dt in range(KD):
                        pe.wait_ge(sig["e_xev", l], cnt * 8 + max(dt - 1, 0))
                        b = 6 + dt % 2
                        if both:
                            lo = ps[:, b, 0:XW].rearrange("p (x y) -> p x y", y=64)[:, 0:3:2, :]
                        else:
                            lo = ps[:, b, 0:XW]
                        for t in range(TL):
                            mm = pe.matmul(lo, utok[:, t, P * dt:P * dt + P], gl[:, t, :], start=t == 0, stop=t == TL - 1)
                        if both:
                            for t in range(TC):
                                mm = pe.matmul(ps[:, b, 64:128], utok[:, TL + t, P * dt:P * dt + P], gc[:, t, :],
                                               start=t == 0, stop=t == TC - 1)
                        mm.then_inc(sig["e_xmm", l], 1)

                pe.wait_ge(sig["e_clear", l], 1)
                gather(0, 0)
                with pe.Fori(0, PAIRS // 2) as pp:
                    for half_p in range(2):
                        buf = half_p
                        pe.wait_ge(sig["e_xev", l], pp * 16 + (half_p + 1) * 8)
                        n0 = at[f"exp{l}"] + 12 * half_p
                        held = None
                        for e in range(2):
                            x0 = 64 * e if both else 0
                            for half in range(2):
                                for gu in range(2):
                                    n = n0 + 4 * e + 2 * half + gu
                                    w = ready(n, pp * 2)
                                    b = 2 * half + gu
                                    pe.wait_ge(sig["e_h", l], pp * 8 + max(4 * half_p + 2 * e + half - 1, 0))
                                    for f in range(4):
                                        for k in range(KD):
                                            mm = pe.matmul(ps[:, b, P * f:P * f + P], w[:, k, P * f:P * f + P],
                                                           xe[buf][:, k, x0:x0 + P], start=k == 0, stop=k == KD - 1)
                                        if f == 0:
                                            release(held)
                                    mm.then_inc(sig["e_gu", l], 1)
                                    held = (n, sig["e_gu", l], pp * 16 + 8 * half_p + 4 * e + 2 * half + gu + 1)
                        for e in range(2):
                            pe.wait_ge(sig["e_h", l], pp * 8 + 4 * half_p + 2 * e + 2)
                            for dh in range(2):
                                n = n0 + 8 + 2 * e + dh
                                w = ready(n, pp * 2)
                                pe.wait_ge(sig["e_y", l], pp * 8 + max(4 * half_p + 2 * e + dh - 1, 0))
                                for k in range(KD):
                                    mm = pe.matmul(ps[:, 4 + dh, :], he[e][:, k, :], w[:, k, :],
                                                   start=k == 0, stop=k == KD - 1)
                                    if k == 1:
                                        release(held)
                                mm.then_inc(sig["e_dn", l], 1)
                                held = (n, sig["e_dn", l], pp * 8 + 4 * half_p + 2 * e + dh + 1)
                        gather(1 - buf, pp * 2 + half_p + 1)
                        release(held)
                        pe.wait_ge(sig["e_s", l], pp * 2 + half_p + 1)
                        pe.wait_ge(sig["e_y", l], pp * 8 + 4 * half_p + 4)
                        pe.wait_ge(sig["e_xev", l], (pp * 2 + half_p + 2) * 8)
                        for dt in range(KD):
                            if both:
                                pe.wait_ge(sig["e_acc", l], pp * 16 + half_p * 8 + max(dt - 1, 0))
                                pe.matmul(ps[:, 2 + dt % 2, 0:CTX], yc[:, P * dt:P * dt + P], s_ctx, start=True, stop=True)
                            else:
                                pe.wait_ge(sig["e_acc", l], pp * 16 + half_p * 8 + max(dt - 1, 0))
                            pe.matmul(ps[:, 6 + dt % 2, :], yl[:, P * dt:P * dt + P], s_lat, start=True,
                                      stop=True).then_inc(sig["e_sc", l], 1)
                        pe.wait_ge(sig["e_acc", l], (pp * 2 + half_p + 1) * 8)
            for k in range(KD):
                pe.wait_ge(sig["fin_sq"], k + 1)
                pe.matmul(ps[:, 0, :], cst("ones_d"), ex[:, k % 2, 0:LAT], start=k == 0,
                          stop=k == KD - 1).then_inc(sig["fin_mm"], 1)

        @block.scalar
        def _(act):
            act.wait_ge(sig["loaded"], 48)
            act.activation(cond_t[:], cond[:], ACT.Tanh, scale=0.5).then_inc(sig["cond_tanh"], 1)

            def norm(which, l, parts):
                for k in range(KD):
                    if k >= 2:
                        act.wait_ge(sig[which + "_mm", l], since(which + "_mm", l) + k - 1)
                    t1 = parts[-1][0] + parts[-1][1]
                    act.activation(ex[:, k % 2, 0:t1], h[:, k, 0:t1], ACT.Square).then_inc(sig[which + "_sq", l], 1)
                act.wait_ge(sig[which + "_mm", l], since(which + "_mm", l) + KD)
                act.activation(ex[:, 2, 0:t1], bank2(0, t1), ACT.Sqrt, bias=cst("eps")).then_inc(sig[which + "_root", l], 1)
                sh = 0 if which == "n1" else 24
                for k in range(KD):
                    act.wait_ge(sig[which + "_pre", l], since(which + "_pre", l) + k + 1)
                    for t0, n, c in parts:
                        last = act.activation(u[:, k, t0:t0 + n], u[:, k, t0:t0 + n], ACT.Identity,
                                              bias=mod[:, l, sh + k, c:c + 1])
                    last.then_inc(sig[which + "_u", l], 1)

            for l in range(LAYERS):
                if l == 0:
                    act.wait_ge(sig["x_loaded"], 16)
                    act.wait_ge(sig["lam_dot"], 2 * LAYERS)
                    act.activation(lam[:, 0:4], lam[:, 0:4], ACT.Exp).then_inc(sig["lam_exp"], 1)
                norm("n1", l, parts_of(l))
                act.wait_ge(sig["n1_u", l], since("n1_u", l) + KD)
                nt = nv = 0
                for blk in range(IN_BLOCKS):
                    for what, i in P_ORDER[blk]:
                        if what == "t":
                            kind, _, _, dst = T_TILES[i]
                            wd = t_width(l, kind)
                            src = bank2(2 * (nt % 2), wd)
                            act.wait_ge(sig["t_mm", l], since("t_mm", l) + nt + 1)
                            if kind == "g":
                                last = act.activation(th[:, dst, 0:wd], src, ACT.Tanh, scale=0.5)
                            elif kind == "a":
                                last = act.activation(a_raw[:, dst, 0:wd], src, ACT.Copy, scale=0.5)
                            else:
                                scale = {"nq": HD ** -0.5, "dq": DQ ** -0.5}.get(kind, 1.0)
                                last = act.activation(qk[:, dst, 0:wd], src, ACT.Copy, scale=scale)
                            last.then_inc(sig["t_ev", l], 1)
                            nt += 1
                        else:
                            _, _, cn, v0 = V_COLS[i]
                            for t in range(TL + TC):
                                act.wait_ge(sig["v_mm", l], since("v_mm", l) + nv + 1)
                                act.activation(val[:, t, v0:v0 + cn], ps[:, 4 + nv % 2, 0:cn],
                                               ACT.Copy).then_inc(sig["v_ev", l], 1)
                                nv += 1
                act.wait_ge(sig["z_done", l], since("z_done", l) + 2)
                act.wait_ge(sig["t_ev", l], since("t_ev", l) + len(T_TILES))
                for i, (tile, g) in enumerate(HN):
                    wd = t_width(l, g)
                    act.activation(tmp[i][:, 0:wd], qk[:, tile, 0:wd], ACT.Square).then_inc(sig["hn_sq", l], 1)
                for i, (tile, g) in enumerate(HN):
                    wd = t_width(l, g)
                    act.wait_ge(sig["hn_mm", l], since("hn_mm", l) + i + 1)
                    act.activation(tmp[i][:, 0:wd], bank2(2 * i, wd), ACT.Sqrt, bias=cst("eps")).then_inc(sig["hn_root", l], 1)
                pc = parts_of(0)[:2 - l]
                act.wait_ge(sig["c_cent", l], since("c_cent", l) + 1)
                for j in range(2):
                    for t0, n, c in pc:
                        s0 = t0 + (2 * HALO if c else 0)
                        last = act.activation(tmp[j][:, t0:t0 + n], acc[:, j, s0:s0 + n], ACT.Square)
                    last.then_inc(sig["c_sq", l], 1)
                wc = pc[-1][0] + pc[-1][1]
                act.wait_ge(sig["c_var", l], since("c_var", l) + 1)
                act.activation(tmp[2][:, 0:wc], bank2(2, wc), ACT.Sqrt, bias=cst("eps")).then_inc(sig["c_root", l], 1)
                for j in range(2):
                    act.wait_ge(sig["c_lin", l], since("c_lin", l) + j + 1)
                    for t0, n, c in pc:
                        s0 = t0 + (2 * HALO if c else 0)
                        last = act.activation(tmp[j][:, t0:t0 + n], acc[:, j, s0:s0 + n], ACT.Tanh, scale=0.5)
                    last.then_inc(sig["c_tanh", l], 1)
                for co in range(2):
                    act.wait_ge(sig["c_pw", l], since("c_pw", l) + co + 1)
                    act.activation(u[:, 2 + co, 0:wc], bank2(4 * co, wc), ACT.Identity, scale=0.5,
                                   bias=sm(l, "pw_b")[:, co:co + 1]).then_inc(sig["c_out", l], 1)
                for kind in kinds(l):
                    s, s0 = at_sem, attn_since(l, kind)
                    lat = kind == "lat"
                    k0, kn, trips = (0, TOK, TL) if lat else (LAT, CTX, TC)
                    with act.Fori(0, trips) as it:
                        def evac(i):
                            if lat:
                                act.wait_ge(s["t_mm"], s0["t_mm"] + it * 24 + 2 * i + 2)
                                act.activation(pt[:, LAT:TOK], ps[:, 5, 0:CTX], ACT.Copy).then_inc(s["t_act"], 1)

                        done = 0
                        for j in range(16):
                            act.wait_ge(s["s_max"], s0["s_max"] + it * 16 + j + 1)
                            src = ex[:, j % 3, 0:kn] if (lat and j < 4) else bank2(2 * (j % 2), kn)
                            act.activation(ex[:, j % 3, 0:kn], src, ACT.Exp, bias=negmax[:, j:j + 1],
                                           accum_out=sums[:, j:j + 1]).then_inc(s["s_exp"], 1)
                            while done < 12 and last_score[done] < j:
                                evac(done)
                                done += 1
                        while done < 12:
                            evac(done)
                            done += 1
                        base = k0 + it * P
                        act.wait_ge(s["y_mm"], s0["y_mm"] + it * 2 + 1)
                        for x, y0 in enumerate((0, 4)):
                            act.activation(u[:, y0:y0 + 2, bass.ds(base, P)],
                                           ps[:, 4, 256 * x:256 * x + 256].rearrange("p (a b) -> p a b", b=P),
                                           ACT.Copy).then_inc(s["y_ev"], 1)
                        act.wait_ge(s["y_mm"], s0["y_mm"] + it * 2 + 2)
                        act.activation(u[:, 6:8, bass.ds(base, P)],
                                       ps[:, 5, 0:256].rearrange("p (a b) -> p a b", b=P),
                                       ACT.Copy).then_inc(s["y_ev"], 1)
                    act.wait_ge(s["y_ev"], s0["y_ev"] + 3 * trips)
                wc = TOK if l == 0 else LAT
                for i in range(2):
                    act.activation(ex[:, i, 0:wc], u[:, 6 + i, 0:wc], ACT.Square).then_inc(sig["dn_sq", l], 1)
                for i in range(2):
                    act.wait_ge(sig["dn_mm", l], since("dn_mm", l) + i + 1)
                    act.activation(ex[:, i, 0:wc], bank2(2 * i, wc), ACT.Sqrt, bias=cst("eps")).then_inc(sig["dn_root", l], 1)
                act.wait_ge(sig["o_ev", l], since("o_ev", l) + 8)
                act.wait_ge(sig["dn_done", l], since("dn_done", l) + 2)
                norm("n2", l, parts_of(l, True))
                nt = TL + (TC if l == 0 else 0)
                act.wait_ge(sig["r_cp", l], since("r_cp", l) + 1)
                act.activation(lg[:, 0:nt, :], lg[:, 0:nt, :], ACT.Exp).then_inc(sig["r_exp", l], 1)
                for x in range(2 * nt):
                    act.wait_ge(sig["ut_mm", l], since("ut_mm", l) + x + 1)
                    act.activation(utok[:, x // 2, 512 * (x % 2):512 * (x % 2) + 512], ps[:, 4 + x % 2, :],
                                   ACT.Copy).then_inc(sig["ut_ev", l], 1)
                act.wait_ge(sig["r_tr", l], since("r_tr", l) + 1)
                act.activation(afft[:, 0:P * nt], psf[0:E, 0:P * nt], ACT.Copy, scale=0.5).then_inc(sig["r_afft", l], 1)
                both = l == 0
                XW = 192 if both else P
                xe = [view(XE_AT + i * KD * 192, KD, XW) for i in range(2)]

                def take_gather(buf, cnt):
                    for dt in range(KD):
                        act.wait_ge(sig["e_xmm", l], cnt * 8 + dt + 1)
                        act.activation(xe[buf][:, dt, :], ps[:, 6 + dt % 2, 0:XW], ACT.Copy).then_inc(sig["e_xev", l], 1)

                act.wait_ge(sig["ut_ev", l], since("ut_ev", l) + 2 * nt)
                take_gather(0, 0)
                with act.Fori(0, PAIRS // 2) as pp:
                    for half_p in range(2):
                        for e in range(2):
                            for half in range(2):
                                act.wait_ge(sig["e_gu", l], pp * 16 + 8 * half_p + 4 * e + 2 * half + 1)
                                act.wait_ge(sig["e_h", l], pp * 8 + 4 * half_p + 2 * e + half)
                                act.activation(th2, ps[:, 2 * half, :], ACT.Tanh, scale=0.5).then_inc(sig["e_tanh", l], 1)
                        for e in range(2):
                            for dh in range(2):
                                act.wait_ge(sig["e_dn", l], pp * 8 + 4 * half_p + 2 * e + dh + 1)
                                act.wait_ge(sig["e_sc", l], pp * 16 + 8 * half_p)
                                rows = slice(64 * e, 64 * e + 64)
                                last = act.activation(yl[rows, 512 * dh:512 * dh + 512], ps[rows, 4 + dh, :], ACT.Copy)
                                if both:
                                    rows = slice(32 + 32 * (1 - e), 64 + 32 * (1 - e))
                                    last = act.activation(yc[rows, 512 * dh:512 * dh + 512], ps[rows, 4 + dh, :], ACT.Copy)
                                last.then_inc(sig["e_y", l], 1)
                        take_gather(1 - half_p, pp * 2 + half_p + 1)
                act.wait_ge(sig["e_acc", l], 8 * PAIRS)
            for k in range(KD):
                if k >= 2:
                    act.wait_ge(sig["fin_mm"], k - 1)
                act.activation(ex[:, k % 2, 0:LAT], h[:, k, 0:LAT], ACT.Square).then_inc(sig["fin_sq"], 1)
            act.wait_ge(sig["fin_mm"], KD)
            act.activation(ex[:, 2, 0:LAT], ps[:, 0, :], ACT.Sqrt, bias=cst("eps")).then_inc(sig["fin_root"], 1)

        @block.vector
        def _(dve):
            selfs = {}

            def link(ins, key):
                selfs[key] = selfs.get(key, 0) + 1
                ins.then_inc(sig[key], 1)
                dve.wait_ge(sig[key], selfs[key])

            dve.wait_ge(sig["loaded"], 48)
            for l in range(LAYERS):
                lv = sm(l, "lam").rearrange("p (a b) -> p a b", b=DQ)
                for i in range(2):
                    dve.tensor_tensor_reduce(ex[:, i, 0:DQ], lv[:, 2 * i, :], lv[:, 2 * i + 1, :], 1.0, 0.0, ALU.mult,
                                             ALU.add, lam[:, 2 * l + i:2 * l + i + 1]).then_inc(sig["lam_dot"], 1)
                    dve.wait_ge(sig["lam_dot"], 2 * l + i + 1)
            dve.wait_ge(sig["cond_tanh"], 1)
            link(dve.scalar_tensor_tensor(cond[:], cond_t[:], 1.0, cond[:], ALU.add, ALU.mult), "self0")
            dve.tensor_scalar(cond[:], cond[:], 0.5, None, ALU.mult).then_inc(sig["cond_done"], 1)
            dve.wait_ge(sig["lam_exp"], 1)
            for l in range(LAYERS):
                link(dve.tensor_tensor(lam[:, 2 * l:2 * l + 1], lam[:, 2 * l + 1:2 * l + 2], lam[:, 2 * l:2 * l + 1],
                                       ALU.subtract), "self0")
                link(dve.tensor_scalar(lam[:, 2 * l:2 * l + 1], lam[:, 2 * l:2 * l + 1], -LAM_INIT[l], None, ALU.add), "self0")

            def modulation(l, j0, j1):
                bm = sm(l, "b_mod").rearrange("p (b c) -> p b c", c=2)
                for j in range(j0, j1):
                    dve.wait_ge(sig["mod_mm"], l * MOD_BLOCKS + j + 1)
                    dve.tensor_tensor(mod[:, l, 4 * j:4 * j + 4, :],
                                      ps[:, 6 + j % 2, :].rearrange("p (b c) -> p b c", c=P)[:, :, 0:2],
                                      bm[:, 4 * j:4 * j + 4, :], ALU.add).then_inc(sig["mod_ev"], 1)

            def make_gain(l, i):
                g = sm(l, ("norm1", "norm2")[i]).rearrange("p (k c) -> p k c", c=2)
                dve.scalar_tensor_tensor(gain[:, i, :, :], mod[:, l, 24 * i + 8:24 * i + 16, :], 1.0, g, ALU.add,
                                         ALU.mult).then_inc(sig["gain_done"], 1)
                dve.wait_ge(sig["gain_done"], 2 * l + i + 1)

            def norm(which, l, parts):
                t1 = parts[-1][0] + parts[-1][1]
                dve.wait_ge(sig[which + "_root", l], since(which + "_root", l) + 1)
                link(dve.reciprocal(ex[:, 2, 0:t1], ex[:, 2, 0:t1]), ("self", l))
                i = 0 if which == "n1" else 1
                for k in range(KD):
                    for t0, n, c in parts:
                        last = dve.scalar_tensor_tensor(u[:, k, t0:t0 + n], h[:, k, t0:t0 + n], gain[:, i, k, c:c + 1],
                                                        ex[:, 2, t0:t0 + n], ALU.mult, ALU.mult)
                    last.then_inc(sig[which + "_pre", l], 1)

            for l in range(LAYERS):
                me = ("self", l)
                if l == 0:
                    modulation(0, 0, 4)
                    dve.wait_ge(sig["mod_ev"], 4)
                make_gain(l, 0)
                if l:
                    make_gain(l, 1)
                norm("n1", l, parts_of(l))
                link(dve.tensor_scalar(qn_s[:, 0:1], sm(l, "qn"), HD ** -0.5, None, ALU.mult), me)
                link(dve.tensor_scalar(qn_s[:, 1:2], sm(l, "dn"), 1.0 - LAM_INIT[l], None, ALU.mult), me)
                pc = parts_of(0)[:2 - l]
                dve.wait_ge(sig["z_zero", l], since("z_zero", l) + 1)
                for j in range(2):
                    dve.wait_ge(sig["t_ev", l], since("t_ev", l) + 7 + j)
                    for t0, n, c in pc:
                        z0 = t0 + HALO + (2 * HALO if c else 0)
                        last = dve.scalar_tensor_tensor(z[:, j, z0:z0 + n], th[:, j, t0:t0 + n], 1.0, a_raw[:, j, t0:t0 + n],
                                                        ALU.add, ALU.mult)
                    last.then_inc(sig["z_done", l], 1)
                n = ACCW if l == 0 else LAT
                taps = sm(l, "taps").rearrange("p (j t) -> p j t", t=TAPS)
                dve.wait_ge(sig["z_done", l], since("z_done", l) + 2)
                for j in range(2):
                    dve.tensor_scalar(acc[:, j, 0:n], z[:, j, 0:n], taps[:, j, 0:1], sm(l, "dw_b")[:, j:j + 1], ALU.mult,
                                      ALU.add).then_inc(sig["tap", l], 1)
                with dve.Fori(1, TAPS) as i:
                    for j in range(2):
                        dve.wait_ge(sig["tap", l], i * 2 + j - 1)
                        dve.scalar_tensor_tensor(acc[:, j, 0:n], z[:, j, bass.ds(i, n)], taps[:, j, bass.ds(i, 1)],
                                                 acc[:, j, 0:n], ALU.mult, ALU.add).then_inc(sig["tap", l], 1)
                for i, (tile, g) in enumerate(HN):
                    wd = t_width(l, g)
                    dve.wait_ge(sig["hn_root", l], since("hn_root", l) + i + 1)
                    link(dve.reciprocal(tmp[i][:, 0:wd], tmp[i][:, 0:wd]), me)
                    gcol = qn_s[:, 0:1] if g == "q" else sm(l, "kn")
                    dve.scalar_tensor_tensor(qk[:, tile, 0:wd], qk[:, tile, 0:wd], gcol, tmp[i][:, 0:wd], ALU.mult,
                                             ALU.mult).then_inc(sig["hn_done", l], 1)
                dve.wait_ge(sig["tables", l], since("tables", l) + 16)
                dve.wait_ge(sig["hn_done", l], since("hn_done", l) + 3)
                for i, (tile, _, tb) in enumerate(ROPE):
                    dve.wait_ge(sig["rp_mm", l], since("rp_mm", l) + i + 1)
                    t = tmp[i % 2][:, 0:LAT]
                    dve.tensor_tensor(t, ps[:, 4 + i % 2, :], tab[:, tb + 1, :], ALU.mult).then_inc(sig["rp_done", l], 1)
                    link(dve.tensor_tensor(qk[:, tile, 0:LAT], qk[:, tile, 0:LAT], tab[:, tb, :], ALU.mult), me)
                    dve.wait_ge(sig["rp_done", l], since("rp_done", l) + i + 1)
                    link(dve.tensor_tensor(qk[:, tile, 0:LAT], qk[:, tile, 0:LAT], t, ALU.add), me)
                if l == 0:
                    modulation(0, 4, MOD_BLOCKS)
                    dve.wait_ge(sig["mod_ev"], MOD_BLOCKS)
                    make_gain(0, 1)
                dve.wait_ge(sig["c_mean", l], since("c_mean", l) + 1)
                for t0, n, c in pc:
                    s0 = t0 + (2 * HALO if c else 0)
                    last = dve.tensor_tensor(acc[:, :, s0:s0 + n], acc[:, :, s0:s0 + n],
                                             ps[:, c, 0:n].unsqueeze(1).to_broadcast([P, 2, n]), ALU.subtract)
                last.then_inc(sig["c_cent", l], 1)
                wc = pc[-1][0] + pc[-1][1]
                dve.wait_ge(sig["c_root", l], since("c_root", l) + 1)
                link(dve.reciprocal(tmp[2][:, 0:wc], tmp[2][:, 0:wc]), me)
                for j in range(2):
                    for t0, n, c in pc:
                        s0 = t0 + (2 * HALO if c else 0)
                        link(dve.scalar_tensor_tensor(acc[:, j, s0:s0 + n], acc[:, j, s0:s0 + n], sm(l, "ln_g")[:, j:j + 1],
                                                      tmp[2][:, t0:t0 + n], ALU.mult, ALU.mult), me)
                        last = dve.tensor_scalar(acc[:, j, s0:s0 + n], acc[:, j, s0:s0 + n], sm(l, "ln_b")[:, j:j + 1], None,
                                                 ALU.add)
                    last.then_inc(sig["c_lin", l], 1)
                for j in range(2):
                    dve.wait_ge(sig["c_tanh", l], since("c_tanh", l) + j + 1)
                    for t0, n, c in pc:
                        s0 = t0 + (2 * HALO if c else 0)
                        last = dve.scalar_tensor_tensor(acc[:, j, s0:s0 + n], tmp[j][:, t0:t0 + n], 1.0,
                                                        acc[:, j, s0:s0 + n], ALU.add, ALU.mult)
                last.then_inc(sig["c_act", l], 1)
                for kind in kinds(l):
                    s, s0 = at_sem, attn_since(l, kind)
                    lat = kind == "lat"
                    k0, kn, trips = (0, TOK, TL) if lat else (LAT, CTX, TC)
                    if lat:
                        dve.wait_ge(sig["bias_done", l], since("bias_done", l) + 1)
                    SELF = (4 if lat else 0) + 12 + 8
                    with dve.Fori(0, trips) as it:
                        cnt = [0]

                        def chain(ins):
                            cnt[0] += 1
                            ins.then_inc(s["self"], 1)
                            dve.wait_ge(s["self"], s0["self"] + it * SELF + cnt[0])

                        def top(j):
                            dve.wait_ge(s["s_mm"], s0["s_mm"] + it * 16 + j + 1)
                            b = 2 * (j % 2)
                            if lat and j < 4:
                                off = (6 * GRID_W) - it * (2 * GRID_W)
                                dve.tensor_tensor(ex[:, j % 3, 0:LAT], ps[:, b, :], bt[:, j, bass.ds(off, LAT)], ALU.add)
                                chain(dve.tensor_copy(ex[:, j % 3, LAT:TOK], ps[:, b + 1, 0:CTX]))
                                src = ex[:, j % 3, 0:kn]
                            else:
                                src = bank2(b, kn)
                            dve.tensor_reduce(negmax[:, j:j + 1], src, AX.X, ALU.max, negate=True).then_inc(s["s_max"], 1)

                        def evac(i):
                            n = LAT if lat else CTX
                            dve.wait_ge(s["t_mm"], s0["t_mm"] + it * (24 if lat else 12) + ((2 if lat else 1) * i + 1))
                            dve.tensor_copy(pt[:, 0:n], ps[:, 4, 0:n]).then_inc(s["t_dve"], 1)

                        def finish(i):
                            j = i if i < 8 else last_score[i] - 1
                            if i < 8:
                                dve.wait_ge(s["s_exp"], s0["s_exp"] + it * 16 + j + 1)
                                chain(dve.reciprocal(rsum[:, j:j + 1], sums[:, j:j + 1]))
                            dve.wait_ge(s["o_mm"], s0["o_mm"] + it * 12 + i + 1)
                            o0 = HD * (i % 2)
                            dve.tensor_scalar(otok[:, HD * i:HD * i + HD], ps[:, 6 + i % 2, o0:o0 + HD], rsum[:, j:j + 1], None,
                                              ALU.mult).then_inc(s["o_ev"], 1)

                        def difference(i):
                            j1 = last_score[i]
                            j0 = j1 - 1
                            dve.wait_ge(s["s_exp"], s0["s_exp"] + it * 16 + j1 + 1)
                            chain(dve.reciprocal(rsum[:, j0:j1 + 1], sums[:, j0:j1 + 1]))
                            chain(dve.scalar_tensor_tensor(rsum[:, j1:j1 + 1], rsum[:, j1:j1 + 1], lam[:, 2 * l:2 * l + 1],
                                                           sums[:, j0:j0 + 1], ALU.mult, ALU.mult))
                            chain(dve.scalar_tensor_tensor(ex[:, j1 % 3, 0:kn], ex[:, j1 % 3, 0:kn], rsum[:, j1:j1 + 1],
                                                           ex[:, j0 % 3, 0:kn], ALU.mult, ALU.add))
                            dve.sem_inc(s["p_diff"], 1)

                        top(0)
                        top(1)
                        nxt = 2
                        for i in range(12):
                            if i >= 8:
                                difference(i)
                            evac(i)
                            while nxt < 16 and nxt <= last_score[i] + 2:
                                top(nxt)
                                nxt += 1
                            finish(i)
                        assert cnt[0] == SELF, cnt
                wc = TOK if l == 0 else LAT
                for i in range(2):
                    dve.wait_ge(sig["dn_root", l], since("dn_root", l) + i + 1)
                    link(dve.reciprocal(ex[:, i, 0:wc], ex[:, i, 0:wc]), me)
                    dve.scalar_tensor_tensor(u[:, 6 + i, 0:wc], u[:, 6 + i, 0:wc], qn_s[:, 1:2], ex[:, i, 0:wc], ALU.mult,
                                             ALU.mult).then_inc(sig["dn_done", l], 1)
                for i in range(8):
                    dve.wait_ge(sig["o_mm", l], since("o_mm", l) + i + 1)
                    for t0, n, c in parts_of(0)[:2 - l]:
                        last = dve.scalar_tensor_tensor(h[:, i, t0:t0 + n], ps[:, 4 + 2 * (i % 2) + c, 0:n],
                                                        mod[:, l, 16 + i, c:c + 1], h[:, i, t0:t0 + n], ALU.mult, ALU.add)
                    last.then_inc(sig["o_ev", l], 1)
                dve.wait_ge(sig["o_ev", l], since("o_ev", l) + 8)
                norm("n2", l, parts_of(l, True))
                nt = TL + (TC if l == 0 else 0)
                dve.wait_ge(sig["r_mm", l], since("r_mm", l) + 1)
                lgv = lg[:, 0:nt, :]
                link(dve.tensor_copy(lgv, ps[:, 2, 0:E * nt].rearrange("p (t e) -> p t e", e=E)), me)
                link(dve.tensor_reduce(mx6[:, 0:nt], lgv, AX.X, ALU.max), me)
                dve.tensor_tensor(lgv, lgv, mx6[:, 0:nt].unsqueeze(2).to_broadcast([P, nt, E]),
                                  ALU.subtract).then_inc(sig["r_cp", l], 1)
                dve.wait_ge(sig["r_exp", l], since("r_exp", l) + 1)
                link(dve.tensor_reduce(mx6[:, 0:nt], lgv, AX.X, ALU.add), me)
                link(dve.reciprocal(mx6[:, 0:nt], mx6[:, 0:nt]), me)
                dve.tensor_tensor(lgv, lgv, mx6[:, 0:nt].unsqueeze(2).to_broadcast([P, nt, E]),
                                  ALU.mult).then_inc(sig["r_aff", l], 1)
                dve.wait_ge(sig["r_afft", l], since("r_afft", l) + 1)
                wt = P * nt
                link(dve.tensor_copy(wrk[:, 0:wt], afft[:, 0:wt]), me)
                groups = [(0, LAT, CAP_L)] + ([(LAT, CTX, CAP_C)] if l == 0 else [])
                for t0, n, cap in groups:
                    for r in range(cap // 8):
                        link(dve.max(top8[:], wrk[:, t0:t0 + n]), me)
                        link(dve.match_replace(wrk[:, t0:t0 + n], top8[:], wrk[:, t0:t0 + n], -1.0), me)
                link(dve.tensor_scalar(wrk[:, 0:wt], wrk[:, 0:wt], 0.0, None, ALU.is_lt), me)
                for t0, n, cap in groups:
                    link(dve.tensor_tensor_scan(cum[:, t0:t0 + n], wrk[:, t0:t0 + n], wrk[:, t0:t0 + n], 0.0, ALU.add,
                                                ALU.max), me)
                link(dve.tensor_tensor(pos[:, 0:wt], cum[:, 0:wt], wrk[:, 0:wt], ALU.mult), me)
                dve.tensor_scalar(pos[:, 0:wt], pos[:, 0:wt], -1.0, None, ALU.add).then_inc(sig["r_pos", l], 1)
                if l == 0:
                    modulation(1, 0, MOD_BLOCKS)
                    dve.wait_ge(sig["mod_ev"], 2 * MOD_BLOCKS)
                both = l == 0
                dve.wait_ge(sig["e_clear", l], 1)
                dve.wait_ge(sig["r_ptr", l], since("r_ptr", l) + 1)
                link(dve.tensor_copy(ptok[:, 0:nt, 0:E], ps[:, 3, 0:E * nt].rearrange("p (t e) -> p t e", e=E)), me)

                def one_hot(cnt, off):
                    dve.wait_ge(sig["e_xmm", l], cnt * 8)
                    last = dve.tensor_tensor(gl[:, :, :].rearrange("p t (e j) -> p t e j", j=64),
                                             cst("iota").unsqueeze(1).unsqueeze(1).to_broadcast([P, TL, 2, 64]),
                                             ptok[:, 0:TL, bass.ds(off, 2)].unsqueeze(3).to_broadcast([P, TL, 2, 64]),
                                             ALU.is_equal)
                    if both:
                        last = dve.tensor_tensor(gc[:, :, :].rearrange("p t (e j) -> p t e j", j=32),
                                                 cst("iota")[:, 0:32].unsqueeze(1).unsqueeze(1).to_broadcast([P, TC, 2, 32]),
                                                 ptok[:, TL:TL + TC, bass.ds(off, 2)].unsqueeze(3).to_broadcast([P, TC, 2, 32]),
                                                 ALU.is_equal)
                    last.then_inc(sig["e_g", l], 1)

                one_hot(0, 0)
                with dve.Fori(0, PAIRS // 2) as pp:
                    for half_p in range(2):
                        dve.wait_ge(sig["e_bc", l], (pp * 2 + half_p + 1) * 16 * (4 if both else 2))
                        dve.wait_ge(sig["e_sc", l], (pp * 2 + half_p) * 8)
                        last = dve.scalar_tensor_tensor(s_lat, pbl[:, 0, :], cst("j_lat"), pbl[:, 1, :], ALU.is_equal, ALU.mult)
                        if both:
                            last = dve.scalar_tensor_tensor(s_ctx, pbc[:, 0, :], cst("j_ctx"), pbc[:, 1, :], ALU.is_equal,
                                                            ALU.mult)
                        last.then_inc(sig["e_s", l], 1)
                        one_hot(pp * 2 + half_p + 1, pp * 4 + (2 * half_p + 2))
                        for e in range(2):
                            for half in range(2):
                                dve.wait_ge(sig["e_tanh", l], pp * 8 + 4 * half_p + 2 * e + half + 1)
                                dve.scalar_tensor_tensor(th2, th2, 1.0, ps[:, 2 * half, :], ALU.add, ALU.mult).then_inc(sig["tap", l], 1)
                                dve.wait_ge(sig["tap", l], pp * 8 + (2 * TAPS + 4 * half_p + 2 * e + half + 1))
                                dve.wait_ge(sig["e_gu", l], pp * 16 + 8 * half_p + 4 * e + 2 * half + 2)
                                dve.wait_ge(sig["e_dn", l], pp * 8 + max(4 * half_p + 2 * e - 2, 0))
                                dve.tensor_tensor(he[e][:, 4 * half:4 * half + 4, :],
                                                  th2.rearrange("p (f w) -> p f w", w=P),
                                                  ps[:, 2 * half + 1, :].rearrange("p (f w) -> p f w", w=P), ALU.mult).then_inc(sig["e_h", l], 1)
                        for dt in range(KD):
                            dve.wait_ge(sig["e_sc", l], pp * 16 + 8 * half_p + dt + 1)
                            last = dve.scalar_tensor_tensor(h[:, dt, 0:LAT], ps[:, 6 + dt % 2, :],
                                                            mod[:, l, 40 + dt, 0:1], h[:, dt, 0:LAT], ALU.mult, ALU.add)
                            if both:
                                last = dve.scalar_tensor_tensor(h[:, dt, LAT:TOK], ps[:, 2 + dt % 2, 0:CTX],
                                                                mod[:, l, 40 + dt, 1:2], h[:, dt, LAT:TOK], ALU.mult, ALU.add)
                            last.then_inc(sig["e_acc", l], 1)
                dve.wait_ge(sig["e_acc", l], 8 * PAIRS)
            dve.wait_ge(sig["fin_root"], 1)
            dve.reciprocal(ex[:, 2, 0:LAT], ex[:, 2, 0:LAT]).then_inc(sig["fin_rinv"], 1)
            dve.wait_ge(sig["fin_rinv"], 1)
            for k in range(KD):
                dve.scalar_tensor_tensor(u[:, k, 0:LAT], h[:, k, 0:LAT], sm(0, "final")[:, k:k + 1], ex[:, 2, 0:LAT], ALU.mult,
                                         ALU.mult).then_inc(sig["fin_out"], 1)

        @block.gpsimd
        def _(pool):
            for l in range(LAYERS):
                pool.wait_ge(sig["n1_pre", l], since("n1_pre", l) + KD)
                pool.memset(z[:, :, :], 0.0).then_inc(sig["z_zero", l], 1)
                pool.dma_start(tab[:, :, :], a["tables"]).then_inc(sig["tables", l], 16)
                pool.dma_start(pw[:], a["pw"][l]).then_inc(sig["layer_in", l], 16)
                pool.wait_ge(sig["c_pw", l], since("c_pw", l) + 2)
                pool.dma_start(bt[:, :, :], a["rpb"][l]).then_inc(sig["bias_ld", l], 16)
                pool.wait_ge(sig["bias_ld", l], since("bias_ld", l) + 16)
                btv = bt[:, :, :].rearrange("p h (m w) -> p (h m) w", w=GRID_W)
                pool.tensor_tensor(btv, btv, cst("mask").unsqueeze(1).to_broadcast([P, 4 * BIAS_DR, GRID_W]),
                                   ALU.add).then_inc(sig["bias_done", l], 1)
                pool.memset(qst[:, :, :], 0.0).then_inc(sig["q_zero", l], 1)
                pool.wait_ge(sig["q_zero", l], since("q_zero", l) + 1)
                for kind in kinds(l):
                    s, s0 = at_sem, attn_since(l, kind)
                    k0, trips = (0, TL) if kind == "lat" else (LAT, TC)
                    if kind == "ctx":
                        pool.wait_ge(at_sem["s_mm"], 16 * TL)

                    def stage(g, t0, before):
                        for x, (pn, src, dst, tiles, units) in enumerate(STAGE[g]):
                            pool.tensor_copy(qst[dst:dst + pn, units, :],
                                             qk[src:src + pn, tiles, bass.ds(t0, P)]).then_inc(s["q_st"], 1)
                            pool.wait_ge(s["q_st"], before + (0, 2, 6)[g] + x + 1)

                    for g in range(3):
                        stage(g, k0, s0["q_st"])
                    with pool.Fori(1, trips) as it:
                        for g in range(3):
                            pool.wait_ge(s["s_mm"], it * 16 + (s0["s_mm"] - 16 + (4, 8, 16)[g]))
                            stage(g, it * P + k0, it * 10 + s0["q_st"])
                nt = TL + (TC if l == 0 else 0)
                pool.wait_ge(sig["n2_pre", l], since("n2_pre", l) + KD)
                both = l == 0
                pool.memset(ptok[:, :, :], -1.0)
                pool.memset(pbc[:, :, :], -7.0)
                pool.memset(yc, 0.0).then_inc(sig["e_clear", l], 1)
                pool.wait_ge(sig["r_pos", l], since("r_pos", l) + 1)
                pool.dma_start(route[:, 0, 0:P * nt], pos[:, 0:P * nt]).then_inc(sig["r_store", l], 16)
                pool.dma_start(route[:, 1, 0:P * nt], afft[:, 0:P * nt]).then_inc(sig["r_store", l], 16)
                pool.wait_ge(sig["r_store", l], since("r_store", l) + 32)
                pool.wait_ge(sig["e_clear", l], 1)
                with pool.Fori(0, PAIRS) as p:
                    pool.wait_ge(sig["e_s", l], p)
                    for e in range(2):
                        src = route[bass.ds(p * 2 + e, 1), :, 0:LAT].to_broadcast([64, 2, LAT])
                        pool.dma_start(pbl[64 * e:64 * e + 64, :, :], src).then_inc(sig["e_bc", l], 16)
                        if both:
                            r0 = 64 - 32 * e
                            src = route[bass.ds(p * 2 + e, 1), :, LAT:TOK].to_broadcast([32, 2, CTX])
                            pool.dma_start(pbc[r0:r0 + 32, :, :], src).then_inc(sig["e_bc", l], 16)


def constants():
    c = np.zeros((P, CONST_N), np.float32)

    def put(name, v):
        lo, hi = CONST[name]
        c[:, lo:hi] = v

    p = np.arange(P)
    put("ident", np.eye(P))
    put("ones_d", 1.0 / D)
    put("ones_c", 1.0 / 256)
    put("ones_h", (p[:, None] // HD == p[None, :] // HD) / HD)
    put("swap32", p[:, None] == (p[None, :] ^ 32))
    put("swap16", p[:, None] == (p[None, :] ^ 16))
    j = p % GRID_W
    start = np.clip(j - WIN_C // 2, 0, GRID_W - WIN_C)[:, None]
    w = np.arange(GRID_W)[None, :]
    put("mask", np.where((w >= start) & (w < start + WIN_C), 0.0, NEG))
    put("iota", np.arange(64)[None, :])
    put("j_lat", (p % 64)[:, None])
    put("j_ctx", (p % 32)[:, None])
    put("eps", EPS)
    tables = np.zeros((P, 4, LAT), np.float32)
    t = np.arange(LAT)
    rows, cols = (t // GRID_W).astype(np.float32), (t % GRID_W).astype(np.float32)
    for i, d in enumerate((HD, DQ)):
        half, nf = d // 2, d // 4
        inv = (1.0 / (np.float32(10000.0) ** (np.arange(nf, dtype=np.float32) / np.float32(nf)))).astype(np.float32)
        ang = np.concatenate([rows[:, None] * inv, cols[:, None] * inv], 1).T.astype(np.float32)
        r = p % d
        tables[:, 2 * i] = np.cos(ang)[r % half]
        tables[:, 2 * i + 1] = np.sin(ang)[r % half] * np.where(r < half, -1.0, 1.0)[:, None]
    return c, tables


def kernel(x, c, ctx, c_ctx, norm1_g, w_mod, b_mod, w_in, na_rpb, conv_dw_w, conv_dw_b, conv_ln_g, conv_ln_b,
           conv_pw_w, conv_pw_b, gqa_qn_g, gqa_kn_g, diff_lq1, diff_lk1, diff_lq2, diff_lk2, diff_norm_g, w_out,
           norm2_g, w_router, w_gate, w_up, w_down, final_g):
    import concourse.bacc as bacc
    from concourse.bass_utils import run_bass_kernel_spmd

    L = LAYERS

    def cols(v):
        v = np.asarray(v)
        return np.moveaxis(v.reshape(*v.shape[:-1], -1, P), -1, -2)

    def blocks(w):
        w = np.asarray(w)
        n = w.shape[-1] // BLK
        w = w.reshape(*w.shape[:-2], KD, P, n, BLK)
        return np.ascontiguousarray(np.moveaxis(w, (-2, -3, -4), (-4, -3, -2)))

    stream = np.concatenate([np.asarray(x)[0], np.asarray(ctx)[0]], 0)
    cmat, tables = constants()
    small = np.zeros((P, L, SMALL_N), np.float32)

    def put(name, v):
        lo, hi = SMALL[name]
        small[:, :, lo:hi] = np.moveaxis(np.asarray(v).reshape(L, P, -1), 0, 1)

    def twice(v):
        return np.repeat(cols(v)[..., None], 2, -1)

    put("b_mod", twice(b_mod))
    put("norm1", twice(norm1_g))
    put("norm2", twice(norm2_g))
    put("taps", np.moveaxis(cols(conv_dw_w), 1, 3))
    put("dw_b", cols(conv_dw_b))
    put("ln_g", cols(conv_ln_g))
    put("ln_b", cols(conv_ln_b))
    put("pw_b", cols(conv_pw_b))
    put("qn", np.tile(np.asarray(gqa_qn_g), (1, 2)))
    put("kn", np.tile(np.asarray(gqa_kn_g), (1, 2)))
    put("dn", np.tile(np.asarray(diff_norm_g), (1, 2)))
    lam = np.stack([np.asarray(v) for v in (diff_lq1, diff_lk1, diff_lq2, diff_lk2)], 1)
    put("lam", np.repeat(lam[:, None], P, 1))
    put("router", np.moveaxis(np.asarray(w_router).reshape(L, KD, P, E), 1, 2))
    put("final", np.repeat(cols(final_g)[None], L, 0))
    g, up, dn = blocks(w_gate), blocks(w_up), blocks(w_down)
    gate_up = np.stack([g[:, :, 0], up[:, :, 0], g[:, :, 1], up[:, :, 1]], 2).reshape(L, PAIRS, 8, P, KD, BLK)
    w_exp = np.concatenate([gate_up, dn.reshape(L, PAIRS, 4, P, KD, BLK)], 2)
    del g, up, dn, gate_up
    rpb = np.zeros((L, 4, 15, 2 * GRID_W - 1), np.float32)
    rpb[..., GRID_W - WIN_C:GRID_W - WIN_C + 2 * WIN_C - 1] = np.asarray(na_rpb)
    j, w = np.arange(GRID_W)[:, None], np.arange(GRID_W)[None, :]
    rpb = rpb[..., w - j + GRID_W - 1]
    rpb = np.stack([rpb[:, :, 1 - r:1 - r + BIAS_DR] for r in range(2)], 1)
    rpb = np.ascontiguousarray(rpb.transpose(0, 1, 4, 2, 3, 5)).reshape(L, P, 4, BIAS_DR * GRID_W)
    arrays = {
        "x": np.ascontiguousarray(np.moveaxis(stream.T.reshape(KD, P, TOK), 0, 1)),
        "cond": np.ascontiguousarray(np.stack([cols(np.asarray(c)[0]), cols(c_ctx)], -1)),
        "const": cmat, "tables": tables, "small": small, "rpb": rpb,
        "w_mod": blocks(w_mod), "w_in": blocks(w_in), "w_out": blocks(w_out), "w_exp": w_exp,
        "pw": np.ascontiguousarray(np.moveaxis(np.asarray(conv_pw_w).reshape(L, 2, P, 256), 1, 2)),
    }
    nc = bacc.Bacc("TRN2", target_bir_lowering=False, num_devices=1)
    args = {n: nc.dram_tensor("in_" + n, v.shape, F32, kind="ExternalInput").ap() for n, v in arrays.items()}
    out = nc.dram_tensor("out_t", (P, KD, LAT), F32, kind="ExternalOutput").ap()
    program(nc, args, out)
    r = run_bass_kernel_spmd(nc, [{"in_" + n: v for n, v in arrays.items()}], core_ids=[0])
    res = np.asarray(r.results[0]["out_t"])
    return np.ascontiguousarray(np.moveaxis(res, 0, 1).reshape(D, LAT).T)[None]
```

```python
from contextlib import ExitStack
import math

import numpy as np

import concourse.bass as bass
from concourse import mybir

F32 = mybir.dt.float32
ALU = mybir.AluOpType
ACT = mybir.ActivationFunctionType
AX = mybir.AxisListType

P = 128
D = 1024
KD = D // P
LAT, CTX = 512, 256
TOK = LAT + CTX
TL, TC = LAT // P, CTX // P
LAYERS = 2
GRID_W, ROWS = 64, LAT // 64
WIN_R, WIN_C = 8, 16
TAPS = 31
HALO = TAPS // 2
HD = 64
DQ = 32
E = 16
CAP_L, CAP_C = 2 * LAT // E, 2 * CTX // E
EPS = 1e-6
RING = 4
BLK = 512
MOD_BLOCKS = 6 * D // BLK
IN_BLOCKS = 5
OUT_BLOCKS = D // BLK
PAIRS = E // 2
LAM_INIT = [0.8 - 0.6 * math.exp(-0.3 * l) for l in range(LAYERS)]
NEG = -1.0e30

SMALL = {}
_at = 0
for _name, _n in (("router", KD * E), ("b_mod", 96), ("norm1", 16), ("norm2", 16), ("taps", 2 * TAPS), ("dw_b", 2), ("ln_g", 2),
                  ("ln_b", 2), ("pw_b", 2), ("qn", 1), ("kn", 1), ("dn", 1), ("lam", 4 * DQ),
                  ("final", KD)):
    SMALL[_name] = (_at, _at + _n)
    _at += _n
SMALL_N = _at

CONST = {}
_at = 0
for _name, _n in (("ident", P), ("ones_d", P), ("ones_c", P), ("ones_h", P), ("swap32", P), ("swap16", P),
                  ("mask", GRID_W), ("iota", 64), ("j_lat", 1), ("j_ctx", 1), ("eps", 1), ("pick", 4)):
    CONST[_name] = (_at, _at + _n)
    _at += _n
CONST_N = _at

QK_AT = 0
V_AT = QK_AT + 11 * TOK
WORK_AT = V_AT + 6 * 640
ZW = TOK + 4 * HALO
ACCW = ZW - 2 * HALO
TH_AT = WORK_AT
Z_AT = TH_AT + 2 * TOK
PW_AT = Z_AT + 2 * ZW
ACC_AT = PW_AT + 2 * 256
TAB_AT = ACC_AT + max(2 * ACCW, TOK + 2 * LAT)
TA_AT = TAB_AT + 4 * LAT
TB_AT = TA_AT + TOK
BIAS_DR = 14
BT_AT = WORK_AT
EX_AT = BT_AT + 4 * BIAS_DR * GRID_W
PT_AT = EX_AT + 3 * TOK
QST_AT = PT_AT + TOK
OT_AT = QST_AT + 16 * P
UTOK_AT = 0
XE_AT = UTOK_AT + 6 * D
HE0_AT = XE_AT + 2 * KD * 192
HE1_AT = HE0_AT + KD * P
TH2_AT = HE1_AT + KD * P
YL_AT = 13056
YC_AT = YL_AT + D
SL_AT = YC_AT + D
SC_AT = SL_AT + LAT
GL_AT = SC_AT + CTX
GC_AT = GL_AT + TL * P
PBL_AT = GC_AT + TC * 64
PBC_AT = PBL_AT + 2 * LAT
PTOK_AT = PBC_AT + 2 * CTX
LG_AT = PTOK_AT + 6 * (E + 2)
AFFT_AT = LG_AT + 6 * E
WRK_AT = AFFT_AT + TOK
CUM_AT = WRK_AT + TOK
POS_AT = CUM_AT + TOK
ARENA = max(OT_AT + 6 * P, TB_AT + TOK, POS_AT + TOK)
assert EX_AT <= ACC_AT
assert TH2_AT + 8 * P <= YL_AT


def program(nc, a, out):
    ctx = ExitStack()
    with ctx:
        def sb(name, shape):
            return ctx.enter_context(nc.sbuf_tensor(name, shape, F32))

        ring = sb("ring", [P, RING, KD, BLK])
        h = sb("h", [P, KD, TOK])
        u = sb("u", [P, KD, TOK])
        arena = sb("arena", [P, ARENA])
        small = sb("small", [P, LAYERS, SMALL_N])
        const = sb("const", [P, CONST_N])
        cond = sb("cond", [P, KD, 2])
        cond_t = sb("cond_t", [P, KD, 2])
        cond_w = sb("cond_w", [P, KD, 32])
        mod = sb("mod", [P, LAYERS, 48, 2])
        gain = sb("gain", [P, 2, KD, 2])
        lam = sb("lam", [P, 4])
        qn_s = sb("qn_s", [P, 2])
        negmax = sb("negmax", [P, 16])
        sums = sb("sums", [P, 16])
        rsum = sb("rsum", [P, 16])
        top8 = sb("top8", [E, 8])
        mx6 = sb("mx6", [P, 12])
        ps = ctx.enter_context(nc.psum_tensor("ps", [P, 8, 512], F32))
        route = nc.dram_tensor("route", [E, 2, TOK], F32, kind="Internal").ap()

        def view(at, *shape, parts=P):
            n = int(np.prod(shape))
            v = arena[0:parts, at:at + n]
            if len(shape) == 2:
                v = v.rearrange("p (a b) -> p a b", b=shape[1])
            if len(shape) == 3:
                v = v.rearrange("p (a b c) -> p a b c", b=shape[1], c=shape[2])
            return v

        def sm(l, name):
            lo, hi = SMALL[name]
            return small[:, l, lo:hi]

        def cst(name, parts=P):
            lo, hi = CONST[name]
            return const[0:parts, lo:hi]

        psf = ps[:, :, :].rearrange("p b n -> p (b n)")

        def bank2(b, n=TOK):
            return psf[:, 512 * b:512 * b + n]

        qk = view(QK_AT, 11, TOK)
        val = view(V_AT, 6, 640)
        acc, th, z = view(ACC_AT, 2, ACCW), view(TH_AT, 2, TOK), view(Z_AT, 2, ZW)
        a_raw = arena[:, ACC_AT:ACC_AT + 2 * TOK].rearrange("p (a b) -> p a b", b=TOK)
        tab = view(TAB_AT, 4, LAT)
        tmp = [view(TA_AT, TOK), view(TB_AT, TOK), view(TH_AT, TOK)]
        conv_y = view(Z_AT, 2, TOK)
        hn_tmp = [tmp[0], tmp[1], view(ACC_AT, TOK)]
        rope_tmp = [view(ACC_AT + TOK + i * LAT, LAT) for i in range(2)]
        bt = view(BT_AT, 4, BIAS_DR * GRID_W)
        ex = view(EX_AT, 3, TOK)
        pt = view(PT_AT, TOK)
        qst = view(QST_AT, 16, P)
        pw = view(PW_AT, 2, 256)
        otok = view(OT_AT, TOK)
        utok = view(UTOK_AT, 6, D)
        gl, gc = view(GL_AT, TL, P), view(GC_AT, TC, 64)
        s_lat, s_ctx = view(SL_AT, LAT), view(SC_AT, CTX)
        yl, yc = view(YL_AT, D), view(YC_AT, D)
        pbl, pbc = view(PBL_AT, 2, LAT), view(PBC_AT, 2, CTX)
        ptok = view(PTOK_AT, 6, E + 2)
        rt = view(CUM_AT, 256)
        mod_tok = [view(EX_AT + i * 256, 256) for i in range(2)]
        lg = view(LG_AT, 6, E)
        afft, wrk = view(AFFT_AT, TOK, parts=E), view(WRK_AT, TOK, parts=E)
        cum, pos = view(CUM_AT, TOK, parts=E), view(POS_AT, TOK, parts=E)
        he = [view(HE0_AT, KD, P), view(HE1_AT, KD, P)]
        th2 = view(TH2_AT, 4 * P)
        h_tok = [view(TH2_AT + i * 4 * P, 4 * P) for i in range(2)]
        he64 = [view(HE0_AT, KD, 64), view(HE1_AT, KD, 64)]

        filled = [ctx.enter_context(nc.semaphore(f"filled{s}")) for s in range(RING)]
        used = [ctx.enter_context(nc.semaphore(f"used{s}")) for s in range(RING)]
        names = ("loaded x_loaded stored cond_tanh cond_done mod_mm mod_cp mod_pk mod_ev self0 gain_done lam_dot lam_exp fin_mm fin_sq "
                 "fin_root fin_rinv fin_out").split()
        sig = {n: ctx.enter_context(nc.semaphore(n)) for n in names}
        SINCE = {}
        for names_, n_ in (("n1_sq n1_mm n1_pre n1_u n2_sq n2_mm n2_pre n2_u o_mm o_ev", 8), ("t_mm t_ev", 15),
                           ("v_mm v_ev", 18), ("z_done c_sq c_lin c_tanh c_pw c_out dn_sq dn_mm dn_root dn_done", 2),
                           ("n1_root n2_root z_zero c_mean c_cent c_var c_root c_act bias_done r_mm r_cp r_exp r_aff r_tr "
                            "r_afft r_pos r_ptr q_zero c_y r_grp r_cpy", 1), ("tables layer_in", 16), ("hn_sq hn_mm hn_root hn_done", 3),
                           ("rp_mm rp_done rp_add", 7), ("bias_ld", 16), ("r_store", 32), ("ut_mm ut_ev", 12)):
            for n in names_.split():
                SINCE[n] = n_
                sig[n, 0] = sig[n, 1] = ctx.enter_context(nc.semaphore(n))

        def since(n, l):
            return l * SINCE[n]

        per_layer = "tap e_clear e_bc e_s e_g e_xmm e_xev e_gu e_tanh e_h e_dn e_y e_sc e_acc self".split()
        sig["e_ht"], sig["e_hev"] = (ctx.enter_context(nc.semaphore(n)) for n in ("e_ht", "e_hev"))
        ATTN = {"q_st": (10, 10), "s_mm": (16, 16), "s_max": (16, 16), "s_exp": (16, 16), "p_diff": (4, 4), "t_mm": (24, 12),
                "t_dve": (12, 12), "t_act": (12, 0), "o_mm": (12, 12), "o_ev": (12, 12), "y_mm": (2, 2), "y_ev": (2, 2),
                "self": (24, 20)}
        at_sem = {n: ctx.enter_context(nc.semaphore("at_" + n)) for n in ATTN}

        def attn_since(l, kind):
            done = (0, 0) if (l, kind) == (0, "lat") else (TL, 0) if kind == "ctx" else (TL, TC)
            return {n: done[0] * x + done[1] * y for n, (x, y) in ATTN.items()}

        for l in range(LAYERS):
            for n in per_layer:
                sig[n, l] = ctx.enter_context(nc.semaphore(f"{n}_{l}"))
        def parts_of(l, second=False):
            both = [(0, LAT, 0), (LAT, CTX, 1)]
            return both[:1] if (l and second) else both

        at = {"mod0a": 0}
        at["in0"] = at["mod0a"] + 4
        at["mod0b"] = at["in0"] + IN_BLOCKS
        at["out0"] = at["mod0b"] + MOD_BLOCKS - 4
        at["mod1"] = at["out0"] + OUT_BLOCKS
        at["exp0"] = at["mod1"] + MOD_BLOCKS
        at["in1"] = at["exp0"] + 6 * E
        at["out1"] = at["in1"] + IN_BLOCKS
        at["exp1"] = at["out1"] + OUT_BLOCKS

        T_TILES = [("nq", 0, 0, 0), ("nq", 0, 1, 1), ("k", 0, 2, 2), ("k", 0, 3, 3),
                   ("a", 1, 2, 0), ("a", 1, 3, 1), ("g", 2, 0, 0), ("g", 2, 1, 1),
                   ("q", 2, 2, 4), ("q", 2, 3, 5), ("k", 3, 0, 6),
                   ("dq", 3, 2, 7), ("dq", 3, 3, 8), ("k", 4, 0, 9), ("k", 4, 1, 10)]
        V_COLS = [(1, 0, 256, 0), (3, 128, 128, 256), (4, 256, 256, 384)]
        IN_ORDER = (1, 2, 0, 3, 4)

        def values(i):
            return [("v", i, t) for t in range(TL + TC)]

        P_STEPS = [("blk", 0)] + values(0) + [("t", 4), ("t", 5)]
        P_STEPS += [("blk", 1)] + [("t", i) for i in (6, 7, 8, 9)]
        P_STEPS += [("blk", 2)] + [("t", i) for i in (0, 1, 2, 3)]
        P_STEPS += [("blk", 3), ("t", 10), ("c_mean",)] + values(1)[:3] + [("c_sq",)] + values(1)[3:5] + [("c_var",)]
        P_STEPS += values(1)[5:] + [("t", 11), ("c_tanh",), ("t", 12), ("c_pw", 0)]
        P_STEPS += [("blk", 4), ("t", 13), ("c_pw", 1), ("hn_sq",), ("t", 14), values(2)[0], ("hn",)]
        P_STEPS += [x for i, v in enumerate(values(2)[1:]) for x in (v, ("rope", i))] + [("rope", 5), ("rope", 6)]

        def place(kind, i):
            return max(n for n, x in enumerate([x for x in P_STEPS if x[0] == kind]) if x[1] == i)

        def t_width(l, kind):
            return TOK if (l == 0 or kind == "k") else LAT

        HN = [(4, "q"), (5, "q"), (6, "k")]
        ROPE = [(7, "swap16", 2), (8, "swap16", 2), (9, "swap16", 2), (10, "swap16", 2),
                (4, "swap32", 0), (5, "swap32", 0), (6, "swap32", 0)]

        def kinds(l):
            return ("lat", "ctx") if l == 0 else ("lat",)

        SU = [6] * 4 + [9] * 4 + [10] * 4 + [2, 2, 3, 3]
        GROUPS = (0, 4, 12)
        NA0 = GROUPS[2]
        STAGE = [
                 [(64, 64 * r, 64 * g, slice(4 + g, 5 + g), slice(2 * g + r, 2 * g + r + 1))
                  for g in range(2) for r in range(2)],
                 [(32, 32 * r, 32 * r, slice(7, 9), slice(4 + r, 12, 4)) for r in range(4)],
                 [(64, 64 * r, 64 * r, slice(0, 2), slice(12 + r, 16, 2)) for r in range(2)]]
        STAGED = (4, 8, 10)
        last_score = [0, 1, 2, 3] + [5, 7, 9, 11] + [12, 13, 14, 15]
        v_col = [256 + 64 * (i // 2) for i in range(4)] + [384 + 64 * i for i in range(4)] + [64 * i for i in range(4)]
        DIFF = range(4, 8)
        AHEAD = 3

        def new_scores(i):
            first = last_score[i - 1] + AHEAD + 1 if i else AHEAD
            return range(first, min(last_score[i] + AHEAD + 1, 16))

        block = ctx.enter_context(nc.Block())

        @block.sync
        def _(sp):
            sp.dma_start(cond[:], a["cond"]).then_inc(sig["loaded"], 16)
            sp.dma_start(const[:], a["const"]).then_inc(sig["loaded"], 16)
            sp.dma_start(small[:], a["small"]).then_inc(sig["loaded"], 16)

            def fill(n, src):
                s = n % RING
                if n >= RING:
                    sp.wait_ge(used[s], n // RING)
                sp.dma_start(ring[:, s, :, :], src).then_inc(filled[s], 16)

            for l in range(LAYERS):
                if l == 0:
                    sp.dma_start(h[:], a["x"]).then_inc(sig["x_loaded"], 16)
                    for j in range(4):
                        fill(at["mod0a"] + j, a["w_mod"][0, j])
                for j in range(IN_BLOCKS):
                    fill(at[f"in{l}"] + j, a["w_in"][l, IN_ORDER[j]])
                if l == 0:
                    for j in range(MOD_BLOCKS - 4):
                        fill(at["mod0b"] + j, a["w_mod"][0, 4 + j])
                for j in range(OUT_BLOCKS):
                    fill(at[f"out{l}"] + j, a["w_out"][l, j])
                if l == 0:
                    for j in range(MOD_BLOCKS):
                        fill(at["mod1"] + j, a["w_mod"][1, j])
                with sp.Fori(0, PAIRS) as p:
                    for j in range(12):
                        n = at[f"exp{l}"] + j
                        s = n % RING
                        sp.wait_ge(used[s], p * 3 + n // RING)
                        sp.dma_start(ring[:, s, :, :], a["w_exp"][l, p, j]).then_inc(filled[s], 16)
            for k in range(KD):
                sp.wait_ge(sig["fin_out"], k + 1)
                sp.dma_start(out[:, k, :], u[:, k, 0:LAT]).then_inc(sig["stored"], 16)
            sp.wait_ge(sig["stored"], 16 * KD)

        @block.tensor
        def _(pe):
            def ready(n, p3=None):
                s = n % RING
                v = 16 * (n // RING + 1)
                pe.wait_ge(filled[s], v if p3 is None else p3 * 48 + v)
                return ring[:, s, :, :]

            def release(held, p3=0):
                if held:
                    n, sem, count = held
                    pe.wait_ge(sem, count)
                    pe.sem_inc(used[n % RING], 1)

            def modulation(l, j0, j1, n0):
                def pick(j):
                    pe.wait_ge(sig["mod_cp"], l * MOD_BLOCKS + j + 1)
                    for x in range(2):
                        mm = pe.matmul(ps[:, 6 + j % 2, 256 + 4 * x:260 + 4 * x], mod_tok[j % 2][:, P * x:P * x + P],
                                       cst("pick"), start=True, stop=True)
                    mm.then_inc(sig["mod_pk"], 1)

                held = None
                for j in range(j0, j1):
                    w = ready(n0 + j - j0)
                    m = l * MOD_BLOCKS + j
                    if m >= 2:
                        pe.wait_ge(sig["mod_ev"], m - 1)
                    for k in range(KD):
                        for c in range(2):
                            g = 2 * c + k % 2
                            mm = pe.matmul(ps[32 * g:32 * g + 32, 6 + j % 2, 0:256], cond_w[:, k, :],
                                           w[:, k, 256 * c:256 * c + 256], start=k < 2, stop=k >= KD - 2,
                                           tile_position=(0, 32 * g))
                    mm.then_inc(sig["mod_mm"], 1)
                    if j > j0:
                        pick(j - 1)
                    release(held)
                    held = (n0 + j - j0, sig["mod_mm"], m + 1)
                release(held)
                pick(j1 - 1)

            def norm_sum(which, l, parts, ks=range(KD)):
                for k in ks:
                    pe.wait_ge(sig[which + "_sq", l], since(which + "_sq", l) + k + 1)
                    for t0, n, c in parts:
                        mm = pe.matmul(ps[:, c, 0:n], cst("ones_d"), ex[:, k % 2, t0:t0 + n],
                                       start=k == 0, stop=k == KD - 1)
                    mm.then_inc(sig[which + "_mm", l], 1)

            pe.wait_ge(sig["loaded"], 48)
            for l in range(LAYERS):
                norm_sum("n1", l, parts_of(l))
                if l == 0:
                    pe.wait_ge(sig["cond_done"], 1)
                    modulation(0, 0, 4, at["mod0a"])
                else:
                    pe.wait_ge(sig["e_acc", 0], 8 * PAIRS)
                nt = nv = 0
                pc = parts_of(0)[:2 - l]
                held = now = None
                for step in P_STEPS:
                    what = step[0]
                    if what == "blk":
                        blk = step[1]
                        held = now
                        w = ready(at[f"in{l}"] + blk)
                        if blk == 0:
                            pe.wait_ge(sig["n1_root", l], since("n1_root", l) + 1)
                    elif what == "t":
                        kind, _, ct, _ = T_TILES[step[1]]
                        if nt >= 2:
                            pe.wait_ge(sig["t_ev", l], since("t_ev", l) + nt - 1)
                        b = 2 * (nt % 2)
                        halves = [(0, LAT, b)] + ([(LAT, CTX, b + 1)] if t_width(l, kind) > LAT else [])
                        for k in range(KD):
                            for t0, n, bb in halves:
                                mm = pe.matmul(ps[:, bb, 0:n], w[:, k, P * ct:P * ct + P], u[:, k, t0:t0 + n],
                                               start=k == 0, stop=k == KD - 1)
                        mm.then_inc(sig["t_mm", l], 1)
                        nt += 1
                        release(held)
                        held, now = None, (at[f"in{l}"] + blk, sig["t_mm", l], since("t_mm", l) + nt)
                    elif what == "v":
                        _, c0, cn, _ = V_COLS[step[1]]
                        t = step[2]
                        if nv >= 2:
                            pe.wait_ge(sig["v_ev", l], since("v_ev", l) + nv - 1)
                        for k in range(KD):
                            if nv == 0:
                                pe.wait_ge(sig["n1_u", l], since("n1_u", l) + k + 1)
                            mm = pe.matmul(ps[:, 4 + nv % 2, 0:cn], u[:, k, P * t:P * t + P],
                                           w[:, k, c0:c0 + cn], start=k == 0, stop=k == KD - 1)
                        mm.then_inc(sig["v_mm", l], 1)
                        nv += 1
                        release(held)
                        held, now = None, (at[f"in{l}"] + blk, sig["v_mm", l], since("v_mm", l) + nv)
                    elif what == "c_mean":
                        pe.wait_ge(sig["tap", l], 2 * TAPS)
                        for j in range(2):
                            for t0, n, c in pc:
                                s0 = t0 + (2 * HALO if c else 0)
                                mm = pe.matmul(ps[:, 6 + c, 0:n], cst("ones_c"), acc[:, j, s0:s0 + n],
                                               start=j == 0, stop=j == 1)
                        mm.then_inc(sig["c_mean", l], 1)
                    elif what == "c_var":
                        pe.wait_ge(sig["c_sq", l], since("c_sq", l) + 2)
                        for j in range(2):
                            for t0, n, c in pc:
                                mm = pe.matmul(ps[:, 6 + c, 0:n], cst("ones_c"), tmp[j][:, t0:t0 + n],
                                               start=j == 0, stop=j == 1)
                        mm.then_inc(sig["c_var", l], 1)
                    elif what == "c_pw":
                        co = step[1]
                        if co == 0:
                            pe.wait_ge(sig["c_act", l], since("c_act", l) + 1)
                            pe.wait_ge(sig["layer_in", l], since("layer_in", l) + 16)
                        else:
                            pe.wait_ge(sig["c_out", l], since("c_out", l) + 1)
                        for t0, n, c in pc:
                            s0 = t0 + (2 * HALO if c else 0)
                            for ci in range(2):
                                mm = pe.matmul(ps[:, 6 + c, 0:n], pw[:, ci, P * co:P * co + P], acc[:, ci, s0:s0 + n],
                                               start=ci == 0, stop=ci == 1)
                        mm.then_inc(sig["c_pw", l], 1)
                    elif what == "hn":
                        pe.wait_ge(sig["t_ev", l], since("t_ev", l) + len(T_TILES))
                        pe.wait_ge(sig["c_out", l], since("c_out", l) + 2)
                        for i, (tile, g) in enumerate(HN):
                            pe.wait_ge(sig["hn_sq", l], since("hn_sq", l) + i + 1)
                            wd = t_width(l, g)
                            for t0, n, c in parts_of(0)[:1 if wd == LAT else 2]:
                                mm = pe.matmul(ps[:, (0, 2, 6)[i] + c, 0:n], cst("ones_h"), hn_tmp[i][:, t0:t0 + n],
                                               start=True, stop=True)
                            mm.then_inc(sig["hn_mm", l], 1)
                    elif what == "rope":
                        i = step[1]
                        tile, perm, _ = ROPE[i]
                        if i < 2:
                            pe.wait_ge(sig["hn_root", l], since("hn_root", l) + i + 1)
                        else:
                            pe.wait_ge(sig["rp_done", l], since("rp_done", l) + i - 1)
                        if i >= 4:
                            pe.wait_ge(sig["hn_done", l], since("hn_done", l) + i - 3)
                        pe.matmul(ps[:, 2 * (i % 2), :], cst(perm), qk[:, tile, 0:LAT], start=True,
                                  stop=True).then_inc(sig["rp_mm", l], 1)
                release(now)
                pe.wait_ge(sig["hn_root", l], since("hn_root", l) + 3)
                pe.wait_ge(sig["v_ev", l], since("v_ev", l) + nv)
                if l == 0:
                    modulation(0, 4, MOD_BLOCKS, at["mod0b"])
                pe.wait_ge(sig["rp_add", l], since("rp_add", l) + 7)
                if l == 0:
                    pe.wait_ge(sig["mod_ev"], MOD_BLOCKS)
                for kind in kinds(l):
                    s, s0 = at_sem, attn_since(l, kind)
                    lat = kind == "lat"
                    k0, kn, trips = (0, TOK, TL) if lat else (LAT, CTX, TC)
                    ktiles = range(k0 // P, (k0 + kn) // P)
                    cuts = [(0, LAT, 0), (LAT, CTX, 1)] if lat else [(LAT, CTX, 0)]

                    def outputs_transposed(it):
                        pe.wait_ge(s["o_ev"], s0["o_ev"] + it * 12 + 12)
                        for x in range(6):
                            mm = pe.transpose(ps[:, 6 + x // 4, P * (x % 4):P * (x % 4) + P],
                                              otok[:, P * x:P * x + P], cst("ident"))
                            if x in (3, 5):
                                mm.then_inc(s["y_mm"], 1)

                    def tile(it, first):
                        def scores(j):
                            if j in GROUPS:
                                pe.wait_ge(s["q_st"], it * 10 + (s0["q_st"] + STAGED[GROUPS.index(j)]))
                            for t0, n, c in cuts:
                                mm = pe.matmul(ps[:, 2 * (j % AHEAD) + c, 0:n], qst[:, j, :], qk[:, SU[j], t0:t0 + n],
                                               start=True, stop=True)
                            mm.then_inc(s["s_mm"], 1)

                        for j in range(AHEAD):
                            scores(j)
                        if not first:
                            outputs_transposed(it - 1)
                        for i in range(12):
                            if i in DIFF:
                                pe.wait_ge(s["p_diff"], it * 4 + (s0["p_diff"] + i - 3))
                            else:
                                pe.wait_ge(s["s_exp"], it * 16 + (s0["s_exp"] + last_score[i] + 1))
                            src = ex[:, last_score[i] % AHEAD, :]
                            if i:
                                pe.wait_ge(s["t_dve"], it * 12 + (s0["t_dve"] + i))
                                if lat:
                                    pe.wait_ge(s["t_act"], it * 12 + (s0["t_act"] + i))
                            elif not first:
                                pe.wait_ge(s["y_ev"], it * 2 + s0["y_ev"])
                            for x, kt in enumerate(ktiles):
                                if i and x == 4:
                                    pe.wait_ge(s["o_ev"], it * 12 + (s0["o_ev"] + i))
                                mm = pe.transpose(ps[:, 6 + x // 4, P * (x % 4):P * (x % 4) + P],
                                                  src[:, P * x:P * x + P], cst("ident"))
                                if x in (3, len(ktiles) - 1):
                                    mm.then_inc(s["t_mm"], 1)
                            new = new_scores(i)
                            for j in new[:1]:
                                scores(j)
                            pe.wait_ge(s["t_dve"], it * 12 + (s0["t_dve"] + i + 1))
                            if lat:
                                pe.wait_ge(s["t_act"], it * 12 + (s0["t_act"] + i + 1))
                            if i and not lat:
                                pe.wait_ge(s["o_ev"], it * 12 + (s0["o_ev"] + i))
                            v0 = v_col[i] - (HD if i % 2 else 0)
                            for x, kt in enumerate(ktiles):
                                mm = pe.matmul(ps[:, 7, 0:P], pt[:, P * x:P * x + P], val[:, kt, v0:v0 + P],
                                               start=x == 0, stop=x == len(ktiles) - 1)
                            mm.then_inc(s["o_mm"], 1)
                            for j in new[1:]:
                                scores(j)

                    tile(0, True)
                    with pe.Fori(1, trips) as it:
                        tile(it, False)
                    outputs_transposed(trips - 1)
                    pe.wait_ge(s["y_ev"], s0["y_ev"] + 2 * trips)
                wp = parts_of(0)[:2 - l]
                for i in range(2):
                    pe.wait_ge(sig["dn_sq", l], since("dn_sq", l) + i + 1)
                    for t0, n, c in wp:
                        mm = pe.matmul(ps[:, 2 * i + c, 0:n], cst("ones_h"), ex[:, i, t0:t0 + n], start=True, stop=True)
                    mm.then_inc(sig["dn_mm", l], 1)
                pe.wait_ge(sig["dn_done", l], since("dn_done", l) + 2)
                pe.wait_ge(sig["c_y", l], since("c_y", l) + 1)
                held = None
                for blk in range(OUT_BLOCKS):
                    w = ready(at[f"out{l}"] + blk)
                    for ct in range(4):
                        i = 4 * blk + ct
                        if i >= 2:
                            pe.wait_ge(sig["o_ev", l], since("o_ev", l) + i - 1)
                        for k in range(KD):
                            for t0, n, c in wp:
                                mm = pe.matmul(ps[:, 4 + 2 * (i % 2) + c, 0:n], w[:, k, P * ct:P * ct + P],
                                               u[:, k, t0:t0 + n], start=k == 0, stop=k == KD - 1)
                        mm.then_inc(sig["o_mm", l], 1)
                        release(held)
                        held = None
                        if i >= 2:
                            norm_sum("n2", l, wp, [i - 2])
                    held = (at[f"out{l}"] + blk, sig["o_mm", l], since("o_mm", l) + 4 * blk + 4)
                release(held)
                norm_sum("n2", l, wp, [KD - 2, KD - 1])
                nt = TL + (TC if l == 0 else 0)
                wr = small[:, l, SMALL["router"][0]:SMALL["b_mod"][1]]
                for k in range(KD):
                    pe.wait_ge(sig["n2_u", l], since("n2_u", l) + k + 1)
                    for g in range(nt // 2):
                        mm = pe.matmul(ps[32 * g:32 * g + 32, 2, 0:256], wr[:, E * k:E * k + 32],
                                       u[:, k, 256 * g:256 * g + 256], start=k == 0, stop=k == KD - 1,
                                       tile_position=(0, 32 * g))
                mm.then_inc(sig["r_grp", l], 1)
                pe.wait_ge(sig["r_cpy", l], since("r_cpy", l) + 1)
                for x in range(2):
                    mm = pe.transpose(ps[:, 3, P * x:P * x + 16 * nt], rt[0:16 * nt, P * x:P * x + P],
                                      cst("ident", 16 * nt)[:, 0:16 * nt])
                mm.then_inc(sig["r_mm", l], 1)
                pe.wait_ge(sig["o_ev", l], since("o_ev", l) + 8)
                for x in range(2 * nt):
                    if x >= 2:
                        pe.wait_ge(sig["ut_ev", l], since("ut_ev", l) + x - 1)
                    for y in range(4):
                        mm = pe.transpose(ps[:, 4 + x % 2, P * y:P * y + P],
                                          u[:, 4 * (x % 2) + y, P * (x // 2):P * (x // 2) + P], cst("ident"))
                    mm.then_inc(sig["ut_mm", l], 1)
                pe.wait_ge(sig["r_aff", l], since("r_aff", l) + 1)
                for t in range(nt):
                    mm = pe.transpose(ps[0:E, t // 4, P * (t % 4):P * (t % 4) + P], lg[:, t, :], cst("ident"))
                mm.then_inc(sig["r_tr", l], 1)
                if l == 0:
                    modulation(1, 0, MOD_BLOCKS, at["mod1"])
                pe.wait_ge(sig["r_pos", l], since("r_pos", l) + 1)
                for t in range(nt):
                    mm = pe.transpose(ps[:, 3, E * t:E * t + E], pos[:, P * t:P * t + P], cst("ident", E)[:, 0:E])
                mm.then_inc(sig["r_ptr", l], 1)
                both = l == 0
                XW = 192 if both else P
                pe.wait_ge(sig["ut_ev", l], since("ut_ev", l) + 2 * nt)
                pe.wait_ge(sig["mod_ev"], 2 * MOD_BLOCKS)
                xe = [view(XE_AT + i * KD * 192, KD, XW) for i in range(2)]

                def gather(buf, cnt):
                    pe.wait_ge(sig["e_g", l], cnt * 1 + 1)
                    for dt in range(KD):
                        pe.wait_ge(sig["e_xev", l], cnt * 8 + max(dt - 1, 0))
                        b = 6 + dt % 2
                        if both:
                            lo = ps[:, b, 0:XW].rearrange("p (x y) -> p x y", y=64)[:, 0:3:2, :]
                        else:
                            lo = ps[:, b, 0:XW]
                        for t in range(TL):
                            mm = pe.matmul(lo, utok[:, t, P * dt:P * dt + P], gl[:, t, :], start=t == 0, stop=t == TL - 1)
                        if both:
                            for t in range(TC):
                                mm = pe.matmul(ps[:, b, 64:128], utok[:, TL + t, P * dt:P * dt + P], gc[:, t, :],
                                               start=t == 0, stop=t == TC - 1)
                        mm.then_inc(sig["e_xmm", l], 1)

                pe.wait_ge(sig["e_clear", l], 1)
                gather(0, 0)
                with pe.Fori(0, PAIRS // 2) as pp:
                    for half_p in range(2):
                        buf = half_p
                        pe.wait_ge(sig["e_xev", l], pp * 16 + (half_p + 1) * 8)
                        n0 = at[f"exp{l}"] + 12 * half_p
                        held = None
                        if not both:
                            for x, step in enumerate(["gu"] * 7 + ["ht", "gu", "dn", "ht", "dn", "dn", "dn"]):
                                if step == "gu":
                                    x -= x > 7
                                    e, half, gu = x // 4, x // 2 % 2, x % 2
                                    n = n0 + x
                                    w = ready(n, pp * 2)
                                    b = 2 * e + gu
                                    if half == 0:
                                        pe.wait_ge(sig["e_h", l], pp * 4 + (2 * half_p + e - 1 if half_p else 0))
                                        pe.wait_ge(sig["e_hev"], pp * 4 + (2 * half_p + e - 1 if half_p else 0))
                                    for k in range(KD):
                                        for c in range(2):
                                            mm = pe.matmul(ps[64 * c:64 * c + 64, b, 256 * half:256 * half + 256],
                                                           xe[buf][:, k, 64 * e:64 * e + 64], w[:, k, 256 * c:256 * c + 256],
                                                           start=k == 0, stop=k == KD - 1)
                                        if k == 1:
                                            release(held)
                                    mm.then_inc(sig["e_gu", l], 1)
                                    held = (n, sig["e_gu", l], pp * 16 + 8 * half_p + x + 1)
                                elif step == "ht":
                                    e = int(x > 7)
                                    pe.wait_ge(sig["e_h", l], pp * 4 + 2 * half_p + e + 1)
                                    for q in range(4):
                                        mm = pe.transpose(ps[:, 2 * e, P * q:P * q + P], h_tok[e][:, P * q:P * q + P],
                                                          cst("ident"))
                                    mm.then_inc(sig["e_ht"], 1)
                                else:
                                    y = {9: 0, 11: 1, 12: 2, 13: 3}[x]
                                    e, dh = y // 2, y % 2
                                    n = n0 + 8 + y
                                    w = ready(n, pp * 2)
                                    pe.wait_ge(sig["e_hev"], pp * 4 + 2 * half_p + e + 1)
                                    pe.wait_ge(sig["e_y", l], pp * 8 + max(4 * half_p + y - 1, 0))
                                    for k in range(KD):
                                        for c in range(2):
                                            mm = pe.matmul(ps[64 * c:64 * c + 64, 4 + dh, 0:256], he64[e][:, k, :],
                                                           w[:, k, 256 * c:256 * c + 256], start=k == 0, stop=k == KD - 1)
                                        if k == 1:
                                            release(held)
                                    mm.then_inc(sig["e_dn", l], 1)
                                    held = (n, sig["e_dn", l], pp * 8 + 4 * half_p + y + 1)
                        else:
                            for e in range(2):
                                x0 = 64 * e
                                for half in range(2):
                                    for gu in range(2):
                                        n = n0 + 4 * e + 2 * half + gu
                                        w = ready(n, pp * 2)
                                        b = 2 * half + gu
                                        pe.wait_ge(sig["e_h", l], pp * 8 + max(4 * half_p + 2 * e + half - 1, 0))
                                        if e == 0 and half:
                                            pe.wait_ge(sig["e_acc", l], pp * 16 + half_p * 8)
                                        for f in range(4):
                                            for k in range(KD):
                                                mm = pe.matmul(ps[:, b, P * f:P * f + P], w[:, k, P * f:P * f + P],
                                                               xe[buf][:, k, x0:x0 + P], start=k == 0, stop=k == KD - 1)
                                            if f == 0:
                                                release(held)
                                        mm.then_inc(sig["e_gu", l], 1)
                                        held = (n, sig["e_gu", l], pp * 16 + 8 * half_p + 4 * e + 2 * half + gu + 1)
                            for e in range(2):
                                pe.wait_ge(sig["e_h", l], pp * 8 + 4 * half_p + 2 * e + 2)
                                for dh in range(2):
                                    n = n0 + 8 + 2 * e + dh
                                    w = ready(n, pp * 2)
                                    pe.wait_ge(sig["e_y", l], pp * 8 + max(4 * half_p + 2 * e + dh - 1, 0))
                                    for k in range(KD):
                                        mm = pe.matmul(ps[:, 4 + dh, :], he[e][:, k, :], w[:, k, :],
                                                       start=k == 0, stop=k == KD - 1)
                                        if k == 1:
                                            release(held)
                                    mm.then_inc(sig["e_dn", l], 1)
                                    held = (n, sig["e_dn", l], pp * 8 + 4 * half_p + 2 * e + dh + 1)
                        pe.wait_ge(sig["e_acc", l], (pp * 2 + half_p) * 8)
                        gather(1 - buf, pp * 2 + half_p + 1)
                        release(held)
                        pe.wait_ge(sig["e_s", l], pp * 2 + half_p + 1)
                        pe.wait_ge(sig["e_y", l], pp * 8 + 4 * half_p + 4)
                        pe.wait_ge(sig["e_xev", l], (pp * 2 + half_p + 2) * 8)
                        for dt in range(KD):
                            if both:
                                pe.wait_ge(sig["e_acc", l], pp * 16 + half_p * 8 + max(dt - 1, 0))
                                pe.matmul(ps[:, 2 + dt % 2, 0:CTX], yc[:, P * dt:P * dt + P], s_ctx, start=True, stop=True)
                            else:
                                pe.wait_ge(sig["e_acc", l], pp * 16 + half_p * 8 + max(dt - 1, 0))
                            pe.matmul(ps[:, 6 + dt % 2, :], yl[:, P * dt:P * dt + P], s_lat, start=True,
                                      stop=True).then_inc(sig["e_sc", l], 1)
            for k in range(KD):
                pe.wait_ge(sig["fin_sq"], k + 1)
                pe.matmul(ps[:, 0, :], cst("ones_d"), ex[:, k % 2, 0:LAT], start=k == 0,
                          stop=k == KD - 1).then_inc(sig["fin_mm"], 1)

        @block.scalar
        def _(act):
            act.wait_ge(sig["loaded"], 48)
            act.activation(cond_t[:], cond[:], ACT.Tanh, scale=0.5).then_inc(sig["cond_tanh"], 1)

            def norm(which, l, parts):
                for k in range(KD):
                    if k >= 2:
                        act.wait_ge(sig[which + "_mm", l], since(which + "_mm", l) + k - 1)
                    if which == "n2":
                        act.wait_ge(sig["o_ev", l], since("o_ev", l) + k + 1)
                    elif l:
                        act.wait_ge(sig["e_acc", l - 1], 8 * (PAIRS - 1) + k + 1)
                    t1 = parts[-1][0] + parts[-1][1]
                    act.activation(ex[:, k % 2, 0:t1], h[:, k, 0:t1], ACT.Square).then_inc(sig[which + "_sq", l], 1)
                act.wait_ge(sig[which + "_mm", l], since(which + "_mm", l) + KD)
                act.activation(ex[:, 2, 0:t1], bank2(0, t1), ACT.Sqrt, bias=cst("eps")).then_inc(sig[which + "_root", l], 1)
                sh = 0 if which == "n1" else 24
                for k in range(KD):
                    act.wait_ge(sig[which + "_pre", l], since(which + "_pre", l) + k + 1)
                    for t0, n, c in parts:
                        last = act.activation(u[:, k, t0:t0 + n], u[:, k, t0:t0 + n], ACT.Identity,
                                              bias=mod[:, l, sh + k, c:c + 1])
                    last.then_inc(sig[which + "_u", l], 1)

            for l in range(LAYERS):
                if l == 0:
                    act.wait_ge(sig["x_loaded"], 16)
                    act.wait_ge(sig["lam_dot"], 2 * LAYERS)
                    act.activation(lam[:, 0:4], lam[:, 0:4], ACT.Exp).then_inc(sig["lam_exp"], 1)
                norm("n1", l, parts_of(l))
                act.wait_ge(sig["n1_u", l], since("n1_u", l) + KD)
                nt = nv = 0
                pc = parts_of(0)[:2 - l]
                wc = pc[-1][0] + pc[-1][1]
                for step in P_STEPS:
                    what = step[0]
                    if what == "t":
                        kind, _, _, dst = T_TILES[step[1]]
                        wd = t_width(l, kind)
                        src = bank2(2 * (nt % 2), wd)
                        act.wait_ge(sig["t_mm", l], since("t_mm", l) + nt + 1)
                        if kind == "g":
                            last = act.activation(th[:, dst, 0:wd], src, ACT.Tanh, scale=0.5)
                        elif kind == "a":
                            last = act.activation(a_raw[:, dst, 0:wd], src, ACT.Copy, scale=0.5)
                        else:
                            scale = {"nq": HD ** -0.5, "dq": DQ ** -0.5}.get(kind, 1.0)
                            last = act.activation(qk[:, dst, 0:wd], src, ACT.Copy, scale=scale)
                        last.then_inc(sig["t_ev", l], 1)
                        nt += 1
                    elif what == "v":
                        _, _, cn, v0 = V_COLS[step[1]]
                        act.wait_ge(sig["v_mm", l], since("v_mm", l) + nv + 1)
                        act.activation(val[:, step[2], v0:v0 + cn], ps[:, 4 + nv % 2, 0:cn],
                                       ACT.Copy).then_inc(sig["v_ev", l], 1)
                        nv += 1
                    elif what == "c_sq":
                        act.wait_ge(sig["c_cent", l], since("c_cent", l) + 1)
                        for j in range(2):
                            for t0, n, c in pc:
                                s0 = t0 + (2 * HALO if c else 0)
                                last = act.activation(tmp[j][:, t0:t0 + n], acc[:, j, s0:s0 + n], ACT.Square)
                            last.then_inc(sig["c_sq", l], 1)
                    elif what == "c_var":
                        act.wait_ge(sig["c_var", l], since("c_var", l) + 1)
                        act.activation(tmp[2][:, 0:wc], bank2(6, wc), ACT.Sqrt,
                                       bias=cst("eps")).then_inc(sig["c_root", l], 1)
                    elif what == "c_tanh":
                        for j in range(2):
                            act.wait_ge(sig["c_lin", l], since("c_lin", l) + j + 1)
                            for t0, n, c in pc:
                                s0 = t0 + (2 * HALO if c else 0)
                                last = act.activation(tmp[j][:, t0:t0 + n], acc[:, j, s0:s0 + n], ACT.Tanh, scale=0.5)
                            last.then_inc(sig["c_tanh", l], 1)
                    elif what == "c_pw":
                        co = step[1]
                        act.wait_ge(sig["c_pw", l], since("c_pw", l) + co + 1)
                        act.activation(conv_y[:, co, 0:wc], bank2(6, wc), ACT.Identity, scale=0.5,
                                       bias=sm(l, "pw_b")[:, co:co + 1]).then_inc(sig["c_out", l], 1)
                    elif what == "hn_sq":
                        for i, (tile, g) in enumerate(HN):
                            wd = t_width(l, g)
                            act.activation(hn_tmp[i][:, 0:wd], qk[:, tile, 0:wd], ACT.Square).then_inc(sig["hn_sq", l], 1)
                    elif what == "hn":
                        for i, (tile, g) in enumerate(HN):
                            wd = t_width(l, g)
                            act.wait_ge(sig["hn_mm", l], since("hn_mm", l) + i + 1)
                            act.activation(hn_tmp[i][:, 0:wd], bank2((0, 2, 6)[i], wd), ACT.Sqrt,
                                           bias=cst("eps")).then_inc(sig["hn_root", l], 1)
                act.wait_ge(sig["v_mm", l], since("v_mm", l) + nv)
                act.activation(u[:, 2:4, 0:wc], conv_y[:, :, 0:wc], ACT.Copy).then_inc(sig["c_y", l], 1)
                for kind in kinds(l):
                    s, s0 = at_sem, attn_since(l, kind)
                    lat = kind == "lat"
                    k0, kn, trips = (0, TOK, TL) if lat else (LAT, CTX, TC)

                    def outputs(it):
                        base = it * P + k0
                        act.wait_ge(s["y_mm"], it * 2 + (s0["y_mm"] + 1))
                        act.activation(u[:, 4:8, bass.ds(base, P)], ps[:, 6, :].rearrange("p (a b) -> p a b", b=P),
                                       ACT.Copy).then_inc(s["y_ev"], 1)
                        act.wait_ge(s["y_mm"], it * 2 + (s0["y_mm"] + 2))
                        act.activation(u[:, 0:2, bass.ds(base, P)], ps[:, 7, 0:CTX].rearrange("p (a b) -> p a b", b=P),
                                       ACT.Copy).then_inc(s["y_ev"], 1)

                    def tile(it, first):
                        def exp(j):
                            act.wait_ge(s["s_max"], it * 16 + (s0["s_max"] + j + 1))
                            src = ex[:, j % AHEAD, 0:kn] if (lat and j >= NA0) else bank2(2 * (j % AHEAD), kn)
                            act.activation(ex[:, j % AHEAD, 0:kn], src, ACT.Exp, bias=negmax[:, j:j + 1],
                                           accum_out=sums[:, j:j + 1]).then_inc(s["s_exp"], 1)

                        exp(0)
                        if not first:
                            outputs(it - 1)
                        for j in range(1, AHEAD):
                            exp(j)
                        for i in range(12):
                            if lat:
                                act.wait_ge(s["t_mm"], it * 24 + (s0["t_mm"] + 2 * i + 2))
                                act.activation(pt[:, LAT:TOK], ps[:, 7, 0:CTX], ACT.Copy).then_inc(s["t_act"], 1)
                            for j in new_scores(i):
                                exp(j)

                    tile(0, True)
                    with act.Fori(1, trips) as it:
                        tile(it, False)
                    outputs(trips - 1)
                    act.wait_ge(s["y_ev"], s0["y_ev"] + 2 * trips)
                wc = TOK if l == 0 else LAT
                for i in range(2):
                    act.activation(ex[:, i, 0:wc], u[:, 6 + i, 0:wc], ACT.Square).then_inc(sig["dn_sq", l], 1)
                for i in range(2):
                    act.wait_ge(sig["dn_mm", l], since("dn_mm", l) + i + 1)
                    act.activation(ex[:, i, 0:wc], bank2(2 * i, wc), ACT.Sqrt, bias=cst("eps")).then_inc(sig["dn_root", l], 1)
                act.wait_ge(sig["dn_done", l], since("dn_done", l) + 2)
                norm("n2", l, parts_of(l, True))
                nt = TL + (TC if l == 0 else 0)
                act.wait_ge(sig["r_cp", l], since("r_cp", l) + 1)
                act.activation(lg[:, 0:nt, :], lg[:, 0:nt, :], ACT.Exp).then_inc(sig["r_exp", l], 1)
                for x in range(2 * nt):
                    act.wait_ge(sig["ut_mm", l], since("ut_mm", l) + x + 1)
                    act.activation(utok[:, x // 2, 512 * (x % 2):512 * (x % 2) + 512], ps[:, 4 + x % 2, :],
                                   ACT.Copy).then_inc(sig["ut_ev", l], 1)
                act.wait_ge(sig["r_tr", l], since("r_tr", l) + 1)
                act.activation(afft[:, 0:P * nt], psf[0:E, 0:P * nt], ACT.Copy, scale=0.5).then_inc(sig["r_afft", l], 1)
                both = l == 0
                XW = 192 if both else P
                xe = [view(XE_AT + i * KD * 192, KD, XW) for i in range(2)]

                def take_gather(buf, cnt):
                    for dt in range(KD):
                        act.wait_ge(sig["e_xmm", l], cnt * 8 + dt + 1)
                        act.activation(xe[buf][:, dt, :], ps[:, 6 + dt % 2, 0:XW], ACT.Copy).then_inc(sig["e_xev", l], 1)

                act.wait_ge(sig["ut_ev", l], since("ut_ev", l) + 2 * nt)
                take_gather(0, 0)
                with act.Fori(0, PAIRS // 2) as pp:
                    for half_p in range(2):
                        def tanh(e, half):
                            if both:
                                act.wait_ge(sig["e_gu", l], pp * 16 + 8 * half_p + 4 * e + 2 * half + 1)
                                act.wait_ge(sig["e_h", l], pp * 8 + 4 * half_p + 2 * e + half)
                                act.activation(th2, ps[:, 2 * half, :], ACT.Tanh, scale=0.5).then_inc(sig["e_tanh", l], 1)
                            else:
                                act.wait_ge(sig["e_gu", l], pp * 16 + 8 * half_p + 4 * e + 3)
                                act.activation(h_tok[e], ps[:, 2 * e, :], ACT.Tanh, scale=0.5).then_inc(sig["e_tanh", l], 1)

                        def h_transposed(e):
                            act.wait_ge(sig["e_ht"], pp * 4 + 2 * half_p + e + 1)
                            for c in range(2):
                                dst = he64[e].rearrange("p (b c q) t -> p b c q t", b=2, c=2)[:, :, c, :, :]
                                src = ps[:, 2 * e, :].rearrange("p (b q c t) -> p b q c t", b=2, q=2, c=2)[:, :, :, c, :]
                                last = act.activation(dst, src, ACT.Copy)
                            last.then_inc(sig["e_hev"], 1)

                        def take_y(e, dh):
                            act.wait_ge(sig["e_dn", l], pp * 8 + 4 * half_p + 2 * e + dh + 1)
                            act.wait_ge(sig["e_sc", l], pp * 16 + 8 * half_p)
                            rows = slice(64 * e, 64 * e + 64)
                            if both:
                                act.activation(yl[rows, 512 * dh:512 * dh + 512], ps[rows, 4 + dh, :], ACT.Copy)
                                rows = slice(32 + 32 * (1 - e), 64 + 32 * (1 - e))
                                last = act.activation(yc[rows, 512 * dh:512 * dh + 512], ps[rows, 4 + dh, :], ACT.Copy)
                            else:
                                for c in range(2):
                                    c0 = 512 * dh + 256 * c
                                    last = act.activation(yl[rows, c0:c0 + 256], ps[64 * c:64 * c + 64, 4 + dh, 0:256],
                                                          ACT.Copy)
                            last.then_inc(sig["e_y", l], 1)

                        if both:
                            for x in range(4):
                                tanh(x // 2, x % 2)
                            for x in range(4):
                                take_y(x // 2, x % 2)
                        else:
                            tanh(0, 0)
                            h_transposed(0)
                            tanh(1, 0)
                            take_y(0, 0)
                            h_transposed(1)
                            for x in range(1, 4):
                                take_y(x // 2, x % 2)
                        take_gather(1 - half_p, pp * 2 + half_p + 1)
            for k in range(KD):
                act.wait_ge(sig["e_acc", LAYERS - 1], 8 * (PAIRS - 1) + k + 1)
                if k >= 2:
                    act.wait_ge(sig["fin_mm"], k - 1)
                act.activation(ex[:, k % 2, 0:LAT], h[:, k, 0:LAT], ACT.Square).then_inc(sig["fin_sq"], 1)
            act.wait_ge(sig["fin_mm"], KD)
            act.activation(ex[:, 2, 0:LAT], ps[:, 0, :], ACT.Sqrt, bias=cst("eps")).then_inc(sig["fin_root"], 1)

        @block.vector
        def _(dve):
            selfs = {}

            def link(ins, key):
                selfs[key] = selfs.get(key, 0) + 1
                ins.then_inc(sig[key], 1)
                dve.wait_ge(sig[key], selfs[key])

            dve.wait_ge(sig["loaded"], 48)
            for l in range(LAYERS):
                lv = sm(l, "lam").rearrange("p (a b) -> p a b", b=DQ)
                for i in range(2):
                    dve.tensor_tensor_reduce(ex[:, i, 0:DQ], lv[:, 2 * i, :], lv[:, 2 * i + 1, :], 1.0, 0.0, ALU.mult,
                                             ALU.add, lam[:, 2 * l + i:2 * l + i + 1]).then_inc(sig["lam_dot"], 1)
                    dve.wait_ge(sig["lam_dot"], 2 * l + i + 1)
            dve.wait_ge(sig["cond_tanh"], 1)
            link(dve.scalar_tensor_tensor(cond[:], cond_t[:], 1.0, cond[:], ALU.add, ALU.mult), "self0")
            link(dve.tensor_scalar(cond[:], cond[:], 0.5, None, ALU.mult), "self0")
            dve.tensor_copy(cond_w[:, :, :].rearrange("p k (r c) -> p k r c", c=2),
                            cond[:].unsqueeze(2).to_broadcast([P, KD, 16, 2])).then_inc(sig["cond_done"], 1)
            dve.wait_ge(sig["lam_exp"], 1)
            for l in range(LAYERS):
                link(dve.tensor_tensor(lam[:, 2 * l:2 * l + 1], lam[:, 2 * l + 1:2 * l + 2], lam[:, 2 * l:2 * l + 1],
                                       ALU.subtract), "self0")
                link(dve.tensor_scalar(lam[:, 2 * l:2 * l + 1], lam[:, 2 * l:2 * l + 1], -LAM_INIT[l], None, ALU.add), "self0")

            def modulation(l, j0, j1):
                bm = sm(l, "b_mod").rearrange("p (b c) -> p b c", c=2)
                for j in range(j0, j1):
                    dve.wait_ge(sig["mod_mm"], l * MOD_BLOCKS + j + 1)
                    dve.tensor_copy(mod_tok[j % 2], ps[:, 6 + j % 2, 0:256]).then_inc(sig["mod_cp"], 1)
                    dve.wait_ge(sig["mod_pk"], l * MOD_BLOCKS + j + 1)
                    dve.tensor_tensor(mod[:, l, 4 * j:4 * j + 4, :].rearrange("p (c x) d -> p x c d", x=2),
                                      ps[:, 6 + j % 2, 256:264].rearrange("p (x c d) -> p x c d", x=2, c=2),
                                      bm[:, 4 * j:4 * j + 4, :].rearrange("p (c x) d -> p x c d", x=2),
                                      ALU.add).then_inc(sig["mod_ev"], 1)

            def make_gain(l, i):
                g = sm(l, ("norm1", "norm2")[i]).rearrange("p (k c) -> p k c", c=2)
                dve.scalar_tensor_tensor(gain[:, i, :, :], mod[:, l, 24 * i + 8:24 * i + 16, :], 1.0, g, ALU.add,
                                         ALU.mult).then_inc(sig["gain_done"], 1)
                dve.wait_ge(sig["gain_done"], 2 * l + i + 1)

            def norm(which, l, parts):
                t1 = parts[-1][0] + parts[-1][1]
                dve.wait_ge(sig[which + "_root", l], since(which + "_root", l) + 1)
                link(dve.reciprocal(ex[:, 2, 0:t1], ex[:, 2, 0:t1]), ("self", l))
                i = 0 if which == "n1" else 1
                for k in range(KD):
                    for t0, n, c in parts:
                        last = dve.scalar_tensor_tensor(u[:, k, t0:t0 + n], h[:, k, t0:t0 + n], gain[:, i, k, c:c + 1],
                                                        ex[:, 2, t0:t0 + n], ALU.mult, ALU.mult)
                    last.then_inc(sig[which + "_pre", l], 1)

            for l in range(LAYERS):
                me = ("self", l)
                if l == 0:
                    modulation(0, 0, 4)
                    dve.wait_ge(sig["mod_ev"], 4)
                make_gain(l, 0)
                if l:
                    make_gain(l, 1)
                norm("n1", l, parts_of(l))
                link(dve.tensor_scalar(qn_s[:, 0:1], sm(l, "qn"), HD ** -0.5, None, ALU.mult), me)
                link(dve.tensor_scalar(qn_s[:, 1:2], sm(l, "dn"), 1.0 - LAM_INIT[l], None, ALU.mult), me)
                pc = parts_of(0)[:2 - l]
                dve.wait_ge(sig["z_zero", l], since("z_zero", l) + 1)
                for j in range(2):
                    dve.wait_ge(sig["t_ev", l], since("t_ev", l) + place("t", 6 + j) + 1)
                    for t0, n, c in pc:
                        z0 = t0 + HALO + (2 * HALO if c else 0)
                        last = dve.scalar_tensor_tensor(z[:, j, z0:z0 + n], th[:, j, t0:t0 + n], 1.0, a_raw[:, j, t0:t0 + n],
                                                        ALU.add, ALU.mult)
                    last.then_inc(sig["z_done", l], 1)
                n = ACCW if l == 0 else LAT
                taps = sm(l, "taps").rearrange("p (j t) -> p j t", t=TAPS)
                dve.wait_ge(sig["z_done", l], since("z_done", l) + 2)
                for j in range(2):
                    dve.tensor_scalar(acc[:, j, 0:n], z[:, j, 0:n], taps[:, j, 0:1], sm(l, "dw_b")[:, j:j + 1], ALU.mult,
                                      ALU.add).then_inc(sig["tap", l], 1)
                with dve.Fori(1, TAPS) as i:
                    for j in range(2):
                        dve.wait_ge(sig["tap", l], i * 2 + j - 1)
                        dve.scalar_tensor_tensor(acc[:, j, 0:n], z[:, j, bass.ds(i, n)], taps[:, j, bass.ds(i, 1)],
                                                 acc[:, j, 0:n], ALU.mult, ALU.add).then_inc(sig["tap", l], 1)
                dve.wait_ge(sig["c_mean", l], since("c_mean", l) + 1)
                for t0, n, c in pc:
                    s0 = t0 + (2 * HALO if c else 0)
                    last = dve.tensor_tensor(acc[:, :, s0:s0 + n], acc[:, :, s0:s0 + n],
                                             ps[:, 6 + c, 0:n].unsqueeze(1).to_broadcast([P, 2, n]), ALU.subtract)
                last.then_inc(sig["c_cent", l], 1)
                wc = pc[-1][0] + pc[-1][1]
                dve.wait_ge(sig["c_root", l], since("c_root", l) + 1)
                link(dve.reciprocal(tmp[2][:, 0:wc], tmp[2][:, 0:wc]), me)
                for j in range(2):
                    for t0, n, c in pc:
                        s0 = t0 + (2 * HALO if c else 0)
                        link(dve.scalar_tensor_tensor(acc[:, j, s0:s0 + n], acc[:, j, s0:s0 + n], sm(l, "ln_g")[:, j:j + 1],
                                                      tmp[2][:, t0:t0 + n], ALU.mult, ALU.mult), me)
                        last = dve.tensor_scalar(acc[:, j, s0:s0 + n], acc[:, j, s0:s0 + n], sm(l, "ln_b")[:, j:j + 1], None,
                                                 ALU.add)
                    last.then_inc(sig["c_lin", l], 1)
                for j in range(2):
                    dve.wait_ge(sig["c_tanh", l], since("c_tanh", l) + j + 1)
                    for t0, n, c in pc:
                        s0 = t0 + (2 * HALO if c else 0)
                        last = dve.scalar_tensor_tensor(acc[:, j, s0:s0 + n], tmp[j][:, t0:t0 + n], 1.0,
                                                        acc[:, j, s0:s0 + n], ALU.add, ALU.mult)
                last.then_inc(sig["c_act", l], 1)
                for i, (tile, g) in enumerate(HN):
                    wd = t_width(l, g)
                    dve.wait_ge(sig["hn_root", l], since("hn_root", l) + i + 1)
                    link(dve.reciprocal(hn_tmp[i][:, 0:wd], hn_tmp[i][:, 0:wd]), me)
                    gcol = qn_s[:, 0:1] if g == "q" else sm(l, "kn")
                    dve.scalar_tensor_tensor(qk[:, tile, 0:wd], qk[:, tile, 0:wd], gcol, hn_tmp[i][:, 0:wd], ALU.mult,
                                             ALU.mult).then_inc(sig["hn_done", l], 1)
                dve.wait_ge(sig["tables", l], since("tables", l) + 16)
                dve.wait_ge(sig["hn_done", l], since("hn_done", l) + 3)
                dve.wait_ge(sig["c_out", l], since("c_out", l) + 2)
                for i, (tile, _, tb) in enumerate(ROPE):
                    dve.wait_ge(sig["rp_mm", l], since("rp_mm", l) + i + 1)
                    t = rope_tmp[i % 2]
                    dve.tensor_tensor(t, ps[:, 2 * (i % 2), :], tab[:, tb + 1, :], ALU.mult).then_inc(sig["rp_done", l], 1)
                    link(dve.tensor_tensor(qk[:, tile, 0:LAT], qk[:, tile, 0:LAT], tab[:, tb, :], ALU.mult), me)
                    dve.wait_ge(sig["rp_done", l], since("rp_done", l) + i + 1)
                    dve.tensor_tensor(qk[:, tile, 0:LAT], qk[:, tile, 0:LAT], t, ALU.add).then_inc(sig["rp_add", l], 1)
                    dve.wait_ge(sig["rp_add", l], since("rp_add", l) + i + 1)
                if l == 0:
                    modulation(0, 4, MOD_BLOCKS)
                    dve.wait_ge(sig["mod_ev"], MOD_BLOCKS)
                    make_gain(0, 1)
                for kind in kinds(l):
                    s, s0 = at_sem, attn_since(l, kind)
                    lat = kind == "lat"
                    k0, kn, trips = (0, TOK, TL) if lat else (LAT, CTX, TC)
                    SELF = (4 if lat else 0) + 12 + 8

                    def tile(it):
                        cnt = [0]

                        def chain(ins):
                            cnt[0] += 1
                            ins.then_inc(s["self"], 1)
                            dve.wait_ge(s["self"], it * SELF + (s0["self"] + cnt[0]))

                        def top(j):
                            dve.wait_ge(s["s_mm"], it * 16 + (s0["s_mm"] + j + 1))
                            b = 2 * (j % AHEAD)
                            if lat and j == NA0:
                                dve.wait_ge(sig["bias_done", l], since("bias_done", l) + 1)
                            if lat and j >= NA0:
                                off = (6 * GRID_W) - it * (2 * GRID_W)
                                dve.tensor_tensor(ex[:, j % AHEAD, 0:LAT], ps[:, b, :], bt[:, j - NA0, bass.ds(off, LAT)],
                                                  ALU.add)
                                chain(dve.tensor_copy(ex[:, j % AHEAD, LAT:TOK], ps[:, b + 1, 0:CTX]))
                                src = ex[:, j % AHEAD, 0:kn]
                            else:
                                src = bank2(b, kn)
                            dve.tensor_reduce(negmax[:, j:j + 1], src, AX.X, ALU.max, negate=True).then_inc(s["s_max"], 1)

                        def difference(i):
                            j1 = last_score[i]
                            j0 = j1 - 1
                            dve.wait_ge(s["s_exp"], it * 16 + (s0["s_exp"] + j1 + 1))
                            chain(dve.reciprocal(rsum[:, j0:j1 + 1], sums[:, j0:j1 + 1]))
                            chain(dve.scalar_tensor_tensor(rsum[:, j1:j1 + 1], rsum[:, j1:j1 + 1], lam[:, 2 * l:2 * l + 1],
                                                           sums[:, j0:j0 + 1], ALU.mult, ALU.mult))
                            chain(dve.scalar_tensor_tensor(ex[:, j1 % AHEAD, 0:kn], ex[:, j1 % AHEAD, 0:kn],
                                                           rsum[:, j1:j1 + 1], ex[:, j0 % AHEAD, 0:kn], ALU.mult, ALU.add))
                            dve.sem_inc(s["p_diff"], 1)

                        for j in range(AHEAD):
                            top(j)
                        for i in range(12):
                            n = LAT if lat else CTX
                            dve.wait_ge(s["t_mm"], it * (24 if lat else 12) + (s0["t_mm"] + (2 if lat else 1) * i + 1))
                            dve.tensor_copy(pt[:, 0:n], ps[:, 6, 0:n]).then_inc(s["t_dve"], 1)
                            new = new_scores(i)
                            for j in new[:1]:
                                top(j)
                            j = last_score[i] - (1 if i in DIFF else 0)
                            if i not in DIFF:
                                dve.wait_ge(s["s_exp"], it * 16 + (s0["s_exp"] + j + 1))
                                chain(dve.reciprocal(rsum[:, j:j + 1], sums[:, j:j + 1]))
                            dve.wait_ge(s["o_mm"], it * 12 + (s0["o_mm"] + i + 1))
                            o0 = HD * (i % 2)
                            dve.tensor_scalar(otok[:, HD * i:HD * i + HD], ps[:, 7, o0:o0 + HD], rsum[:, j:j + 1], None,
                                              ALU.mult).then_inc(s["o_ev"], 1)
                            if i + 1 in DIFF:
                                difference(i + 1)
                            for j in new[1:]:
                                top(j)
                        assert cnt[0] == SELF, cnt

                    tile(0)
                    with dve.Fori(1, trips) as it:
                        tile(it)
                wc = TOK if l == 0 else LAT
                for i in range(2):
                    dve.wait_ge(sig["dn_root", l], since("dn_root", l) + i + 1)
                    link(dve.reciprocal(ex[:, i, 0:wc], ex[:, i, 0:wc]), me)
                    dve.scalar_tensor_tensor(u[:, 6 + i, 0:wc], u[:, 6 + i, 0:wc], qn_s[:, 1:2], ex[:, i, 0:wc], ALU.mult,
                                             ALU.mult).then_inc(sig["dn_done", l], 1)
                for i in range(8):
                    dve.wait_ge(sig["o_mm", l], since("o_mm", l) + i + 1)
                    for t0, n, c in parts_of(0)[:2 - l]:
                        last = dve.scalar_tensor_tensor(h[:, i, t0:t0 + n], ps[:, 4 + 2 * (i % 2) + c, 0:n],
                                                        mod[:, l, 16 + i, c:c + 1], h[:, i, t0:t0 + n], ALU.mult, ALU.add)
                    last.then_inc(sig["o_ev", l], 1)
                dve.wait_ge(sig["o_ev", l], since("o_ev", l) + 8)
                norm("n2", l, parts_of(l, True))
                nt = TL + (TC if l == 0 else 0)
                dve.wait_ge(sig["r_grp", l], since("r_grp", l) + 1)
                dve.tensor_copy(rt[0:16 * nt, :], ps[0:16 * nt, 2, 0:256]).then_inc(sig["r_cpy", l], 1)
                dve.wait_ge(sig["r_mm", l], since("r_mm", l) + 1)
                lgv = lg[:, 0:nt, :]
                for x in range(2):
                    last = dve.tensor_copy(lgv.rearrange("p (g x) e -> p x g e", x=2)[:, x, :, :],
                                           ps[:, 3, P * x:P * x + 16 * nt].rearrange("p (g e) -> p g e", e=32)[:, :, 0:E])
                link(last, me)
                link(dve.tensor_reduce(mx6[:, 0:nt], lgv, AX.X, ALU.max), me)
                dve.tensor_tensor(lgv, lgv, mx6[:, 0:nt].unsqueeze(2).to_broadcast([P, nt, E]),
                                  ALU.subtract).then_inc(sig["r_cp", l], 1)
                dve.wait_ge(sig["r_exp", l], since("r_exp", l) + 1)
                link(dve.tensor_reduce(mx6[:, 0:nt], lgv, AX.X, ALU.add), me)
                link(dve.reciprocal(mx6[:, 0:nt], mx6[:, 0:nt]), me)
                dve.tensor_tensor(lgv, lgv, mx6[:, 0:nt].unsqueeze(2).to_broadcast([P, nt, E]),
                                  ALU.mult).then_inc(sig["r_aff", l], 1)
                dve.wait_ge(sig["r_afft", l], since("r_afft", l) + 1)
                wt = P * nt
                link(dve.tensor_copy(wrk[:, 0:wt], afft[:, 0:wt]), me)
                groups = [(0, LAT, CAP_L)] + ([(LAT, CTX, CAP_C)] if l == 0 else [])
                for t0, n, cap in groups:
                    for r in range(cap // 8):
                        link(dve.max(top8[:], wrk[:, t0:t0 + n]), me)
                        link(dve.match_replace(wrk[:, t0:t0 + n], top8[:], wrk[:, t0:t0 + n], -1.0), me)
                link(dve.tensor_scalar(wrk[:, 0:wt], wrk[:, 0:wt], 0.0, None, ALU.is_lt), me)
                for t0, n, cap in groups:
                    link(dve.tensor_tensor_scan(cum[:, t0:t0 + n], wrk[:, t0:t0 + n], wrk[:, t0:t0 + n], 0.0, ALU.add,
                                                ALU.max), me)
                link(dve.tensor_tensor(pos[:, 0:wt], cum[:, 0:wt], wrk[:, 0:wt], ALU.mult), me)
                dve.tensor_scalar(pos[:, 0:wt], pos[:, 0:wt], -1.0, None, ALU.add).then_inc(sig["r_pos", l], 1)
                if l == 0:
                    modulation(1, 0, MOD_BLOCKS)
                    dve.wait_ge(sig["mod_ev"], 2 * MOD_BLOCKS)
                both = l == 0
                dve.wait_ge(sig["e_clear", l], 1)
                dve.wait_ge(sig["r_ptr", l], since("r_ptr", l) + 1)
                link(dve.tensor_copy(ptok[:, 0:nt, 0:E], ps[:, 3, 0:E * nt].rearrange("p (t e) -> p t e", e=E)), me)

                def one_hot(cnt, off):
                    dve.wait_ge(sig["e_xmm", l], cnt * 8)
                    last = dve.tensor_tensor(gl[:, :, :].rearrange("p t (e j) -> p t e j", j=64),
                                             cst("iota").unsqueeze(1).unsqueeze(1).to_broadcast([P, TL, 2, 64]),
                                             ptok[:, 0:TL, bass.ds(off, 2)].unsqueeze(3).to_broadcast([P, TL, 2, 64]),
                                             ALU.is_equal)
                    if both:
                        last = dve.tensor_tensor(gc[:, :, :].rearrange("p t (e j) -> p t e j", j=32),
                                                 cst("iota")[:, 0:32].unsqueeze(1).unsqueeze(1).to_broadcast([P, TC, 2, 32]),
                                                 ptok[:, TL:TL + TC, bass.ds(off, 2)].unsqueeze(3).to_broadcast([P, TC, 2, 32]),
                                                 ALU.is_equal)
                    last.then_inc(sig["e_g", l], 1)

                one_hot(0, 0)
                with dve.Fori(0, PAIRS // 2) as pp:
                    for half_p in range(2):
                        dve.wait_ge(sig["e_bc", l], (pp * 2 + half_p + 1) * 16 * (4 if both else 2))
                        dve.wait_ge(sig["e_sc", l], (pp * 2 + half_p) * 8)
                        last = dve.scalar_tensor_tensor(s_lat, pbl[:, 0, :], cst("j_lat"), pbl[:, 1, :], ALU.is_equal, ALU.mult)
                        if both:
                            last = dve.scalar_tensor_tensor(s_ctx, pbc[:, 0, :], cst("j_ctx"), pbc[:, 1, :], ALU.is_equal,
                                                            ALU.mult)
                        last.then_inc(sig["e_s", l], 1)
                        one_hot(pp * 2 + half_p + 1, pp * 4 + (2 * half_p + 2))
                        if not both:
                            for e in range(2):
                                dve.wait_ge(sig["e_tanh", l], pp * 4 + 2 * half_p + e + 1)
                                dve.scalar_tensor_tensor(h_tok[e], h_tok[e], 1.0, ps[:, 2 * e, :], ALU.add,
                                                         ALU.mult).then_inc(sig["tap", l], 1)
                                dve.wait_ge(sig["tap", l], pp * 4 + (2 * TAPS + 2 * half_p + e + 1))
                                dve.wait_ge(sig["e_gu", l], pp * 16 + 8 * half_p + 4 * e + 4)
                                dve.tensor_tensor(h_tok[e], h_tok[e], ps[:, 2 * e + 1, :], ALU.mult).then_inc(sig["e_h", l], 1)
                        else:
                            for e in range(2):
                                for half in range(2):
                                    dve.wait_ge(sig["e_tanh", l], pp * 8 + 4 * half_p + 2 * e + half + 1)
                                    dve.scalar_tensor_tensor(th2, th2, 1.0, ps[:, 2 * half, :], ALU.add, ALU.mult).then_inc(sig["tap", l], 1)
                                    dve.wait_ge(sig["tap", l], pp * 8 + (2 * TAPS + 4 * half_p + 2 * e + half + 1))
                                    dve.wait_ge(sig["e_gu", l], pp * 16 + 8 * half_p + 4 * e + 2 * half + 2)
                                    dve.wait_ge(sig["e_dn", l], pp * 8 + max(4 * half_p + 2 * e - 2, 0))
                                    dve.tensor_tensor(he[e][:, 4 * half:4 * half + 4, :],
                                                      th2.rearrange("p (f w) -> p f w", w=P),
                                                      ps[:, 2 * half + 1, :].rearrange("p (f w) -> p f w", w=P), ALU.mult).then_inc(sig["e_h", l], 1)
                        for dt in range(KD):
                            dve.wait_ge(sig["e_sc", l], pp * 16 + 8 * half_p + dt + 1)
                            last = dve.scalar_tensor_tensor(h[:, dt, 0:LAT], ps[:, 6 + dt % 2, :],
                                                            mod[:, l, 40 + dt, 0:1], h[:, dt, 0:LAT], ALU.mult, ALU.add)
                            if both:
                                last = dve.scalar_tensor_tensor(h[:, dt, LAT:TOK], ps[:, 2 + dt % 2, 0:CTX],
                                                                mod[:, l, 40 + dt, 1:2], h[:, dt, LAT:TOK], ALU.mult, ALU.add)
                            last.then_inc(sig["e_acc", l], 1)
                dve.wait_ge(sig["e_acc", l], 8 * PAIRS)
            dve.wait_ge(sig["fin_root"], 1)
            dve.reciprocal(ex[:, 2, 0:LAT], ex[:, 2, 0:LAT]).then_inc(sig["fin_rinv"], 1)
            dve.wait_ge(sig["fin_rinv"], 1)
            for k in range(KD):
                dve.scalar_tensor_tensor(u[:, k, 0:LAT], h[:, k, 0:LAT], sm(0, "final")[:, k:k + 1], ex[:, 2, 0:LAT], ALU.mult,
                                         ALU.mult).then_inc(sig["fin_out"], 1)

        @block.gpsimd
        def _(pool):
            for l in range(LAYERS):
                pool.wait_ge(sig["n1_pre", l], since("n1_pre", l) + KD)
                pool.memset(z[:, :, :], 0.0).then_inc(sig["z_zero", l], 1)
                pool.dma_start(tab[:, :, :], a["tables"]).then_inc(sig["tables", l], 16)
                pool.dma_start(pw[:], a["pw"][l]).then_inc(sig["layer_in", l], 16)
                pool.wait_ge(sig["c_y", l], since("c_y", l) + 1)
                pool.dma_start(bt[:, :, :], a["rpb"][l]).then_inc(sig["bias_ld", l], 16)
                pool.wait_ge(sig["rp_add", l], since("rp_add", l) + 7)
                pool.memset(qst[:, :, :], 0.0).then_inc(sig["q_zero", l], 1)
                pool.wait_ge(sig["q_zero", l], since("q_zero", l) + 1)
                for kind in kinds(l):
                    s, s0 = at_sem, attn_since(l, kind)
                    k0, trips = (0, TL) if kind == "lat" else (LAT, TC)
                    if kind == "ctx":
                        pool.wait_ge(at_sem["s_mm"], 16 * TL)

                    def stage(g, t0, before):
                        for x, (pn, src, dst, tiles, units) in enumerate(STAGE[g]):
                            pool.tensor_copy(qst[dst:dst + pn, units, :],
                                             qk[src:src + pn, tiles, bass.ds(t0, P)]).then_inc(s["q_st"], 1)
                            pool.wait_ge(s["q_st"], before + (0, 4, 8)[g] + x + 1)

                    for g in range(3):
                        stage(g, k0, s0["q_st"])
                    if kind == "lat":
                        pool.wait_ge(sig["bias_ld", l], since("bias_ld", l) + 16)
                        btv = bt[:, :, :].rearrange("p h (m w) -> p (h m) w", w=GRID_W)
                        pool.tensor_tensor(btv, btv, cst("mask").unsqueeze(1).to_broadcast([P, 4 * BIAS_DR, GRID_W]),
                                           ALU.add).then_inc(sig["bias_done", l], 1)
                    with pool.Fori(1, trips) as it:
                        for g in range(3):
                            pool.wait_ge(s["s_mm"], it * 16 + (s0["s_mm"] - 16 + (4, 12, 16)[g]))
                            stage(g, it * P + k0, it * 10 + s0["q_st"])
                nt = TL + (TC if l == 0 else 0)
                pool.wait_ge(sig["n2_pre", l], since("n2_pre", l) + KD)
                both = l == 0
                pool.memset(ptok[:, :, :], -1.0)
                pool.memset(pbc[:, :, :], -7.0)
                pool.memset(yc, 0.0).then_inc(sig["e_clear", l], 1)
                pool.wait_ge(sig["r_pos", l], since("r_pos", l) + 1)
                pool.dma_start(route[:, 0, 0:P * nt], pos[:, 0:P * nt]).then_inc(sig["r_store", l], 16)
                pool.dma_start(route[:, 1, 0:P * nt], afft[:, 0:P * nt]).then_inc(sig["r_store", l], 16)
                pool.wait_ge(sig["r_store", l], since("r_store", l) + 32)
                pool.wait_ge(sig["e_clear", l], 1)
                with pool.Fori(0, PAIRS) as p:
                    pool.wait_ge(sig["e_s", l], p)
                    for e in range(2):
                        src = route[bass.ds(p * 2 + e, 1), :, 0:LAT].to_broadcast([64, 2, LAT])
                        pool.dma_start(pbl[64 * e:64 * e + 64, :, :], src).then_inc(sig["e_bc", l], 16)
                        if both:
                            r0 = 64 - 32 * e
                            src = route[bass.ds(p * 2 + e, 1), :, LAT:TOK].to_broadcast([32, 2, CTX])
                            pool.dma_start(pbc[r0:r0 + 32, :, :], src).then_inc(sig["e_bc", l], 16)


def constants():
    c = np.zeros((P, CONST_N), np.float32)

    def put(name, v):
        lo, hi = CONST[name]
        c[:, lo:hi] = v

    p = np.arange(P)
    put("ident", np.eye(P))
    put("ones_d", 1.0 / D)
    put("ones_c", 1.0 / 256)
    put("ones_h", (p[:, None] // HD == p[None, :] // HD) / HD)
    put("swap32", p[:, None] == (p[None, :] ^ 32))
    put("swap16", p[:, None] == (p[None, :] ^ 16))
    j = p % GRID_W
    start = np.clip(j - WIN_C // 2, 0, GRID_W - WIN_C)[:, None]
    w = np.arange(GRID_W)[None, :]
    put("mask", np.where((w >= start) & (w < start + WIN_C), 0.0, NEG))
    put("iota", np.arange(64)[None, :])
    put("j_lat", (p % 64)[:, None])
    put("j_ctx", (p % 32)[:, None])
    put("eps", EPS)
    put("pick", (p[:, None] // 64 == np.arange(4)[None, :] // 2) & (p[:, None] % 32 == np.arange(4)[None, :] % 2))
    tables = np.zeros((P, 4, LAT), np.float32)
    t = np.arange(LAT)
    rows, cols = (t // GRID_W).astype(np.float32), (t % GRID_W).astype(np.float32)
    for i, d in enumerate((HD, DQ)):
        half, nf = d // 2, d // 4
        inv = (1.0 / (np.float32(10000.0) ** (np.arange(nf, dtype=np.float32) / np.float32(nf)))).astype(np.float32)
        ang = np.concatenate([rows[:, None] * inv, cols[:, None] * inv], 1).T.astype(np.float32)
        r = p % d
        tables[:, 2 * i] = np.cos(ang)[r % half]
        tables[:, 2 * i + 1] = np.sin(ang)[r % half] * np.where(r < half, -1.0, 1.0)[:, None]
    return c, tables


def kernel(x, c, ctx, c_ctx, norm1_g, w_mod, b_mod, w_in, na_rpb, conv_dw_w, conv_dw_b, conv_ln_g, conv_ln_b,
           conv_pw_w, conv_pw_b, gqa_qn_g, gqa_kn_g, diff_lq1, diff_lk1, diff_lq2, diff_lk2, diff_norm_g, w_out,
           norm2_g, w_router, w_gate, w_up, w_down, final_g):
    import concourse.bacc as bacc
    from concourse.bass_utils import run_bass_kernel_spmd

    L = LAYERS

    def cols(v):
        v = np.asarray(v)
        return np.moveaxis(v.reshape(*v.shape[:-1], -1, P), -1, -2)

    def blocks(w):
        w = np.asarray(w)
        n = w.shape[-1] // BLK
        w = w.reshape(*w.shape[:-2], KD, P, n, BLK)
        return np.ascontiguousarray(np.moveaxis(w, (-2, -3, -4), (-4, -3, -2)))

    stream = np.concatenate([np.asarray(x)[0], np.asarray(ctx)[0]], 0)
    cmat, tables = constants()
    small = np.zeros((P, L, SMALL_N), np.float32)

    def put(name, v):
        lo, hi = SMALL[name]
        small[:, :, lo:hi] = np.moveaxis(np.asarray(v).reshape(L, P, -1), 0, 1)

    def twice(v):
        return np.repeat(cols(v)[..., None], 2, -1)

    put("b_mod", twice(b_mod))
    put("norm1", twice(norm1_g))
    put("norm2", twice(norm2_g))
    put("taps", np.moveaxis(cols(conv_dw_w), 1, 3))
    put("dw_b", cols(conv_dw_b))
    put("ln_g", cols(conv_ln_g))
    put("ln_b", cols(conv_ln_b))
    put("pw_b", cols(conv_pw_b))
    put("qn", np.tile(np.asarray(gqa_qn_g), (1, 2)))
    put("kn", np.tile(np.asarray(gqa_kn_g), (1, 2)))
    put("dn", np.tile(np.asarray(diff_norm_g), (1, 2)))
    lam = np.stack([np.asarray(v) for v in (diff_lq1, diff_lk1, diff_lq2, diff_lk2)], 1)
    put("lam", np.repeat(lam[:, None], P, 1))
    put("router", np.moveaxis(np.asarray(w_router).reshape(L, KD, P, E), 1, 2))
    put("final", np.repeat(cols(final_g)[None], L, 0))
    g, up, dn = blocks(w_gate), blocks(w_up), blocks(w_down)
    gate_up = np.stack([g[:, :, 0], up[:, :, 0], g[:, :, 1], up[:, :, 1]], 2).reshape(L, PAIRS, 8, P, KD, BLK)
    w_exp = np.concatenate([gate_up, dn.reshape(L, PAIRS, 4, P, KD, BLK)], 2)
    del g, up, dn, gate_up
    rpb = np.zeros((L, 4, 15, 2 * GRID_W - 1), np.float32)
    rpb[..., GRID_W - WIN_C:GRID_W - WIN_C + 2 * WIN_C - 1] = np.asarray(na_rpb)
    j, w = np.arange(GRID_W)[:, None], np.arange(GRID_W)[None, :]
    rpb = rpb[..., w - j + GRID_W - 1]
    rpb = np.stack([rpb[:, :, 1 - r:1 - r + BIAS_DR] for r in range(2)], 1)
    rpb = np.ascontiguousarray(rpb.transpose(0, 1, 4, 2, 3, 5)).reshape(L, P, 4, BIAS_DR * GRID_W)
    arrays = {
        "x": np.ascontiguousarray(np.moveaxis(stream.T.reshape(KD, P, TOK), 0, 1)),
        "cond": np.ascontiguousarray(np.stack([cols(np.asarray(c)[0]), cols(c_ctx)], -1)),
        "const": cmat, "tables": tables, "small": small, "rpb": rpb,
        "w_mod": blocks(w_mod), "w_in": blocks(w_in), "w_out": blocks(w_out), "w_exp": w_exp,
        "pw": np.ascontiguousarray(np.moveaxis(np.asarray(conv_pw_w).reshape(L, 2, P, 256), 1, 2)),
    }
    nc = bacc.Bacc("TRN2", target_bir_lowering=False, num_devices=1)
    args = {n: nc.dram_tensor("in_" + n, v.shape, F32, kind="ExternalInput").ap() for n, v in arrays.items()}
    out = nc.dram_tensor("out_t", (P, KD, LAT), F32, kind="ExternalOutput").ap()
    program(nc, args, out)
    r = run_bass_kernel_spmd(nc, [{"in_" + n: v for n, v in arrays.items()}], core_ids=[0])
    res = np.asarray(r.results[0]["out_t"])
    return np.ascontiguousarray(np.moveaxis(res, 0, 1).reshape(D, LAT).T)[None]
```

```python
from contextlib import ExitStack
import math

import numpy as np

import concourse.bass as bass
from concourse import mybir

F32 = mybir.dt.float32
ALU = mybir.AluOpType
ACT = mybir.ActivationFunctionType
AX = mybir.AxisListType

P = 128
D = 1024
KD = D // P
LAT, CTX = 512, 256
TOK = LAT + CTX
TL, TC = LAT // P, CTX // P
LAYERS = 2
GRID_W, ROWS = 64, LAT // 64
WIN_R, WIN_C = 8, 16
TAPS = 31
HALO = TAPS // 2
HD = 64
DQ = 32
E = 16
CAP_L, CAP_C = 2 * LAT // E, 2 * CTX // E
EPS = 1e-6
RING = 4
BLK = 512
MOD_BLOCKS = 6 * D // BLK
IN_BLOCKS = 5
OUT_BLOCKS = D // BLK
PAIRS = E // 2
LAM_INIT = [0.8 - 0.6 * math.exp(-0.3 * l) for l in range(LAYERS)]
NEG = -1.0e30

SMALL = {}
_at = 0
for _name, _n in (("router", KD * E), ("b_mod", 96), ("norm1", 16), ("norm2", 16), ("taps", 2 * TAPS), ("dw_b", 2), ("ln_g", 2),
                  ("ln_b", 2), ("pw_b", 2), ("qn", 1), ("kn", 1), ("dn", 1), ("lam", 4 * DQ),
                  ("final", KD)):
    SMALL[_name] = (_at, _at + _n)
    _at += _n
SMALL_N = _at

CONST = {}
_at = 0
for _name, _n in (("ident", P), ("ones_d", P), ("ones_c", P), ("ones_h", P), ("swap32", P), ("swap16", P),
                  ("mask", GRID_W), ("iota", 64), ("j_lat", 1), ("j_ctx", 1), ("eps", 1), ("pick", 4)):
    CONST[_name] = (_at, _at + _n)
    _at += _n
CONST_N = _at

QK_AT = 0
V_AT = QK_AT + 11 * TOK
WORK_AT = V_AT + 6 * 640
ZW = TOK + 4 * HALO
ACCW = ZW - 2 * HALO
TH_AT = WORK_AT
Z_AT = TH_AT + 2 * TOK
PW_AT = Z_AT + 2 * ZW
ACC_AT = PW_AT + 2 * 256
TAB_AT = ACC_AT + max(2 * ACCW, TOK + 2 * LAT)
TA_AT = TAB_AT + 4 * LAT
TB_AT = TA_AT + TOK
BIAS_DR = 14
BT_AT = WORK_AT
EX_AT = BT_AT + 4 * BIAS_DR * GRID_W
PT_AT = EX_AT + 3 * TOK
QST_AT = PT_AT + TOK
OT_AT = QST_AT + 16 * P
UTOK_AT = 0
XE_AT = UTOK_AT + 6 * D
HE_AT = XE_AT + 2 * KD * 192
HTOK_AT = HE_AT + 3 * KD * 64
YL_AT = 13056
YC_AT = YL_AT + D
SL_AT = YC_AT + D
SC_AT = SL_AT + LAT
GL_AT = SC_AT + CTX
GC_AT = GL_AT + TL * P
PBL_AT = GC_AT + TC * 64
PBC_AT = PBL_AT + 2 * LAT
PTOK_AT = PBC_AT + 2 * CTX
LG_AT = PTOK_AT + 6 * (E + 2)
AFFT_AT = LG_AT + 6 * E
WRK_AT = AFFT_AT + TOK
CUM_AT = WRK_AT + TOK
POS_AT = CUM_AT + TOK
ARENA = max(OT_AT + 6 * P, TB_AT + TOK, POS_AT + TOK)
assert EX_AT <= ACC_AT
assert HTOK_AT + 3 * 512 <= YL_AT


def program(nc, a, out):
    ctx = ExitStack()
    with ctx:
        def sb(name, shape):
            return ctx.enter_context(nc.sbuf_tensor(name, shape, F32))

        ring = sb("ring", [P, RING, KD, BLK])
        h = sb("h", [P, KD, TOK])
        u = sb("u", [P, KD, TOK])
        arena = sb("arena", [P, ARENA])
        small = sb("small", [P, LAYERS, SMALL_N])
        const = sb("const", [P, CONST_N])
        cond = sb("cond", [P, KD, 2])
        cond_t = sb("cond_t", [P, KD, 2])
        cond_w = sb("cond_w", [P, KD, 32])
        mod = sb("mod", [P, LAYERS, 48, 2])
        gain = sb("gain", [P, 2, KD, 2])
        lam = sb("lam", [P, 4])
        qn_s = sb("qn_s", [P, 2])
        negmax = sb("negmax", [P, 16])
        sums = sb("sums", [P, 16])
        rsum = sb("rsum", [P, 16])
        top8 = sb("top8", [E, 8])
        mx6 = sb("mx6", [P, 12])
        ps = ctx.enter_context(nc.psum_tensor("ps", [P, 8, 512], F32))
        route = nc.dram_tensor("route", [E, 2, TOK], F32, kind="Internal").ap()

        def view(at, *shape, parts=P):
            n = int(np.prod(shape))
            v = arena[0:parts, at:at + n]
            if len(shape) == 2:
                v = v.rearrange("p (a b) -> p a b", b=shape[1])
            if len(shape) == 3:
                v = v.rearrange("p (a b c) -> p a b c", b=shape[1], c=shape[2])
            return v

        def sm(l, name):
            lo, hi = SMALL[name]
            return small[:, l, lo:hi]

        def cst(name, parts=P):
            lo, hi = CONST[name]
            return const[0:parts, lo:hi]

        psf = ps[:, :, :].rearrange("p b n -> p (b n)")

        def bank2(b, n=TOK):
            return psf[:, 512 * b:512 * b + n]

        qk = view(QK_AT, 11, TOK)
        val = view(V_AT, 6, 640)
        acc, th, z = view(ACC_AT, 2, ACCW), view(TH_AT, 2, TOK), view(Z_AT, 2, ZW)
        a_raw = arena[:, ACC_AT:ACC_AT + 2 * TOK].rearrange("p (a b) -> p a b", b=TOK)
        tab = view(TAB_AT, 4, LAT)
        tmp = [view(TA_AT, TOK), view(TB_AT, TOK), view(TH_AT, TOK)]
        conv_y = view(Z_AT, 2, TOK)
        hn_tmp = [tmp[0], tmp[1], view(ACC_AT, TOK)]
        rope_tmp = [view(ACC_AT + TOK + i * LAT, LAT) for i in range(2)]
        bt = view(BT_AT, 4, BIAS_DR * GRID_W)
        ex = view(EX_AT, 3, TOK)
        pt = view(PT_AT, TOK)
        qst = view(QST_AT, 16, P)
        pw = view(PW_AT, 2, 256)
        otok = view(OT_AT, TOK)
        utok = view(UTOK_AT, 6, D)
        gl, gc = view(GL_AT, TL, P), view(GC_AT, TC, 64)
        s_lat, s_ctx = view(SL_AT, LAT), view(SC_AT, CTX)
        yl, yc = view(YL_AT, D), view(YC_AT, D)
        pbl, pbc = view(PBL_AT, 2, LAT), view(PBC_AT, 2, CTX)
        ptok = view(PTOK_AT, 6, E + 2)
        rt = view(CUM_AT, 256)
        MOD_TOK = {"start": [view(EX_AT + i * 256, 256) for i in range(2)], "in": [view(TA_AT, 256), view(TB_AT, 256)],
                   "context": [view(PT_AT + (1 + i) * CTX, CTX) for i in range(2)],
                   "out": [view(PT_AT + i * 256, 256) for i in range(2)]}
        lg = view(LG_AT, 6, E)
        afft, wrk = view(AFFT_AT, TOK, parts=E), view(WRK_AT, TOK, parts=E)
        cum, pos = view(CUM_AT, TOK, parts=E), view(POS_AT, TOK, parts=E)
        he = [view(HE_AT + i * KD * 64, KD, 64) for i in range(3)]
        h_tok = [view(HTOK_AT + i * 512, 512) for i in range(3)]

        filled = [ctx.enter_context(nc.semaphore(f"filled{s}")) for s in range(RING)]
        used = [ctx.enter_context(nc.semaphore(f"used{s}")) for s in range(RING)]
        names = ("loaded x_loaded stored cond_tanh cond_done mod_mm mod_cp mod_pk mod_ev self0 gain_done lam_dot lam_exp fin_mm fin_sq "
                 "fin_root fin_rinv fin_out").split()
        sig = {n: ctx.enter_context(nc.semaphore(n)) for n in names}
        SINCE = {}
        for names_, n_ in (("n1_sq n1_mm n2_sq n2_mm o_mm o_ev", 8), ("n1_pre n1_u n2_pre n2_u", 16), ("t_mm t_ev", 15),
                           ("v_mm v_ev", 18), ("q_zero z_done c_sq c_lin c_tanh c_pw c_out dn_sq dn_mm dn_root dn_done", 2),
                           ("n1_root n2_root z_zero c_mean c_cent c_var c_root c_act bias_done r_mm r_cp r_exp r_aff r_tr "
                            "r_afft r_pos r_ptr c_y r_grp r_cpy", 1), ("tables layer_in", 16), ("hn_sq hn_mm hn_root hn_done", 3),
                           ("rp_mm rp_done rp_add", 7), ("bias_ld", 16), ("r_store", 32), ("ut_mm ut_ev", 12)):
            for n in names_.split():
                SINCE[n] = n_
                sig[n, 0] = sig[n, 1] = ctx.enter_context(nc.semaphore(n))

        def since(n, l):
            return l * SINCE[n]

        per_layer = "tap e_clear e_bc e_s e_g e_xmm e_xev e_gu e_tanh e_h e_dn e_y e_sc e_acc self".split()
        for n in ("e_ht", "e_hev", "e_cgu"):
            sig[n] = ctx.enter_context(nc.semaphore(n))
        ATTN = {"q_st": (10, 10), "s_mm": (16, 16), "s_max": (16, 16), "s_exp": (16, 16), "p_diff": (4, 4), "t_mm": (24, 12),
                "t_dve": (12, 12), "t_act": (12, 0), "o_mm": (12, 12), "o_ev": (12, 12), "y_mm": (2, 2), "y_ev": (2, 2),
                "self": (24, 20)}
        at_sem = {n: ctx.enter_context(nc.semaphore("at_" + n)) for n in ATTN}

        def attn_since(l, kind):
            done = (0, 0) if (l, kind) == (0, "lat") else (TL, 0) if kind == "ctx" else (TL, TC)
            return {n: done[0] * x + done[1] * y for n, (x, y) in ATTN.items()}

        for l in range(LAYERS):
            for n in per_layer:
                sig[n, l] = ctx.enter_context(nc.semaphore(f"{n}_{l}"))
        def parts_of(l, second=False):
            both = [(0, LAT, 0), (LAT, CTX, 1)]
            return both[:1] if (l and second) else both

        IN_ORDER = (1, 2, 0, 3, 4)
        MOD_C = MOD_BLOCKS
        STREAM = [("mod", m) for m in range(4)] + [("in", 0, 0)] + [("mod", m) for m in (4, 5)]
        STREAM += [("in", 0, 1)] + [("mod", m) for m in (6, 7)] + [("in", 0, b) for b in (2, 3, 4)]
        STREAM += [("mod", m) for m in range(8, MOD_BLOCKS)]
        STREAM += [("mod", MOD_C + m) for m in range(RING * TC)]
        STREAM += [("out", 0, 0)] + [("mod", m) for m in (20, 21)] + [("out", 0, 1)] + [("mod", m) for m in (22, 23)]
        STREAMS = [STREAM, [("in", 1, b) for b in range(IN_BLOCKS)] + [("out", 1, b) for b in range(OUT_BLOCKS)]]
        at, n_at = {}, 0
        for l in range(LAYERS):
            for key in STREAMS[l]:
                at[key] = n_at
                n_at += 1
            at["exp", l] = n_at
            n_at += 6 * E

        T_TILES = [("nq", 0, 0, 0), ("nq", 0, 1, 1), ("k", 0, 2, 2), ("k", 0, 3, 3),
                   ("a", 1, 2, 0), ("a", 1, 3, 1), ("g", 2, 0, 0), ("g", 2, 1, 1),
                   ("q", 2, 2, 4), ("q", 2, 3, 5), ("k", 3, 0, 6),
                   ("dq", 3, 2, 7), ("dq", 3, 3, 8), ("k", 4, 0, 9), ("k", 4, 1, 10)]
        V_COLS = [(1, 0, 256, 0), (3, 128, 128, 256), (4, 256, 256, 384)]
        def values(i):
            return [("v", i, t) for t in range(TL + TC)]

        v = values(0)
        P_STEPS = [("blk", 0), v[0], v[1], ("mod", 4), v[2], ("pick", 4), v[3], ("mod", 5), v[4], ("pick", 5), v[5],
                   ("t", 4), ("t", 5)]
        P_STEPS += [("blk", 1), ("t", 6), ("mod", 6), ("t", 7), ("pick", 6), ("mod", 7), ("pick", 7), ("t", 8), ("t", 9)]
        P_STEPS += [("blk", 2)] + [("t", i) for i in (0, 1, 2, 3)]
        P_STEPS += [("blk", 3), ("t", 10), ("c_mean",)] + values(1)[:3] + [("c_sq",)] + values(1)[3:5] + [("c_var",)]
        P_STEPS += values(1)[5:] + [("t", 11), ("c_tanh",), ("t", 12), ("c_pw", 0), ("hn_sq", 0), ("hn_sq", 1)]
        P_STEPS += [("blk", 4), ("t", 13), ("hn", 0), ("c_pw", 1), ("t", 14), ("hn", 1), ("hn_sq", 2)]
        P_STEPS += [values(2)[0], ("hn", 2), ("rope", 0)]
        for v, ropes in zip(values(2)[1:], ((1,), (2,), (3,), (4, 5), (6,))):
            P_STEPS += [v] + [("rope", i) for i in ropes]

        OUT_STEPS = [[("g", 0), ("mod", 20), ("g", 1), ("pick", 20), ("g", 2), ("mod", 21), ("g", 3), ("pick", 21), ("g", 4),
                      ("mod", 22), ("g", 5), ("pick", 22), ("g", 6), ("mod", 23), ("g", 7), ("pick", 23)],
                     [("g", i) for i in range(KD)]]

        UT_FIRST = 4

        def place(kind, i):
            return max(n for n, x in enumerate([x for x in P_STEPS if x[0] == kind]) if x[1] == i)

        def t_width(l, kind):
            return TOK if (l == 0 or kind == "k") else LAT

        HN_BANK = (4, 4, 6)
        HN = [(4, "q"), (5, "q"), (6, "k")]
        ROPE = [(7, "swap16", 2), (8, "swap16", 2), (9, "swap16", 2), (10, "swap16", 2),
                (4, "swap32", 0), (5, "swap32", 0), (6, "swap32", 0)]

        def kinds(l):
            return ("lat", "ctx") if l == 0 else ("lat",)

        HEADS = (0, 4, 1, 5, 2, 6, 3, 7, 8, 9, 10, 11)
        TILES = [[hd] if hd < 4 else [2 * hd - 4, 2 * hd - 3] if hd < 8 else [hd + 4] for hd in HEADS]
        SOFTMAX = [t for ts in TILES for t in ts]
        KEYS = [6] * 4 + [9] * 4 + [10] * 4 + [2, 2, 3, 3]
        NA0 = 12
        STAGE = [
                 [(64, 64 * r, 64 * g, slice(4 + g, 5 + g), slice(2 * g + r, 2 * g + r + 1))
                  for g in range(2) for r in range(2)],
                 [(32, 32 * r, 32 * r, slice(7, 9), slice(4 + r, 12, 4)) for r in range(4)],
                 [(64, 64 * r, 64 * r, slice(0, 2), slice(12 + r, 16, 2)) for r in range(2)]]
        STAGED = (0, 4, 8, 10)
        last_score = [sum(len(ts) for ts in TILES[:i + 1]) - 1 for i in range(12)]
        v_col = [256 + 64 * (i // 2) for i in range(4)] + [384 + 64 * i for i in range(4)] + [64 * i for i in range(4)]
        DIFF = [i for i in range(12) if len(TILES[i]) == 2]
        AHEAD = 3

        EARLY = {9: 1, 10: 2, 11: 0}

        def nth(j):
            return (3, 1, 2)[j] if j < AHEAD else j + 1

        def upto(j):
            return max(nth(x) for x in range(j + 1))

        def new_scores(i):
            first = last_score[i - 1] + AHEAD + 1 if i else AHEAD
            return range(first, min(last_score[i] + AHEAD + 1, 16))

        block = ctx.enter_context(nc.Block())

        @block.sync
        def _(sp):
            sp.dma_start(cond[:], a["cond"]).then_inc(sig["loaded"], 16)
            sp.dma_start(const[:], a["const"]).then_inc(sig["loaded"], 16)
            sp.dma_start(small[:], a["small"]).then_inc(sig["loaded"], 16)

            def fill(n, src):
                s = n % RING
                if n >= RING:
                    sp.wait_ge(used[s], n // RING)
                sp.dma_start(ring[:, s, :, :], src).then_inc(filled[s], 16)

            sp.dma_start(h[:], a["x"]).then_inc(sig["x_loaded"], 16)
            for l in range(LAYERS):
                for key in STREAMS[l]:
                    if key[0] == "mod":
                        fill(at[key], a["w_mod"][key[1] // MOD_BLOCKS, key[1] % MOD_BLOCKS])
                    elif key[0] == "in":
                        fill(at[key], a["w_in"][l, IN_ORDER[key[2]]])
                    else:
                        fill(at[key], a["w_out"][l, key[2]])
                with sp.Fori(0, PAIRS) as p:
                    for j in range(12):
                        n = at["exp", l] + j
                        s = n % RING
                        sp.wait_ge(used[s], p * 3 + n // RING)
                        sp.dma_start(ring[:, s, :, :], a["w_exp"][l, p, j]).then_inc(filled[s], 16)
            for k in range(KD):
                sp.wait_ge(sig["fin_out"], k + 1)
                sp.dma_start(out[:, k, :], u[:, k, 0:LAT]).then_inc(sig["stored"], 16)
            sp.wait_ge(sig["stored"], 16 * KD)

        @block.tensor
        def _(pe):
            def ready(n, turn=None, fills=1):
                s = n % RING
                v = 16 * (n // RING + 1)
                pe.wait_ge(filled[s], v if turn is None else turn * (16 * fills) + v)
                return ring[:, s, :, :]

            def release(held):
                if held:
                    n, sem, count = held
                    pe.wait_ge(sem, count)
                    pe.sem_inc(used[n % RING], 1)

            owed = []

            def pay():
                while owed:
                    release(owed.pop(0))

            def mod_products(m, bank, q=None, turn=0):
                q = m if q is None else q
                w = ready(at["mod", q], turn)
                if q >= 2:
                    pe.wait_ge(sig["mod_ev"], m - 1)
                for k in range(KD):
                    for c in range(2):
                        g = 2 * c + k % 2
                        mm = pe.matmul(ps[32 * g:32 * g + 32, bank, 0:256], cond_w[:, k, :],
                                       w[:, k, 256 * c:256 * c + 256], start=k < 2, stop=k >= KD - 2,
                                       tile_position=(0, 32 * g))
                mm.then_inc(sig["mod_mm"], 1)
                pay()
                owed.append((at["mod", q], sig["mod_mm"], m + 1))

            def mod_pick(m, bank, tok):
                pe.wait_ge(sig["mod_cp"], m + 1)
                for x in range(2):
                    mm = pe.matmul(ps[:, bank, 256 + 4 * x:260 + 4 * x], tok[:, P * x:P * x + P], cst("pick"),
                                   start=True, stop=True)
                mm.then_inc(sig["mod_pk"], 1)

            def modulation(ms):
                for m in ms:
                    mod_products(m, 6 + m % 2)
                    if m > ms[0]:
                        mod_pick(m - 1, 7 - m % 2, MOD_TOK["start"][1 - m % 2])
                pay()
                mod_pick(ms[-1], 6 + ms[-1] % 2, MOD_TOK["start"][ms[-1] % 2])

            def norm_sum(which, l, parts, ks=range(KD)):
                for k in ks:
                    pe.wait_ge(sig[which + "_sq", l], since(which + "_sq", l) + k + 1)
                    for t0, n, c in parts:
                        mm = pe.matmul(ps[:, c, 0:n], cst("ones_d"), ex[:, k % 2, t0:t0 + n],
                                       start=k == 0, stop=k == KD - 1)
                    mm.then_inc(sig[which + "_mm", l], 1)

            pe.wait_ge(sig["loaded"], 48)
            for l in range(LAYERS):
                norm_sum("n1", l, parts_of(l))
                if l == 0:
                    pe.wait_ge(sig["cond_done"], 1)
                    modulation(range(4))
                else:
                    pe.wait_ge(sig["e_acc", 0], 8 * PAIRS)
                nt = nv = 0
                pc = parts_of(0)[:2 - l]
                now = None
                for step in P_STEPS:
                    what = step[0]
                    if what == "blk":
                        blk = step[1]
                        if now:
                            owed.append(now)
                        w = ready(at["in", l, blk])
                        if blk == 0:
                            pe.wait_ge(sig["n1_root", l], since("n1_root", l) + 1)
                    elif what == "t":
                        kind, _, ct, _ = T_TILES[step[1]]
                        if nt >= 2:
                            pe.wait_ge(sig["t_ev", l], since("t_ev", l) + nt - 1)
                        b = 2 * (nt % 2)
                        halves = [(0, LAT, b)] + ([(LAT, CTX, b + 1)] if t_width(l, kind) > LAT else [])
                        for k in range(KD):
                            for t0, n, bb in halves:
                                mm = pe.matmul(ps[:, bb, 0:n], w[:, k, P * ct:P * ct + P], u[:, k, t0:t0 + n],
                                               start=k == 0, stop=k == KD - 1)
                        mm.then_inc(sig["t_mm", l], 1)
                        nt += 1
                        pay()
                        now = (at["in", l, blk], sig["t_mm", l], since("t_mm", l) + nt)
                    elif what == "v":
                        _, c0, cn, _ = V_COLS[step[1]]
                        t = step[2]
                        if nv == 2 * (TL + TC):
                            pe.wait_ge(sig["hn_root", l], since("hn_root", l) + 2)
                        if nv >= 2:
                            pe.wait_ge(sig["v_ev", l], since("v_ev", l) + nv - 1)
                        for k in range(KD):
                            if nv == 0:
                                pe.wait_ge(sig["n1_u", l], since("n1_u", l) + k + 1)
                            elif nv == TL:
                                pe.wait_ge(sig["n1_u", l], since("n1_u", l) + KD + k + 1)
                            mm = pe.matmul(ps[:, 4 + nv % 2, 0:cn], u[:, k, P * t:P * t + P],
                                           w[:, k, c0:c0 + cn], start=k == 0, stop=k == KD - 1)
                        mm.then_inc(sig["v_mm", l], 1)
                        nv += 1
                        pay()
                        now = (at["in", l, blk], sig["v_mm", l], since("v_mm", l) + nv)
                    elif what == "mod" and l == 0:
                        mod_products(step[1], 6 + step[1] % 2)
                    elif what == "pick" and l == 0:
                        mod_pick(step[1], 6 + step[1] % 2, MOD_TOK["in"][step[1] % 2])
                    elif what == "c_mean":
                        pe.wait_ge(sig["tap", l], 2 * TAPS)
                        for j in range(2):
                            for t0, n, c in pc:
                                s0 = t0 + (2 * HALO if c else 0)
                                mm = pe.matmul(ps[:, 6 + c, 0:n], cst("ones_c"), acc[:, j, s0:s0 + n],
                                               start=j == 0, stop=j == 1)
                        mm.then_inc(sig["c_mean", l], 1)
                    elif what == "c_var":
                        pe.wait_ge(sig["c_sq", l], since("c_sq", l) + 2)
                        for j in range(2):
                            for t0, n, c in pc:
                                mm = pe.matmul(ps[:, 6 + c, 0:n], cst("ones_c"), tmp[j][:, t0:t0 + n],
                                               start=j == 0, stop=j == 1)
                        mm.then_inc(sig["c_var", l], 1)
                    elif what == "c_pw":
                        co = step[1]
                        if co == 0:
                            pe.wait_ge(sig["c_act", l], since("c_act", l) + 1)
                            pe.wait_ge(sig["layer_in", l], since("layer_in", l) + 16)
                        else:
                            pe.wait_ge(sig["c_out", l], since("c_out", l) + 1)
                        for t0, n, c in pc:
                            s0 = t0 + (2 * HALO if c else 0)
                            for ci in range(2):
                                mm = pe.matmul(ps[:, 6 + c, 0:n], pw[:, ci, P * co:P * co + P], acc[:, ci, s0:s0 + n],
                                               start=ci == 0, stop=ci == 1)
                        mm.then_inc(sig["c_pw", l], 1)
                    elif what == "hn":
                        i = step[1]
                        tile, g = HN[i]
                        if i == 0:
                            pe.wait_ge(sig["v_ev", l], since("v_ev", l) + nv)
                        elif i == 1:
                            pe.wait_ge(sig["hn_root", l], since("hn_root", l) + 1)
                        else:
                            pe.wait_ge(sig["c_out", l], since("c_out", l) + 2)
                        pe.wait_ge(sig["hn_sq", l], since("hn_sq", l) + i + 1)
                        wd = t_width(l, g)
                        for t0, n, c in parts_of(0)[:1 if wd == LAT else 2]:
                            mm = pe.matmul(ps[:, HN_BANK[i] + c, 0:n], cst("ones_h"), hn_tmp[i][:, t0:t0 + n],
                                           start=True, stop=True)
                        mm.then_inc(sig["hn_mm", l], 1)
                    elif what == "rope":
                        i = step[1]
                        tile, perm, _ = ROPE[i]
                        if i < 2:
                            pe.wait_ge(sig["t_ev", l], since("t_ev", l) + len(T_TILES))
                        else:
                            pe.wait_ge(sig["rp_done", l], since("rp_done", l) + i - 1)
                        if i >= 4:
                            pe.wait_ge(sig["hn_done", l], since("hn_done", l) + i - 3)
                        pe.matmul(ps[:, 2 * (i % 2), :], cst(perm), qk[:, tile, 0:LAT], start=True,
                                  stop=True).then_inc(sig["rp_mm", l], 1)
                pay()
                release(now)
                pe.wait_ge(sig["hn_root", l], since("hn_root", l) + 3)
                pe.wait_ge(sig["v_ev", l], since("v_ev", l) + nv)
                if l == 0:
                    modulation(range(8, MOD_BLOCKS))
                pe.wait_ge(sig["rp_add", l], since("rp_add", l) + 7)
                if l == 0:
                    pe.wait_ge(sig["mod_ev"], MOD_BLOCKS)
                for kind in kinds(l):
                    s, s0 = at_sem, attn_since(l, kind)
                    lat = kind == "lat"
                    k0, kn, trips = (0, TOK, TL) if lat else (LAT, CTX, TC)
                    ktiles = range(k0 // P, (k0 + kn) // P)
                    cuts = [(0, LAT, 0), (LAT, CTX, 1)] if lat else [(LAT, CTX, 0)]

                    y_banks = (2, 3) if lat else (2, 5)

                    def outputs_transposed(it):
                        pe.wait_ge(s["o_ev"], s0["o_ev"] + it * 12 + 12)
                        for x in range(6):
                            mm = pe.transpose(ps[:, y_banks[x // 4], P * (x % 4):P * (x % 4) + P],
                                              otok[:, P * x:P * x + P], cst("ident"))
                            if x in (3, 5):
                                mm.then_inc(s["y_mm"], 1)

                    def tile(it, first=False, last=False):
                        def scores(j, ahead=0):
                            if j in (0, 1, NA0):
                                pe.wait_ge(s["q_st"], it * 10 + (10 * ahead + s0["q_st"] + STAGED[min(j, 2) + 1]))
                            if j == 4 and not first:
                                pe.wait_ge(s["y_ev"], it * 2 + s0["y_ev"])
                            for t0, n, c in cuts:
                                mm = pe.matmul(ps[:, 2 * (j % AHEAD) + c, 0:n], qst[:, SOFTMAX[j], :],
                                               qk[:, KEYS[SOFTMAX[j]], t0:t0 + n], start=True, stop=True)
                            mm.then_inc(s["s_mm"], 1)

                        if first:
                            for j in EARLY.values():
                                scores(j)
                        else:
                            pe.wait_ge(s["s_exp"], it * 16 + (s0["s_exp"] + nth(1)))
                            outputs_transposed(it - 1)
                        for i in range(12):
                            if i in DIFF:
                                pe.wait_ge(s["p_diff"], it * 4 + (s0["p_diff"] + DIFF.index(i) + 1))
                            else:
                                pe.wait_ge(s["s_exp"], it * 16 + (s0["s_exp"] + upto(last_score[i])))
                            src = ex[:, last_score[i] % AHEAD, :]
                            if i:
                                pe.wait_ge(s["t_dve"], it * 12 + (s0["t_dve"] + i))
                                if lat:
                                    pe.wait_ge(s["t_act"], it * 12 + (s0["t_act"] + i))
                            for x, kt in enumerate(ktiles):
                                if i and x == 4:
                                    pe.wait_ge(s["o_ev"], it * 12 + (s0["o_ev"] + i))
                                mm = pe.transpose(ps[:, 6 + x // 4, P * (x % 4):P * (x % 4) + P],
                                                  src[:, P * x:P * x + P], cst("ident"))
                                if x in (3, len(ktiles) - 1):
                                    mm.then_inc(s["t_mm"], 1)
                            new = new_scores(i)
                            for j in new[:1]:
                                scores(j)
                            if i in EARLY and not last:
                                scores(EARLY[i], 1)
                            pe.wait_ge(s["t_dve"], it * 12 + (s0["t_dve"] + i + 1))
                            if lat:
                                pe.wait_ge(s["t_act"], it * 12 + (s0["t_act"] + i + 1))
                            if i and not lat:
                                pe.wait_ge(s["o_ev"], it * 12 + (s0["o_ev"] + i))
                            hd = HEADS[i]
                            v0 = v_col[hd] - (HD if hd % 2 else 0)
                            for x, kt in enumerate(ktiles):
                                mm = pe.matmul(ps[:, 7, 0:P], pt[:, P * x:P * x + P], val[:, kt, v0:v0 + P],
                                               start=x == 0, stop=x == len(ktiles) - 1)
                            mm.then_inc(s["o_mm"], 1)
                            for j in new[1:]:
                                scores(j)
                            if not lat:
                                q = i // 3
                                m = it * RING + (MOD_C + q)
                                if i % 3 == 0:
                                    mod_products(m, 1 + 2 * (q % 2), MOD_C + q, it)
                                elif i % 3 == 1:
                                    mod_pick(m, 1 + 2 * (q % 2), MOD_TOK["context"][q % 2])
                        pay()

                    tile(0, first=True)
                    if trips > 2:
                        with pe.Fori(1, trips - 1) as it:
                            tile(it)
                    tile(trips - 1, last=True)
                    outputs_transposed(trips - 1)
                    pe.wait_ge(s["y_ev"], s0["y_ev"] + 2 * trips)
                wp = parts_of(0)[:2 - l]
                if l == 0:
                    pe.wait_ge(sig["mod_ev"], MOD_C + RING * TC)
                for i in range(2):
                    pe.wait_ge(sig["dn_sq", l], since("dn_sq", l) + i + 1)
                    for t0, n, c in wp:
                        mm = pe.matmul(ps[:, 2 * i + c, 0:n], cst("ones_h"), ex[:, i, t0:t0 + n], start=True, stop=True)
                    mm.then_inc(sig["dn_mm", l], 1)
                pe.wait_ge(sig["c_y", l], since("c_y", l) + 1)
                for what, i in OUT_STEPS[l]:
                    if what == "mod":
                        mod_products(i, 2 + i % 2)
                        continue
                    if what == "pick":
                        mod_pick(i, 2 + i % 2, MOD_TOK["out"][i % 2])
                        continue
                    blk, ct = i // 4, i % 4
                    if ct == 0:
                        w = ready(at["out", l, blk])
                    if i >= 2:
                        pe.wait_ge(sig["o_ev", l], since("o_ev", l) + i - 1)
                    for k in range(KD):
                        if i == 0 and k == 6:
                            pe.wait_ge(sig["dn_done", l], since("dn_done", l) + 2)
                        for t0, n, c in wp:
                            mm = pe.matmul(ps[:, 4 + 2 * (i % 2) + c, 0:n], w[:, k, P * ct:P * ct + P],
                                           u[:, k, t0:t0 + n], start=k == 0, stop=k == KD - 1)
                    mm.then_inc(sig["o_mm", l], 1)
                    pay()
                    if ct == 3:
                        owed.append((at["out", l, blk], sig["o_mm", l], since("o_mm", l) + i + 1))
                    if i >= 2:
                        norm_sum("n2", l, wp, [i - 2])
                pay()
                norm_sum("n2", l, wp, [KD - 2, KD - 1])
                nt = TL + (TC if l == 0 else 0)
                wr = small[:, l, SMALL["router"][0]:SMALL["b_mod"][1]]
                for gs in ((0, 1), (2,))[:nt // 2 - 1]:
                    for k in range(KD):
                        pe.wait_ge(sig["n2_u", l], since("n2_u", l) + KD * (gs[0] // 2) + k + 1)
                        for g in gs:
                            mm = pe.matmul(ps[32 * g:32 * g + 32, 2, 0:256], wr[:, E * k:E * k + 32],
                                           u[:, k, 256 * g:256 * g + 256], start=k == 0, stop=k == KD - 1,
                                           tile_position=(0, 32 * g))
                mm.then_inc(sig["r_grp", l], 1)
                pe.wait_ge(sig["r_cpy", l], since("r_cpy", l) + 1)
                for x in range(2):
                    mm = pe.transpose(ps[:, 3, P * x:P * x + 16 * nt], rt[0:16 * nt, P * x:P * x + P],
                                      cst("ident", 16 * nt)[:, 0:16 * nt])
                mm.then_inc(sig["r_mm", l], 1)
                pe.wait_ge(sig["o_ev", l], since("o_ev", l) + 8)
                for x in range(2 * nt):
                    if x == UT_FIRST:
                        pe.wait_ge(sig["r_aff", l], since("r_aff", l) + 1)
                        for t in range(nt):
                            mm = pe.transpose(ps[0:E, t // 4, P * (t % 4):P * (t % 4) + P], lg[:, t, :], cst("ident"))
                        mm.then_inc(sig["r_tr", l], 1)
                    if x >= 2:
                        pe.wait_ge(sig["ut_ev", l], since("ut_ev", l) + x - 1)
                    for y in range(4):
                        mm = pe.transpose(ps[:, 4 + x % 2, P * y:P * y + P],
                                          u[:, 4 * (x % 2) + y, P * (x // 2):P * (x // 2) + P], cst("ident"))
                    mm.then_inc(sig["ut_mm", l], 1)
                pe.wait_ge(sig["r_pos", l], since("r_pos", l) + 1)
                for t in range(nt):
                    mm = pe.transpose(ps[:, 3, E * t:E * t + E], pos[:, P * t:P * t + P], cst("ident", E)[:, 0:E])
                mm.then_inc(sig["r_ptr", l], 1)
                both = l == 0
                XW = 192 if both else P
                pe.wait_ge(sig["ut_ev", l], since("ut_ev", l) + 2 * nt)
                pe.wait_ge(sig["mod_ev"], 2 * MOD_BLOCKS)
                xe = [view(XE_AT + i * KD * 192, KD, XW) for i in range(2)]

                def gather(buf, cnt, dts=range(KD)):
                    pe.wait_ge(sig["e_g", l], cnt + 1)
                    for dt in dts:
                        pe.wait_ge(sig["e_xev", l], cnt * 8 + max(dt - 1, 0))
                        b = 6 + dt % 2
                        if both:
                            lo = ps[:, b, 0:XW].rearrange("p (x y) -> p x y", y=64)[:, 0:3:2, :]
                        else:
                            lo = ps[:, b, 0:XW]
                        for t in range(TL):
                            mm = pe.matmul(lo, utok[:, t, P * dt:P * dt + P], gl[:, t, :], start=t == 0, stop=t == TL - 1)
                        if both:
                            for t in range(TC):
                                mm = pe.matmul(ps[:, b, 64:128], utok[:, TL + t, P * dt:P * dt + P], gc[:, t, :],
                                               start=t == 0, stop=t == TC - 1)
                        mm.then_inc(sig["e_xmm", l], 1)

                NI = 3 if both else 2
                DN = 3 * 2 if both else 2 * 2

                def block_products(i, bank, cols, stationary, w):
                    for k in range(KD):
                        for c in range(2):
                            if i < 2:
                                mm = pe.matmul(ps[64 * c:64 * c + 64, bank, cols:cols + 256], stationary(k, i),
                                               w[i][:, k, 256 * c:256 * c + 256], start=k == 0, stop=k == KD - 1)
                                continue
                            for e in range(2):
                                g = 32 * (2 * c + e)
                                mm = pe.matmul(ps[g:g + 32, bank, cols:cols + 256], stationary(k, 2 + e),
                                               w[e][:, k, 256 * c:256 * c + 256], start=k == 0, stop=k == KD - 1,
                                               tile_position=(0, g))
                        if k == 1:
                            while held:
                                release(held.pop(0))
                    return mm

                pe.wait_ge(sig["e_clear", l], 1)
                gather(0, 0)
                with pe.Fori(0, PAIRS // 2) as pp:
                    for half_p in range(2):
                        buf = half_p
                        pe.wait_ge(sig["e_xev", l], pp * 16 + (half_p + 1) * 8)
                        n0 = at["exp", l] + 12 * half_p
                        held = []
                        ht0 = pp * (2 * NI) + (l * 3 * PAIRS + NI * half_p)

                        def tokens(k, i):
                            x0 = (0, 128, 64, 96)[i] if both else 64 * i
                            return xe[buf][:, k, x0:x0 + (64 if i < 2 else 32)]

                        def hidden(k, i):
                            return he[i][:, k, :] if i < 2 else he[2][:, k, 32 * (i - 2):32 * (i - 2) + 32]

                        def transpose_h(i):
                            pe.wait_ge(sig["e_h", l], pp * (2 * NI) + NI * half_p + i + 1)
                            for q in range(4):
                                mm = pe.transpose(ps[:, 2 * i, P * q:P * q + P], h_tok[i][:, P * q:P * q + P], cst("ident"))
                            mm.then_inc(sig["e_ht"], 1)

                        for x in range(4):
                            half, gu = x // 2, x % 2
                            w = []
                            for e in range(2):
                                n = n0 + 2 * x + e
                                w.append(ready(n, pp * 2, 3))
                                mm = block_products(e, 2 * e + gu, 256 * half, tokens, w)
                                mm.then_inc(sig["e_gu", l], 1)
                                if not both:
                                    held = [(n, sig["e_gu", l], pp * 16 + 8 * half_p + 2 * x + e + 1)]
                            if x == 3:
                                transpose_h(0)
                            if both:
                                if x == 0:
                                    pe.wait_ge(sig["e_acc", l], pp * 16 + half_p * 8)
                                mm = block_products(2, 4 + gu, 256 * half, tokens, w)
                                mm.then_inc(sig["e_cgu"], 1)
                                held = [(n0 + 2 * x + e, sig["e_cgu"], pp * 8 + 4 * half_p + x + 1) for e in range(2)]
                        dn = 0
                        for dh in range(2):
                            w = []
                            for i in range(NI):
                                if i < 2:
                                    n = n0 + 8 + 2 * dh + i
                                    w.append(ready(n, pp * 2, 3))
                                pe.wait_ge(sig["e_hev"], ht0 + i + 1)
                                mm = block_products(i, 2 * i + dh, 0, hidden, w)
                                mm.then_inc(sig["e_dn", l], 1)
                                dn += 1
                                count = pp * (2 * DN) + DN * half_p + dn
                                if i == 2:
                                    held = [(n0 + 8 + 2 * dh + e, sig["e_dn", l], count) for e in range(2)]
                                elif not both:
                                    held = [(n, sig["e_dn", l], count)]
                                if dn == 1:
                                    for ii in range(1, NI):
                                        transpose_h(ii)
                                    pe.wait_ge(sig["e_acc", l], (pp * 2 + half_p) * 8)
                                    gather(1 - buf, pp * 2 + half_p + 1, range(4))
                        gather(1 - buf, pp * 2 + half_p + 1, range(4, KD))
                        while held:
                            release(held.pop(0))
                        pe.wait_ge(sig["e_s", l], pp * 2 + half_p + 1)
                        pe.wait_ge(sig["e_y", l], pp * (2 * DN) + DN * half_p + DN)
                        pe.wait_ge(sig["e_xev", l], (pp * 2 + half_p + 2) * 8)
                        for dt in range(KD):
                            pe.wait_ge(sig["e_acc", l], pp * 16 + half_p * 8 + max(dt - 1, 0))
                            if both and half_p:
                                pe.matmul(ps[:, 4 + dt % 2, 0:CTX], yc[:, P * dt:P * dt + P], s_ctx, start=True, stop=True)
                            pe.matmul(ps[:, 6 + dt % 2, :], yl[:, P * dt:P * dt + P], s_lat, start=True,
                                      stop=True).then_inc(sig["e_sc", l], 1)
            for k in range(KD):
                pe.wait_ge(sig["fin_sq"], k + 1)
                pe.matmul(ps[:, 0, :], cst("ones_d"), ex[:, k % 2, 0:LAT], start=k == 0,
                          stop=k == KD - 1).then_inc(sig["fin_mm"], 1)

        @block.scalar
        def _(act):
            act.wait_ge(sig["loaded"], 48)
            act.activation(cond_t[:], cond[:], ACT.Tanh, scale=0.5).then_inc(sig["cond_tanh"], 1)

            def norm(which, l, parts):
                for k in range(KD):
                    if k >= 2:
                        act.wait_ge(sig[which + "_mm", l], since(which + "_mm", l) + k - 1)
                    if which == "n2":
                        act.wait_ge(sig["o_ev", l], since("o_ev", l) + k + 1)
                    elif l:
                        act.wait_ge(sig["e_acc", l - 1], 8 * (PAIRS - 1) + k + 1)
                    t1 = parts[-1][0] + parts[-1][1]
                    act.activation(ex[:, k % 2, 0:t1], h[:, k, 0:t1], ACT.Square).then_inc(sig[which + "_sq", l], 1)
                act.wait_ge(sig[which + "_mm", l], since(which + "_mm", l) + KD)
                act.activation(ex[:, 2, 0:t1], bank2(0, t1), ACT.Sqrt, bias=cst("eps")).then_inc(sig[which + "_root", l], 1)
                sh = 0 if which == "n1" else 24
                for t0, n, c in parts:
                    for k in range(KD):
                        act.wait_ge(sig[which + "_pre", l], since(which + "_pre", l) + KD * c + k + 1)
                        act.activation(u[:, k, t0:t0 + n], u[:, k, t0:t0 + n], ACT.Identity,
                                       bias=mod[:, l, sh + k, c:c + 1]).then_inc(sig[which + "_u", l], 1)

            for l in range(LAYERS):
                if l == 0:
                    act.wait_ge(sig["x_loaded"], 16)
                    act.wait_ge(sig["lam_dot"], 2 * LAYERS)
                    act.activation(lam[:, 0:4], lam[:, 0:4], ACT.Exp).then_inc(sig["lam_exp"], 1)
                norm("n1", l, parts_of(l))
                act.wait_ge(sig["n1_u", l], since("n1_u", l) + 2 * KD)
                nt = nv = 0
                pc = parts_of(0)[:2 - l]
                wc = pc[-1][0] + pc[-1][1]
                for step in P_STEPS:
                    what = step[0]
                    if what == "t":
                        kind, _, _, dst = T_TILES[step[1]]
                        wd = t_width(l, kind)
                        src = bank2(2 * (nt % 2), wd)
                        act.wait_ge(sig["t_mm", l], since("t_mm", l) + nt + 1)
                        if kind == "g":
                            last = act.activation(th[:, dst, 0:wd], src, ACT.Tanh, scale=0.5)
                        elif kind == "a":
                            last = act.activation(a_raw[:, dst, 0:wd], src, ACT.Copy, scale=0.5)
                        else:
                            scale = {"nq": HD ** -0.5, "dq": DQ ** -0.5}.get(kind, 1.0)
                            last = act.activation(qk[:, dst, 0:wd], src, ACT.Copy, scale=scale)
                        last.then_inc(sig["t_ev", l], 1)
                        nt += 1
                    elif what == "v":
                        _, _, cn, v0 = V_COLS[step[1]]
                        act.wait_ge(sig["v_mm", l], since("v_mm", l) + nv + 1)
                        act.activation(val[:, step[2], v0:v0 + cn], ps[:, 4 + nv % 2, 0:cn],
                                       ACT.Copy).then_inc(sig["v_ev", l], 1)
                        nv += 1
                    elif what == "c_sq":
                        act.wait_ge(sig["c_cent", l], since("c_cent", l) + 1)
                        for j in range(2):
                            for t0, n, c in pc:
                                s0 = t0 + (2 * HALO if c else 0)
                                last = act.activation(tmp[j][:, t0:t0 + n], acc[:, j, s0:s0 + n], ACT.Square)
                            last.then_inc(sig["c_sq", l], 1)
                    elif what == "c_var":
                        act.wait_ge(sig["c_var", l], since("c_var", l) + 1)
                        act.activation(tmp[2][:, 0:wc], bank2(6, wc), ACT.Sqrt,
                                       bias=cst("eps")).then_inc(sig["c_root", l], 1)
                    elif what == "c_tanh":
                        for j in range(2):
                            act.wait_ge(sig["c_lin", l], since("c_lin", l) + j + 1)
                            for t0, n, c in pc:
                                s0 = t0 + (2 * HALO if c else 0)
                                last = act.activation(tmp[j][:, t0:t0 + n], acc[:, j, s0:s0 + n], ACT.Tanh, scale=0.5)
                            last.then_inc(sig["c_tanh", l], 1)
                    elif what == "c_pw":
                        co = step[1]
                        act.wait_ge(sig["c_pw", l], since("c_pw", l) + co + 1)
                        act.activation(conv_y[:, co, 0:wc], bank2(6, wc), ACT.Identity, scale=0.5,
                                       bias=sm(l, "pw_b")[:, co:co + 1]).then_inc(sig["c_out", l], 1)
                    elif what == "hn_sq":
                        i = step[1]
                        wd = t_width(l, HN[i][1])
                        act.activation(hn_tmp[i][:, 0:wd], qk[:, HN[i][0], 0:wd], ACT.Square).then_inc(sig["hn_sq", l], 1)
                    elif what == "hn":
                        i = step[1]
                        wd = t_width(l, HN[i][1])
                        act.wait_ge(sig["hn_mm", l], since("hn_mm", l) + i + 1)
                        act.activation(hn_tmp[i][:, 0:wd], bank2(HN_BANK[i], wd), ACT.Sqrt,
                                       bias=cst("eps")).then_inc(sig["hn_root", l], 1)
                act.wait_ge(sig["v_mm", l], since("v_mm", l) + nv)
                act.activation(u[:, 2:4, 0:wc], conv_y[:, :, 0:wc], ACT.Copy).then_inc(sig["c_y", l], 1)
                for kind in kinds(l):
                    s, s0 = at_sem, attn_since(l, kind)
                    lat = kind == "lat"
                    k0, kn, trips = (0, TOK, TL) if lat else (LAT, CTX, TC)

                    def outputs(it):
                        base = it * P + k0
                        act.wait_ge(s["y_mm"], it * 2 + (s0["y_mm"] + 1))
                        act.activation(u[:, 4:8, bass.ds(base, P)], ps[:, 2, :].rearrange("p (a b) -> p a b", b=P),
                                       ACT.Copy).then_inc(s["y_ev"], 1)
                        act.wait_ge(s["y_mm"], it * 2 + (s0["y_mm"] + 2))
                        act.activation(u[:, 0:2, bass.ds(base, P)],
                                       ps[:, 3 if lat else 5, 0:CTX].rearrange("p (a b) -> p a b", b=P),
                                       ACT.Copy).then_inc(s["y_ev"], 1)

                    def tile(it, first=False, last=False):
                        def exp(j, ahead=0):
                            act.wait_ge(s["s_max"], it * 16 + (16 * ahead + s0["s_max"] + nth(j)))
                            src = ex[:, j % AHEAD, 0:kn] if (lat and j >= NA0) else bank2(2 * (j % AHEAD), kn)
                            act.activation(ex[:, j % AHEAD, 0:kn], src, ACT.Exp, bias=negmax[:, j:j + 1],
                                           accum_out=sums[:, j:j + 1]).then_inc(s["s_exp"], 1)

                        if first:
                            for j in EARLY.values():
                                exp(j)
                        else:
                            outputs(it - 1)
                        late = []
                        for i in range(12):
                            if lat:
                                act.wait_ge(s["t_mm"], it * 24 + (s0["t_mm"] + 2 * i + 2))
                                act.activation(pt[:, LAT:TOK], ps[:, 7, 0:CTX], ACT.Copy).then_inc(s["t_act"], 1)
                            for j in late:
                                exp(j)
                            new = new_scores(i)
                            early = 0 if i + 1 in DIFF else 1
                            for j in new[:early]:
                                exp(j)
                            if i in EARLY and not last:
                                exp(EARLY[i], 1)
                            late = new[early:]
                        assert not late

                    tile(0, first=True)
                    if trips > 2:
                        with act.Fori(1, trips - 1) as it:
                            tile(it)
                    tile(trips - 1, last=True)
                    outputs(trips - 1)
                    act.wait_ge(s["y_ev"], s0["y_ev"] + 2 * trips)
                wc = TOK if l == 0 else LAT
                for i in range(2):
                    act.activation(ex[:, i, 0:wc], u[:, 6 + i, 0:wc], ACT.Square).then_inc(sig["dn_sq", l], 1)
                for i in range(2):
                    act.wait_ge(sig["dn_mm", l], since("dn_mm", l) + i + 1)
                    act.activation(ex[:, i, 0:wc], bank2(2 * i, wc), ACT.Sqrt, bias=cst("eps")).then_inc(sig["dn_root", l], 1)
                act.wait_ge(sig["dn_done", l], since("dn_done", l) + 2)
                norm("n2", l, parts_of(l, True))
                nt = TL + (TC if l == 0 else 0)
                act.wait_ge(sig["r_cp", l], since("r_cp", l) + 1)
                act.activation(lg[:, 0:nt, :], lg[:, 0:nt, :], ACT.Exp).then_inc(sig["r_exp", l], 1)
                for x in range(2 * nt):
                    if x == UT_FIRST:
                        act.wait_ge(sig["r_tr", l], since("r_tr", l) + 1)
                        act.activation(afft[:, 0:P * nt], psf[0:E, 0:P * nt], ACT.Copy, scale=0.5).then_inc(sig["r_afft", l], 1)
                    act.wait_ge(sig["ut_mm", l], since("ut_mm", l) + x + 1)
                    act.activation(utok[:, x // 2, 512 * (x % 2):512 * (x % 2) + 512], ps[:, 4 + x % 2, :],
                                   ACT.Copy).then_inc(sig["ut_ev", l], 1)
                both = l == 0
                XW = 192 if both else P
                xe = [view(XE_AT + i * KD * 192, KD, XW) for i in range(2)]

                def take_gather(buf, cnt, dts=range(KD)):
                    for dt in dts:
                        act.wait_ge(sig["e_xmm", l], cnt * 8 + dt + 1)
                        act.activation(xe[buf][:, dt, :], ps[:, 6 + dt % 2, 0:XW], ACT.Copy).then_inc(sig["e_xev", l], 1)

                NI = 3 if both else 2
                DN = 3 * 2 if both else 2 * 2
                act.wait_ge(sig["ut_ev", l], since("ut_ev", l) + 2 * nt)
                take_gather(0, 0)
                with act.Fori(0, PAIRS // 2) as pp:
                    for half_p in range(2):
                        def tanh(i):
                            if i < 2:
                                act.wait_ge(sig["e_gu", l], pp * 16 + 8 * half_p + 5 + i)
                            else:
                                act.wait_ge(sig["e_cgu"], pp * 8 + 4 * half_p + 3)
                            act.activation(h_tok[i], ps[:, 2 * i, :], ACT.Tanh, scale=0.5).then_inc(sig["e_tanh", l], 1)

                        def h_transposed(i):
                            act.wait_ge(sig["e_ht"], pp * (2 * NI) + (l * 3 * PAIRS + NI * half_p + i + 1))
                            for c in range(2):
                                dst = he[i].rearrange("p (b c q) t -> p b c q t", b=2, c=2)[:, :, c, :, :]
                                src = ps[:, 2 * i, :].rearrange("p (b q c t) -> p b q c t", b=2, q=2, c=2)[:, :, :, c, :]
                                last = act.activation(dst, src, ACT.Copy)
                            last.then_inc(sig["e_hev"], 1)

                        def take_y(dh, i):
                            act.wait_ge(sig["e_dn", l], pp * (2 * DN) + DN * half_p + (DN // 2) * dh + i + 1)
                            act.wait_ge(sig["e_sc", l], pp * 16 + 8 * half_p)
                            y, row = (yl, 64 * i) if i < 2 else (yc, 64 * half_p)
                            for c in range(2):
                                c0 = 512 * dh + 256 * c
                                last = act.activation(y[row:row + 64, c0:c0 + 256],
                                                      ps[64 * c:64 * c + 64, 2 * i + dh, 0:256], ACT.Copy)
                            last.then_inc(sig["e_y", l], 1)

                        for i in range(NI):
                            if i == 2:
                                h_transposed(0)
                            tanh(i)
                        if not both:
                            h_transposed(0)
                        take_y(0, 0)
                        for i in range(1, NI):
                            h_transposed(i)
                        take_gather(1 - half_p, pp * 2 + half_p + 1, range(4))
                        for i in range(1, NI):
                            take_y(0, i)
                        for i in range(NI):
                            take_y(1, i)
                        take_gather(1 - half_p, pp * 2 + half_p + 1, range(4, KD))
            for k in range(KD):
                act.wait_ge(sig["e_acc", LAYERS - 1], 8 * (PAIRS - 1) + k + 1)
                if k >= 2:
                    act.wait_ge(sig["fin_mm"], k - 1)
                act.activation(ex[:, k % 2, 0:LAT], h[:, k, 0:LAT], ACT.Square).then_inc(sig["fin_sq"], 1)
            act.wait_ge(sig["fin_mm"], KD)
            act.activation(ex[:, 2, 0:LAT], ps[:, 0, :], ACT.Sqrt, bias=cst("eps")).then_inc(sig["fin_root"], 1)

        @block.vector
        def _(dve):
            selfs = {}

            def link(ins, key):
                selfs[key] = selfs.get(key, 0) + 1
                ins.then_inc(sig[key], 1)
                dve.wait_ge(sig[key], selfs[key])

            dve.wait_ge(sig["loaded"], 48)
            for l in range(LAYERS):
                lv = sm(l, "lam").rearrange("p (a b) -> p a b", b=DQ)
                for i in range(2):
                    dve.tensor_tensor_reduce(ex[:, i, 0:DQ], lv[:, 2 * i, :], lv[:, 2 * i + 1, :], 1.0, 0.0, ALU.mult,
                                             ALU.add, lam[:, 2 * l + i:2 * l + i + 1]).then_inc(sig["lam_dot"], 1)
                    dve.wait_ge(sig["lam_dot"], 2 * l + i + 1)
            dve.wait_ge(sig["cond_tanh"], 1)
            link(dve.scalar_tensor_tensor(cond[:], cond_t[:], 1.0, cond[:], ALU.add, ALU.mult), "self0")
            link(dve.tensor_scalar(cond[:], cond[:], 0.5, None, ALU.mult), "self0")
            dve.tensor_copy(cond_w[:, :, :].rearrange("p k (r c) -> p k r c", c=2),
                            cond[:].unsqueeze(2).to_broadcast([P, KD, 16, 2])).then_inc(sig["cond_done"], 1)
            dve.wait_ge(sig["lam_exp"], 1)
            for l in range(LAYERS):
                link(dve.tensor_tensor(lam[:, 2 * l:2 * l + 1], lam[:, 2 * l + 1:2 * l + 2], lam[:, 2 * l:2 * l + 1],
                                       ALU.subtract), "self0")
                link(dve.tensor_scalar(lam[:, 2 * l:2 * l + 1], lam[:, 2 * l:2 * l + 1], -LAM_INIT[l], None, ALU.add), "self0")

            bm = small[:, :, SMALL["b_mod"][0]:SMALL["b_mod"][1]].rearrange("p l (b c) -> p l b c", c=2)

            def mod_copy(m, bank, tok):
                dve.wait_ge(sig["mod_mm"], m + 1)
                dve.tensor_copy(tok, ps[:, bank, 0:256]).then_inc(sig["mod_cp"], 1)

            def mod_add(m, bank, l, j):
                dve.wait_ge(sig["mod_pk"], m + 1)
                dve.tensor_tensor(mod[:, l, bass.ds(j * 4, 4), :].rearrange("p (c x) d -> p x c d", x=2),
                                  ps[:, bank, 256:264].rearrange("p (x c d) -> p x c d", x=2, c=2),
                                  bm[:, l, bass.ds(j * 4, 4), :].rearrange("p (c x) d -> p x c d", x=2),
                                  ALU.add).then_inc(sig["mod_ev"], 1)

            def modulation(ms):
                for m in ms:
                    mod_copy(m, 6 + m % 2, MOD_TOK["start"][m % 2])
                    mod_add(m, 6 + m % 2, m // MOD_BLOCKS, m % MOD_BLOCKS)

            def make_gain(l, i):
                g = sm(l, ("norm1", "norm2")[i]).rearrange("p (k c) -> p k c", c=2)
                dve.scalar_tensor_tensor(gain[:, i, :, :], mod[:, l, 24 * i + 8:24 * i + 16, :], 1.0, g, ALU.add,
                                         ALU.mult).then_inc(sig["gain_done"], 1)
                dve.wait_ge(sig["gain_done"], 2 * l + i + 1)

            def invert(l, part):
                t0, n, c = part
                link(dve.reciprocal(ex[:, 2, t0:t0 + n], ex[:, 2, t0:t0 + n]), ("self", l))

            def norm(which, l, parts, inverted=False):
                dve.wait_ge(sig[which + "_root", l], since(which + "_root", l) + 1)
                i = 0 if which == "n1" else 1
                for t0, n, c in parts:
                    if not inverted:
                        invert(l, (t0, n, c))
                    for k in range(KD):
                        dve.scalar_tensor_tensor(u[:, k, t0:t0 + n], h[:, k, t0:t0 + n], gain[:, i, k, c:c + 1],
                                                 ex[:, 2, t0:t0 + n], ALU.mult, ALU.mult).then_inc(sig[which + "_pre", l], 1)

            for l in range(LAYERS):
                me = ("self", l)
                if l == 0:
                    dve.wait_ge(sig["n1_root", 0], 1)
                    for part in parts_of(0):
                        invert(0, part)
                    modulation(range(4))
                    dve.wait_ge(sig["mod_ev"], 4)
                make_gain(l, 0)
                if l:
                    make_gain(l, 1)
                norm("n1", l, parts_of(l), inverted=l == 0)
                link(dve.tensor_scalar(qn_s[:, 0:1], sm(l, "qn"), HD ** -0.5, None, ALU.mult), me)
                link(dve.tensor_scalar(qn_s[:, 1:2], sm(l, "dn"), 1.0 - LAM_INIT[l], None, ALU.mult), me)
                if l == 0:
                    steps = [x for x in P_STEPS if x[0] in ("mod", "pick")]
                    for what, m in steps:
                        if what == "mod":
                            mod_copy(m, 6 + m % 2, MOD_TOK["in"][m % 2])
                        else:
                            mod_add(m, 6 + m % 2, 0, m)
                pc = parts_of(0)[:2 - l]
                dve.wait_ge(sig["z_zero", l], since("z_zero", l) + 1)
                for j in range(2):
                    dve.wait_ge(sig["t_ev", l], since("t_ev", l) + place("t", 6 + j) + 1)
                    for t0, n, c in pc:
                        z0 = t0 + HALO + (2 * HALO if c else 0)
                        last = dve.scalar_tensor_tensor(z[:, j, z0:z0 + n], th[:, j, t0:t0 + n], 1.0, a_raw[:, j, t0:t0 + n],
                                                        ALU.add, ALU.mult)
                    last.then_inc(sig["z_done", l], 1)
                n = ACCW if l == 0 else LAT
                taps = sm(l, "taps").rearrange("p (j t) -> p j t", t=TAPS)
                dve.wait_ge(sig["z_done", l], since("z_done", l) + 2)
                for j in range(2):
                    dve.tensor_scalar(acc[:, j, 0:n], z[:, j, 0:n], taps[:, j, 0:1], sm(l, "dw_b")[:, j:j + 1], ALU.mult,
                                      ALU.add).then_inc(sig["tap", l], 1)
                with dve.Fori(1, TAPS) as i:
                    for j in range(2):
                        dve.wait_ge(sig["tap", l], i * 2 + j - 1)
                        dve.scalar_tensor_tensor(acc[:, j, 0:n], z[:, j, bass.ds(i, n)], taps[:, j, bass.ds(i, 1)],
                                                 acc[:, j, 0:n], ALU.mult, ALU.add).then_inc(sig["tap", l], 1)
                dve.wait_ge(sig["c_mean", l], since("c_mean", l) + 1)
                for t0, n, c in pc:
                    s0 = t0 + (2 * HALO if c else 0)
                    last = dve.tensor_tensor(acc[:, :, s0:s0 + n], acc[:, :, s0:s0 + n],
                                             ps[:, 6 + c, 0:n].unsqueeze(1).to_broadcast([P, 2, n]), ALU.subtract)
                last.then_inc(sig["c_cent", l], 1)
                wc = pc[-1][0] + pc[-1][1]
                dve.wait_ge(sig["c_root", l], since("c_root", l) + 1)
                link(dve.reciprocal(tmp[2][:, 0:wc], tmp[2][:, 0:wc]), me)
                for j in range(2):
                    for t0, n, c in pc:
                        s0 = t0 + (2 * HALO if c else 0)
                        link(dve.scalar_tensor_tensor(acc[:, j, s0:s0 + n], acc[:, j, s0:s0 + n], sm(l, "ln_g")[:, j:j + 1],
                                                      tmp[2][:, t0:t0 + n], ALU.mult, ALU.mult), me)
                        last = dve.tensor_scalar(acc[:, j, s0:s0 + n], acc[:, j, s0:s0 + n], sm(l, "ln_b")[:, j:j + 1], None,
                                                 ALU.add)
                    last.then_inc(sig["c_lin", l], 1)
                for j in range(2):
                    dve.wait_ge(sig["c_tanh", l], since("c_tanh", l) + j + 1)
                    for t0, n, c in pc:
                        s0 = t0 + (2 * HALO if c else 0)
                        last = dve.scalar_tensor_tensor(acc[:, j, s0:s0 + n], tmp[j][:, t0:t0 + n], 1.0,
                                                        acc[:, j, s0:s0 + n], ALU.add, ALU.mult)
                last.then_inc(sig["c_act", l], 1)
                def head_norm(i):
                    tile, g = HN[i]
                    wd = t_width(l, g)
                    dve.wait_ge(sig["hn_root", l], since("hn_root", l) + i + 1)
                    link(dve.reciprocal(hn_tmp[i][:, 0:wd], hn_tmp[i][:, 0:wd]), me)
                    gcol = qn_s[:, 0:1] if g == "q" else sm(l, "kn")
                    dve.scalar_tensor_tensor(qk[:, tile, 0:wd], qk[:, tile, 0:wd], gcol, hn_tmp[i][:, 0:wd], ALU.mult,
                                             ALU.mult).then_inc(sig["hn_done", l], 1)

                def rotate(i):
                    tile, _, tb = ROPE[i]
                    dve.wait_ge(sig["rp_mm", l], since("rp_mm", l) + i + 1)
                    t = rope_tmp[i % 2]
                    dve.tensor_tensor(t, ps[:, 2 * (i % 2), :], tab[:, tb + 1, :], ALU.mult).then_inc(sig["rp_done", l], 1)
                    link(dve.tensor_tensor(qk[:, tile, 0:LAT], qk[:, tile, 0:LAT], tab[:, tb, :], ALU.mult), me)
                    dve.wait_ge(sig["rp_done", l], since("rp_done", l) + i + 1)
                    dve.tensor_tensor(qk[:, tile, 0:LAT], qk[:, tile, 0:LAT], t, ALU.add).then_inc(sig["rp_add", l], 1)
                    dve.wait_ge(sig["rp_add", l], since("rp_add", l) + i + 1)

                head_norm(0)
                head_norm(1)
                dve.wait_ge(sig["tables", l], since("tables", l) + 16)
                dve.wait_ge(sig["c_out", l], since("c_out", l) + 2)
                rotate(0)
                head_norm(2)
                dve.wait_ge(sig["hn_done", l], since("hn_done", l) + 3)
                for i in range(1, len(ROPE)):
                    rotate(i)
                if l == 0:
                    modulation(range(8, MOD_BLOCKS))
                    dve.wait_ge(sig["mod_ev"], MOD_BLOCKS)
                    make_gain(0, 1)
                for kind in kinds(l):
                    s, s0 = at_sem, attn_since(l, kind)
                    lat = kind == "lat"
                    k0, kn, trips = (0, TOK, TL) if lat else (LAT, CTX, TC)
                    SELF = (4 if lat else 0) + 12 + 8

                    def tile(it, first=False, last=False):
                        cnt = [0]

                        def chain(ins):
                            cnt[0] += 1
                            ins.then_inc(s["self"], 1)
                            dve.wait_ge(s["self"], it * SELF + (s0["self"] + cnt[0]))

                        def top(j, ahead=0):
                            dve.wait_ge(s["s_mm"], it * 16 + (16 * ahead + s0["s_mm"] + nth(j)))
                            b = 2 * (j % AHEAD)
                            if lat and j == NA0:
                                dve.wait_ge(sig["bias_done", l], since("bias_done", l) + 1)
                            if lat and j >= NA0:
                                off = (6 * GRID_W) - it * (2 * GRID_W)
                                dve.tensor_tensor(ex[:, j % AHEAD, 0:LAT], ps[:, b, :], bt[:, j - NA0, bass.ds(off, LAT)],
                                                  ALU.add)
                                chain(dve.tensor_copy(ex[:, j % AHEAD, LAT:TOK], ps[:, b + 1, 0:CTX]))
                                src = ex[:, j % AHEAD, 0:kn]
                            else:
                                src = bank2(b, kn)
                            dve.tensor_reduce(negmax[:, j:j + 1], src, AX.X, ALU.max, negate=True).then_inc(s["s_max"], 1)

                        def difference(i):
                            j1 = last_score[i]
                            j0 = j1 - 1
                            dve.wait_ge(s["s_exp"], it * 16 + (s0["s_exp"] + upto(j1)))
                            chain(dve.reciprocal(rsum[:, j0:j1 + 1], sums[:, j0:j1 + 1]))
                            chain(dve.scalar_tensor_tensor(rsum[:, j1:j1 + 1], rsum[:, j1:j1 + 1], lam[:, 2 * l:2 * l + 1],
                                                           sums[:, j0:j0 + 1], ALU.mult, ALU.mult))
                            chain(dve.scalar_tensor_tensor(ex[:, j1 % AHEAD, 0:kn], ex[:, j1 % AHEAD, 0:kn],
                                                           rsum[:, j1:j1 + 1], ex[:, j0 % AHEAD, 0:kn], ALU.mult, ALU.add))
                            dve.sem_inc(s["p_diff"], 1)

                        if first:
                            for j in EARLY.values():
                                top(j)
                        for i in range(12):
                            n = LAT if lat else CTX
                            dve.wait_ge(s["t_mm"], it * (24 if lat else 12) + (s0["t_mm"] + (2 if lat else 1) * i + 1))
                            dve.tensor_copy(pt[:, 0:n], ps[:, 6, 0:n]).then_inc(s["t_dve"], 1)
                            new = new_scores(i)
                            if i + 1 in DIFF:
                                difference(i + 1)
                                late = new
                            else:
                                for j in new[:1]:
                                    top(j)
                                late = new[1:]
                            if i in EARLY and not last:
                                top(EARLY[i], 1)
                            j = last_score[i] - (1 if i in DIFF else 0)
                            if i not in DIFF:
                                dve.wait_ge(s["s_exp"], it * 16 + (s0["s_exp"] + upto(j)))
                                chain(dve.reciprocal(rsum[:, j:j + 1], sums[:, j:j + 1]))
                            dve.wait_ge(s["o_mm"], it * 12 + (s0["o_mm"] + i + 1))
                            hd = HEADS[i]
                            o0 = HD * (hd % 2)
                            dve.tensor_scalar(otok[:, HD * hd:HD * hd + HD], ps[:, 7, o0:o0 + HD], rsum[:, j:j + 1], None,
                                              ALU.mult).then_inc(s["o_ev"], 1)
                            for j in late:
                                top(j)
                            if not lat:
                                q = i // 3
                                m = it * RING + (MOD_C + q)
                                if i % 3 == 0:
                                    mod_copy(m, 1 + 2 * (q % 2), MOD_TOK["context"][q % 2])
                                elif i % 3 == 2:
                                    mod_add(m, 1 + 2 * (q % 2), 1, it * RING + q)
                        assert cnt[0] == SELF, cnt

                    tile(0, first=True)
                    if trips > 2:
                        with dve.Fori(1, trips - 1) as it:
                            tile(it)
                    tile(trips - 1, last=True)
                wc = TOK if l == 0 else LAT
                for i in range(2):
                    dve.wait_ge(sig["dn_root", l], since("dn_root", l) + i + 1)
                    link(dve.reciprocal(ex[:, i, 0:wc], ex[:, i, 0:wc]), me)
                    dve.scalar_tensor_tensor(u[:, 6 + i, 0:wc], u[:, 6 + i, 0:wc], qn_s[:, 1:2], ex[:, i, 0:wc], ALU.mult,
                                             ALU.mult).then_inc(sig["dn_done", l], 1)
                for what, i in OUT_STEPS[l]:
                    if what == "mod":
                        mod_copy(i, 2 + i % 2, MOD_TOK["out"][i % 2])
                        continue
                    if what == "pick":
                        mod_add(i, 2 + i % 2, 1, i - MOD_BLOCKS)
                        continue
                    dve.wait_ge(sig["o_mm", l], since("o_mm", l) + i + 1)
                    for t0, n, c in parts_of(0)[:2 - l]:
                        last = dve.scalar_tensor_tensor(h[:, i, t0:t0 + n], ps[:, 4 + 2 * (i % 2) + c, 0:n],
                                                        mod[:, l, 16 + i, c:c + 1], h[:, i, t0:t0 + n], ALU.mult, ALU.add)
                    last.then_inc(sig["o_ev", l], 1)
                dve.wait_ge(sig["o_ev", l], since("o_ev", l) + 8)
                norm("n2", l, parts_of(l, True))
                nt = TL + (TC if l == 0 else 0)
                dve.wait_ge(sig["r_grp", l], since("r_grp", l) + 1)
                dve.tensor_copy(rt[0:16 * nt, :], ps[0:16 * nt, 2, 0:256]).then_inc(sig["r_cpy", l], 1)
                dve.wait_ge(sig["r_mm", l], since("r_mm", l) + 1)
                lgv = lg[:, 0:nt, :]
                for x in range(2):
                    last = dve.tensor_copy(lgv.rearrange("p (g x) e -> p x g e", x=2)[:, x, :, :],
                                           ps[:, 3, P * x:P * x + 16 * nt].rearrange("p (g e) -> p g e", e=32)[:, :, 0:E])
                link(last, me)
                link(dve.tensor_reduce(mx6[:, 0:nt], lgv, AX.X, ALU.max), me)
                dve.tensor_tensor(lgv, lgv, mx6[:, 0:nt].unsqueeze(2).to_broadcast([P, nt, E]),
                                  ALU.subtract).then_inc(sig["r_cp", l], 1)
                dve.wait_ge(sig["r_exp", l], since("r_exp", l) + 1)
                link(dve.tensor_reduce(mx6[:, 0:nt], lgv, AX.X, ALU.add), me)
                link(dve.reciprocal(mx6[:, 0:nt], mx6[:, 0:nt]), me)
                dve.tensor_tensor(lgv, lgv, mx6[:, 0:nt].unsqueeze(2).to_broadcast([P, nt, E]),
                                  ALU.mult).then_inc(sig["r_aff", l], 1)
                dve.wait_ge(sig["r_afft", l], since("r_afft", l) + 1)
                wt = P * nt
                link(dve.tensor_copy(wrk[:, 0:wt], afft[:, 0:wt]), me)
                groups = [(0, LAT, CAP_L)] + ([(LAT, CTX, CAP_C)] if l == 0 else [])
                for t0, n, cap in groups:
                    for r in range(cap // 8):
                        link(dve.max(top8[:], wrk[:, t0:t0 + n]), me)
                        link(dve.match_replace(wrk[:, t0:t0 + n], top8[:], wrk[:, t0:t0 + n], -1.0), me)
                link(dve.tensor_scalar(wrk[:, 0:wt], wrk[:, 0:wt], 0.0, None, ALU.is_lt), me)
                for t0, n, cap in groups:
                    link(dve.tensor_tensor_scan(cum[:, t0:t0 + n], wrk[:, t0:t0 + n], wrk[:, t0:t0 + n], 0.0, ALU.add,
                                                ALU.max), me)
                link(dve.tensor_tensor(pos[:, 0:wt], cum[:, 0:wt], wrk[:, 0:wt], ALU.mult), me)
                dve.tensor_scalar(pos[:, 0:wt], pos[:, 0:wt], -1.0, None, ALU.add).then_inc(sig["r_pos", l], 1)
                if l == 0:
                    dve.wait_ge(sig["mod_ev"], 2 * MOD_BLOCKS)
                both = l == 0
                dve.wait_ge(sig["e_clear", l], 1)
                dve.wait_ge(sig["r_ptr", l], since("r_ptr", l) + 1)
                link(dve.tensor_copy(ptok[:, 0:nt, 0:E], ps[:, 3, 0:E * nt].rearrange("p (t e) -> p t e", e=E)), me)

                def one_hot(cnt, off):
                    dve.wait_ge(sig["e_xmm", l], cnt * 8)
                    last = dve.tensor_tensor(gl[:, :, :].rearrange("p t (e j) -> p t e j", j=64),
                                             cst("iota").unsqueeze(1).unsqueeze(1).to_broadcast([P, TL, 2, 64]),
                                             ptok[:, 0:TL, bass.ds(off, 2)].unsqueeze(3).to_broadcast([P, TL, 2, 64]),
                                             ALU.is_equal)
                    if both:
                        last = dve.tensor_tensor(gc[:, :, :].rearrange("p t (e j) -> p t e j", j=32),
                                                 cst("iota")[:, 0:32].unsqueeze(1).unsqueeze(1).to_broadcast([P, TC, 2, 32]),
                                                 ptok[:, TL:TL + TC, bass.ds(off, 2)].unsqueeze(3).to_broadcast([P, TC, 2, 32]),
                                                 ALU.is_equal)
                    last.then_inc(sig["e_g", l], 1)

                one_hot(0, 0)
                NI = 3 if both else 2
                with dve.Fori(0, PAIRS // 2) as pp:
                    for half_p in range(2):
                        dve.wait_ge(sig["e_bc", l], (pp * 2 + half_p + 1) * 16 * (4 if both else 2))
                        dve.wait_ge(sig["e_sc", l], (pp * 2 + half_p) * 8)
                        last = dve.scalar_tensor_tensor(s_lat, pbl[:, 0, :], cst("j_lat"), pbl[:, 1, :], ALU.is_equal, ALU.mult)
                        if both and half_p:
                            last = dve.scalar_tensor_tensor(s_ctx, pbc[:, 0, :], cst("j_ctx"), pbc[:, 1, :], ALU.is_equal,
                                                            ALU.mult)
                        last.then_inc(sig["e_s", l], 1)
                        one_hot(pp * 2 + half_p + 1, pp * 4 + (2 * half_p + 2))
                        for i in range(NI):
                            dve.wait_ge(sig["e_tanh", l], pp * (2 * NI) + NI * half_p + i + 1)
                            dve.scalar_tensor_tensor(h_tok[i], h_tok[i], 1.0, ps[:, 2 * i, :], ALU.add,
                                                     ALU.mult).then_inc(sig["tap", l], 1)
                            dve.wait_ge(sig["tap", l], pp * (2 * NI) + (2 * TAPS + NI * half_p + i + 1))
                            if i < 2:
                                dve.wait_ge(sig["e_gu", l], pp * 16 + 8 * half_p + 7 + i)
                            else:
                                dve.wait_ge(sig["e_cgu"], pp * 8 + 4 * half_p + 4)
                            dve.tensor_tensor(h_tok[i], h_tok[i], ps[:, 2 * i + 1, :], ALU.mult).then_inc(sig["e_h", l], 1)
                        for dt in range(KD):
                            dve.wait_ge(sig["e_sc", l], pp * 16 + 8 * half_p + dt + 1)
                            last = dve.scalar_tensor_tensor(h[:, dt, 0:LAT], ps[:, 6 + dt % 2, :],
                                                            mod[:, l, 40 + dt, 0:1], h[:, dt, 0:LAT], ALU.mult, ALU.add)
                            if both and half_p:
                                last = dve.scalar_tensor_tensor(h[:, dt, LAT:TOK], ps[:, 4 + dt % 2, 0:CTX],
                                                                mod[:, l, 40 + dt, 1:2], h[:, dt, LAT:TOK], ALU.mult, ALU.add)
                            last.then_inc(sig["e_acc", l], 1)
                dve.wait_ge(sig["e_acc", l], 8 * PAIRS)
            dve.wait_ge(sig["fin_root"], 1)
            dve.reciprocal(ex[:, 2, 0:LAT], ex[:, 2, 0:LAT]).then_inc(sig["fin_rinv"], 1)
            dve.wait_ge(sig["fin_rinv"], 1)
            for k in range(KD):
                dve.scalar_tensor_tensor(u[:, k, 0:LAT], h[:, k, 0:LAT], sm(0, "final")[:, k:k + 1], ex[:, 2, 0:LAT], ALU.mult,
                                         ALU.mult).then_inc(sig["fin_out"], 1)

        @block.gpsimd
        def _(pool):
            for l in range(LAYERS):
                pool.wait_ge(sig["n1_pre", l], since("n1_pre", l) + 2 * KD)
                pool.memset(z[:, :, :], 0.0).then_inc(sig["z_zero", l], 1)
                pool.dma_start(tab[:, :, :], a["tables"]).then_inc(sig["tables", l], 16)
                pool.dma_start(pw[:], a["pw"][l]).then_inc(sig["layer_in", l], 16)
                pool.wait_ge(sig["c_y", l], since("c_y", l) + 1)
                pool.dma_start(bt[:, :, :], a["rpb"][l]).then_inc(sig["bias_ld", l], 16)
                pool.wait_ge(sig["rp_add", l], since("rp_add", l) + 7)
                pool.memset(qst[:, 0:4, :], 0.0).then_inc(sig["q_zero", l], 1)
                pool.wait_ge(sig["q_zero", l], since("q_zero", l) + 1)
                for kind in kinds(l):
                    s, s0 = at_sem, attn_since(l, kind)
                    k0, trips = (0, TL) if kind == "lat" else (LAT, TC)
                    if kind == "ctx":
                        pool.wait_ge(at_sem["s_mm"], 16 * TL)

                    def stage(g, t0, before):
                        for x, (pn, src, dst, tiles, units) in enumerate(STAGE[g]):
                            pool.tensor_copy(qst[dst:dst + pn, units, :],
                                             qk[src:src + pn, tiles, bass.ds(t0, P)]).then_inc(s["q_st"], 1)
                            pool.wait_ge(s["q_st"], before + STAGED[g] + x + 1)

                    stage(0, k0, s0["q_st"])
                    if kind == "lat":
                        pool.memset(qst[:, 4:16, :], 0.0).then_inc(sig["q_zero", l], 1)
                        pool.wait_ge(sig["q_zero", l], since("q_zero", l) + 2)
                    for g in (1, 2):
                        stage(g, k0, s0["q_st"])
                    if kind == "lat":
                        pool.wait_ge(sig["bias_ld", l], since("bias_ld", l) + 16)
                        btv = bt[:, :, :].rearrange("p h (m w) -> p (h m) w", w=GRID_W)
                        pool.tensor_tensor(btv, btv, cst("mask").unsqueeze(1).to_broadcast([P, 4 * BIAS_DR, GRID_W]),
                                           ALU.add).then_inc(sig["bias_done", l], 1)
                    with pool.Fori(1, trips) as it:
                        for g in range(3):
                            pool.wait_ge(s["s_mm"], it * 16 + (s0["s_mm"] - 16 + (NA0 if g < 2 else 16)))
                            stage(g, it * P + k0, it * 10 + s0["q_st"])
                nt = TL + (TC if l == 0 else 0)
                pool.wait_ge(sig["n2_pre", l], since("n2_pre", l) + KD * len(parts_of(l, True)))
                both = l == 0
                pool.memset(ptok[:, :, :], -1.0).then_inc(sig["e_clear", l], 1)
                pool.wait_ge(sig["r_pos", l], since("r_pos", l) + 1)
                pool.dma_start(route[:, 0, 0:P * nt], pos[:, 0:P * nt]).then_inc(sig["r_store", l], 16)
                pool.dma_start(route[:, 1, 0:P * nt], afft[:, 0:P * nt]).then_inc(sig["r_store", l], 16)
                pool.wait_ge(sig["r_store", l], since("r_store", l) + 32)
                pool.wait_ge(sig["e_clear", l], 1)
                with pool.Fori(0, PAIRS // 2) as pp:
                    for half_p in range(2):
                        pool.wait_ge(sig["e_s", l], pp * 2 + half_p)
                        for e in range(2):
                            expert = bass.ds(pp * 4 + (2 * half_p + e), 1)
                            src = route[expert, :, 0:LAT].to_broadcast([64, 2, LAT])
                            pool.dma_start(pbl[64 * e:64 * e + 64, :, :], src).then_inc(sig["e_bc", l], 16)
                            if both:
                                r0 = 64 * half_p + 32 * e
                                src = route[expert, :, LAT:TOK].to_broadcast([32, 2, CTX])
                                pool.dma_start(pbc[r0:r0 + 32, :, :], src).then_inc(sig["e_bc", l], 16)


def constants():
    c = np.zeros((P, CONST_N), np.float32)

    def put(name, v):
        lo, hi = CONST[name]
        c[:, lo:hi] = v

    p = np.arange(P)
    put("ident", np.eye(P))
    put("ones_d", 1.0 / D)
    put("ones_c", 1.0 / 256)
    put("ones_h", (p[:, None] // HD == p[None, :] // HD) / HD)
    put("swap32", p[:, None] == (p[None, :] ^ 32))
    put("swap16", p[:, None] == (p[None, :] ^ 16))
    j = p % GRID_W
    start = np.clip(j - WIN_C // 2, 0, GRID_W - WIN_C)[:, None]
    w = np.arange(GRID_W)[None, :]
    put("mask", np.where((w >= start) & (w < start + WIN_C), 0.0, NEG))
    put("iota", np.arange(64)[None, :])
    put("j_lat", (p % 64)[:, None])
    put("j_ctx", (p % 32)[:, None])
    put("eps", EPS)
    put("pick", (p[:, None] // 64 == np.arange(4)[None, :] // 2) & (p[:, None] % 32 == np.arange(4)[None, :] % 2))
    tables = np.zeros((P, 4, LAT), np.float32)
    t = np.arange(LAT)
    rows, cols = (t // GRID_W).astype(np.float32), (t % GRID_W).astype(np.float32)
    for i, d in enumerate((HD, DQ)):
        half, nf = d // 2, d // 4
        inv = (1.0 / (np.float32(10000.0) ** (np.arange(nf, dtype=np.float32) / np.float32(nf)))).astype(np.float32)
        ang = np.concatenate([rows[:, None] * inv, cols[:, None] * inv], 1).T.astype(np.float32)
        r = p % d
        tables[:, 2 * i] = np.cos(ang)[r % half]
        tables[:, 2 * i + 1] = np.sin(ang)[r % half] * np.where(r < half, -1.0, 1.0)[:, None]
    return c, tables


def kernel(x, c, ctx, c_ctx, norm1_g, w_mod, b_mod, w_in, na_rpb, conv_dw_w, conv_dw_b, conv_ln_g, conv_ln_b,
           conv_pw_w, conv_pw_b, gqa_qn_g, gqa_kn_g, diff_lq1, diff_lk1, diff_lq2, diff_lk2, diff_norm_g, w_out,
           norm2_g, w_router, w_gate, w_up, w_down, final_g):
    import concourse.bacc as bacc
    from concourse.bass_utils import run_bass_kernel_spmd

    L = LAYERS

    def cols(v):
        v = np.asarray(v)
        return np.moveaxis(v.reshape(*v.shape[:-1], -1, P), -1, -2)

    def blocks(w):
        w = np.asarray(w)
        n = w.shape[-1] // BLK
        w = w.reshape(*w.shape[:-2], KD, P, n, BLK)
        return np.ascontiguousarray(np.moveaxis(w, (-2, -3, -4), (-4, -3, -2)))

    stream = np.concatenate([np.asarray(x)[0], np.asarray(ctx)[0]], 0)
    cmat, tables = constants()
    small = np.zeros((P, L, SMALL_N), np.float32)

    def put(name, v):
        lo, hi = SMALL[name]
        small[:, :, lo:hi] = np.moveaxis(np.asarray(v).reshape(L, P, -1), 0, 1)

    def twice(v):
        return np.repeat(cols(v)[..., None], 2, -1)

    put("b_mod", twice(b_mod))
    put("norm1", twice(norm1_g))
    put("norm2", twice(norm2_g))
    put("taps", np.moveaxis(cols(conv_dw_w), 1, 3))
    put("dw_b", cols(conv_dw_b))
    put("ln_g", cols(conv_ln_g))
    put("ln_b", cols(conv_ln_b))
    put("pw_b", cols(conv_pw_b))
    put("qn", np.tile(np.asarray(gqa_qn_g), (1, 2)))
    put("kn", np.tile(np.asarray(gqa_kn_g), (1, 2)))
    put("dn", np.tile(np.asarray(diff_norm_g), (1, 2)))
    lam = np.stack([np.asarray(v) for v in (diff_lq1, diff_lk1, diff_lq2, diff_lk2)], 1)
    put("lam", np.repeat(lam[:, None], P, 1))
    put("router", np.moveaxis(np.asarray(w_router).reshape(L, KD, P, E), 1, 2))
    put("final", np.repeat(cols(final_g)[None], L, 0))
    g, up, dn = blocks(w_gate), blocks(w_up), blocks(w_down)
    gate_up = np.stack([g, up], 3).reshape(L, PAIRS, 2, 2, 2, P, KD, BLK)
    gate_up = np.moveaxis(gate_up, 2, 4).reshape(L, PAIRS, 8, P, KD, BLK)
    dn = np.moveaxis(dn.reshape(L, PAIRS, 2, 2, P, KD, BLK), 2, 3).reshape(L, PAIRS, 4, P, KD, BLK)
    w_exp = np.concatenate([gate_up, dn], 2)
    del g, up, dn, gate_up
    rpb = np.zeros((L, 4, 15, 2 * GRID_W - 1), np.float32)
    rpb[..., GRID_W - WIN_C:GRID_W - WIN_C + 2 * WIN_C - 1] = np.asarray(na_rpb)
    j, w = np.arange(GRID_W)[:, None], np.arange(GRID_W)[None, :]
    rpb = rpb[..., w - j + GRID_W - 1]
    rpb = np.stack([rpb[:, :, 1 - r:1 - r + BIAS_DR] for r in range(2)], 1)
    rpb = np.ascontiguousarray(rpb.transpose(0, 1, 4, 2, 3, 5)).reshape(L, P, 4, BIAS_DR * GRID_W)
    arrays = {
        "x": np.ascontiguousarray(np.moveaxis(stream.T.reshape(KD, P, TOK), 0, 1)),
        "cond": np.ascontiguousarray(np.stack([cols(np.asarray(c)[0]), cols(c_ctx)], -1)),
        "const": cmat, "tables": tables, "small": small, "rpb": rpb,
        "w_mod": blocks(w_mod), "w_in": blocks(w_in), "w_out": blocks(w_out), "w_exp": w_exp,
        "pw": np.ascontiguousarray(np.moveaxis(np.asarray(conv_pw_w).reshape(L, 2, P, 256), 1, 2)),
    }
    nc = bacc.Bacc("TRN2", target_bir_lowering=False, num_devices=1)
    args = {n: nc.dram_tensor("in_" + n, v.shape, F32, kind="ExternalInput").ap() for n, v in arrays.items()}
    out = nc.dram_tensor("out_t", (P, KD, LAT), F32, kind="ExternalOutput").ap()
    program(nc, args, out)
    r = run_bass_kernel_spmd(nc, [{"in_" + n: v for n, v in arrays.items()}], core_ids=[0])
    res = np.asarray(r.results[0]["out_t"])
    return np.ascontiguousarray(np.moveaxis(res, 0, 1).reshape(D, LAT).T)[None]
```
